# Optimizing a Trainium2 kernel written in Bass

```python
import math
import jax, jax.numpy as jnp
from jax import lax
import numpy as np

D_MODEL = 1024
BATCH = 1
SEQ = 1024
DEPTH = 1

N_MIXERS = 4
HEAD_DIM = 64
N_HEADS = D_MODEL // HEAD_DIM
DIFF_HEADS = N_HEADS // 2
MEM_LEN = 256
X_HEADS = 4
X_WIDTH = X_HEADS * HEAD_DIM
MIX_OUT = D_MODEL + X_WIDTH
D_FF = -(-8 * D_MODEL // (3 * 256)) * 256
Q_BLOCK = 128
NUM_BUCKETS = 32
MAX_DISTANCE = 128
EPS = 1e-6
NEG_INF = -1e30
SCALE = HEAD_DIM ** -0.5
NSA_KV_GROUPS = 4
NSA_HPG = N_HEADS // NSA_KV_GROUPS
CMP_BLOCK = 32
CMP_STRIDE = 16
CMP_HIDDEN = 256
SLC_BLOCK = 64
SLC_TOPN = 16
WINDOW = 512
FORCED_SCORE = 1e4
MOBA_BLOCK = 256
MOBA_TOPK = 3
MOBA_QBLOCK = 64
SB_IN = 3 * D_MODEL + X_WIDTH
DIFF_IN = 3 * D_MODEL + X_WIDTH
NSA_IN = D_MODEL + 6 * NSA_KV_GROUPS * HEAD_DIM + 3 * N_HEADS + X_WIDTH
MOBA_IN = 3 * D_MODEL + X_WIDTH

kernel_name = "hybrid_sb_diff_nsa_moba_trunk"

def rms_norm(x, g):
    xf = x.astype(jnp.float32)
    y = xf * lax.rsqrt(jnp.mean(xf * xf, axis=-1, keepdims=True) + EPS)
    return (y * g.astype(jnp.float32)).astype(x.dtype)

def split_cols(t, widths):
    offs = np.cumsum([0] + list(widths))
    return [t[..., int(offs[a]):int(offs[a + 1])] for a in range(len(widths))]

def to_heads(t, n):
    B, S, _ = t.shape
    return t.reshape(B, S, n, -1).transpose(0, 2, 1, 3)

def from_heads(t):
    B, H, S, d = t.shape
    return t.transpose(0, 2, 1, 3).reshape(B, S, H * d)

def masked_softmax(s, mask):
    s = jnp.where(mask, s, NEG_INF)
    m = jnp.max(s, axis=-1, keepdims=True)
    p = jnp.exp(s - m) * mask
    return p / jnp.maximum(jnp.sum(p, axis=-1, keepdims=True), 1e-30)

def t5_bucket(dist):
    max_exact = NUM_BUCKETS // 2
    large = max_exact + (jnp.log(jnp.maximum(dist, 1).astype(jnp.float32) / max_exact)
                         / math.log(MAX_DISTANCE / max_exact) * (NUM_BUCKETS - max_exact)).astype(jnp.int32)
    large = jnp.minimum(large, NUM_BUCKETS - 1)
    return jnp.where(dist < max_exact, dist, large)

def swiglu(h, w_gate, w_up, w_down):
    return (jax.nn.silu(h @ w_gate) * (h @ w_up)) @ w_down

def cross_attention(xq, mem, mem_g, w_mem_kv, q_g, k_g):
    mk, mv = split_cols(rms_norm(mem, mem_g) @ w_mem_kv, [X_WIDTH, X_WIDTH])
    q = rms_norm(to_heads(xq, X_HEADS), q_g)
    k = rms_norm(to_heads(mk, X_HEADS), k_g)
    v = to_heads(mv, X_HEADS)
    s = jnp.einsum('bhsd,bhmd->bhsm', q, k).astype(jnp.float32) * SCALE
    p = jax.nn.softmax(s, axis=-1)
    return from_heads(jnp.einsum('bhsm,bhmd->bhsd', p.astype(v.dtype), v))

def stick_breaking_mixer(h, w_in):
    B, S, _ = h.shape
    q, k, v, xq = split_cols(h @ w_in, [D_MODEL, D_MODEL, D_MODEL, X_WIDTH])
    q, k, v = to_heads(q, N_HEADS), to_heads(k, N_HEADS), to_heads(v, N_HEADS)
    nq = S // Q_BLOCK
    qb = jnp.moveaxis(q.reshape(B, N_HEADS, nq, Q_BLOCK, HEAD_DIM), 2, 0)
    kpos = jnp.arange(S)

    def block(args):
        qi, i = args
        tpos = i * Q_BLOCK + jnp.arange(Q_BLOCK)
        z = jnp.einsum('bhqd,bhkd->bhqk', qi, k).astype(jnp.float32) * SCALE
        past = kpos[None, :] < tpos[:, None]
        log_fail = jnp.where(past, jax.nn.log_sigmoid(-z), 0.0)
        after = lax.cumsum(log_fail, axis=3, reverse=True) - log_fail
        a = jnp.where(past, jnp.exp(jax.nn.log_sigmoid(z) + after), 0.0)
        return jnp.einsum('bhqk,bhkd->bhqd', a.astype(v.dtype), v)

    o = lax.map(block, (qb, jnp.arange(nq)))
    o = o.transpose(1, 2, 0, 3, 4).reshape(B, N_HEADS, S, HEAD_DIM)
    return from_heads(o), xq

def diff_mixer(h, w_in, q_g, k_g, lam_vecs, subln_g, lam_init, rel_bias):
    B, S, _ = h.shape
    q, k, v, xq = split_cols(h @ w_in, [D_MODEL, D_MODEL, D_MODEL, X_WIDTH])
    q = rms_norm(q.reshape(B, S, DIFF_HEADS, 2, HEAD_DIM), q_g).transpose(3, 0, 2, 1, 4)
    k = rms_norm(k.reshape(B, S, DIFF_HEADS, 2, HEAD_DIM), k_g).transpose(3, 0, 2, 1, 4)
    v = to_heads(v, DIFF_HEADS)
    lv = lam_vecs.astype(jnp.float32)
    lam = jnp.exp(jnp.sum(lv[0] * lv[1])) - jnp.exp(jnp.sum(lv[2] * lv[3])) + lam_init
    nq = S // Q_BLOCK
    qb = jnp.moveaxis(q.reshape(2, B, DIFF_HEADS, nq, Q_BLOCK, HEAD_DIM), 3, 0)
    kpos = jnp.arange(S)

    def block(args):
        qi, i = args
        tpos = i * Q_BLOCK + jnp.arange(Q_BLOCK)
        dist = tpos[:, None] - kpos[None, :]
        causal = dist >= 0
        bias = rel_bias[:, jnp.clip(dist, 0, S - 1)].reshape(DIFF_HEADS, 2, Q_BLOCK, S).transpose(1, 0, 2, 3)
        s = jnp.einsum('cbhqd,cbhkd->cbhqk', qi, k).astype(jnp.float32) * SCALE + bias[:, None]
        p = masked_softmax(s, causal)
        a = p[0] - lam * p[1]
        return jnp.einsum('bhqk,bhkd->bhqd', a.astype(v.dtype), v)

    o = lax.map(block, (qb, jnp.arange(nq)))
    o = o.transpose(1, 2, 0, 3, 4).reshape(B, DIFF_HEADS, S, 2 * HEAD_DIM)
    o = rms_norm(o, subln_g) * (1.0 - lam_init)
    return from_heads(o), xq

def nsa_compress(t, pos, w1, b1, w2):
    B, G, S, dh = t.shape
    n_cmp = (S - CMP_BLOCK) // CMP_STRIDE + 1
    idx = np.arange(n_cmp)[:, None] * CMP_STRIDE + np.arange(CMP_BLOCK)[None, :]
    blocks = (t[:, :, idx] + pos).reshape(B, G, n_cmp, CMP_BLOCK * dh)
    return jax.nn.gelu(blocks @ w1 + b1) @ w2

def nsa_mixer(h, w_in, q_g, k_g, cmp_pos, cmp_w1, cmp_b1, cmp_w2, rel_bias):
    B, S, _ = h.shape
    G, R, dh = NSA_KV_GROUPS, NSA_HPG, HEAD_DIM
    kvw = G * dh
    q, kc, vc, ks, vs, kw, vw, gates, xq = split_cols(
        h @ w_in, [D_MODEL, kvw, kvw, kvw, kvw, kvw, kvw, 3 * N_HEADS, X_WIDTH])
    q = rms_norm(to_heads(q, N_HEADS), q_g)
    kc_c = rms_norm(nsa_compress(to_heads(kc, G), cmp_pos[0], cmp_w1[0], cmp_b1[0], cmp_w2[0]), k_g)
    vc_c = nsa_compress(to_heads(vc, G), cmp_pos[1], cmp_w1[1], cmp_b1[1], cmp_w2[1])
    ks = rms_norm(to_heads(ks, G), k_g)
    vs = to_heads(vs, G)
    kw = rms_norm(to_heads(kw, G), k_g)
    vw = to_heads(vw, G)
    n_cmp = kc_c.shape[2]
    n_slc = S // SLC_BLOCK
    n_sel = min(SLC_TOPN, n_slc)
    cmp_end = jnp.arange(n_cmp) * CMP_STRIDE + CMP_BLOCK - 1
    c_start = np.arange(n_cmp) * CMP_STRIDE
    s_start = np.arange(n_slc) * SLC_BLOCK
    slc_map = jnp.asarray(((c_start[:, None] < s_start[None, :] + SLC_BLOCK)
                           & (c_start[:, None] + CMP_BLOCK > s_start[None, :])).astype(np.float32))
    ks_blk = ks.reshape(B, G, n_slc, SLC_BLOCK, dh)
    vs_blk = vs.reshape(B, G, n_slc, SLC_BLOCK, dh)
    kw_pad = jnp.pad(kw, ((0, 0), (0, 0), (WINDOW, 0), (0, 0)))
    vw_pad = jnp.pad(vw, ((0, 0), (0, 0), (WINDOW, 0), (0, 0)))
    bi = jnp.arange(B)[:, None, None, None]
    gi = jnp.arange(G)[None, :, None, None]
    head_idx = (jnp.arange(G)[:, None] * R + jnp.arange(R)[None, :])[None, :, :, None, None, None]
    jb = jnp.arange(n_slc)
    nq = S // Q_BLOCK
    qb = jnp.moveaxis(q.reshape(B, G, R, nq, Q_BLOCK, dh), 3, 0)

    def block(args):
        qi, i = args
        t0 = i * Q_BLOCK
        tpos = t0 + jnp.arange(Q_BLOCK)
        s = jnp.einsum('bgrqd,bgcd->bgrqc', qi, kc_c).astype(jnp.float32) * SCALE
        p_c = masked_softmax(s, cmp_end[None, :] <= tpos[:, None])
        o_c = jnp.einsum('bgrqc,bgcd->bgrqd', p_c.astype(vc_c.dtype), vc_c)
        score = jnp.einsum('bgrqc,cj->bgqj', p_c, slc_map)
        cur = tpos // SLC_BLOCK
        forced = (jb[None, :] == 0) | (jb[None, :] == cur[:, None]) | (jb[None, :] == cur[:, None] - 1)
        valid = jb[None, :] * SLC_BLOCK <= tpos[:, None]
        score = jnp.where(forced, FORCED_SCORE, jnp.where(valid, score, -1.0))
        _, sel = lax.top_k(score, n_sel)
        k_sel = ks_blk[bi, gi, sel]
        v_sel = vs_blk[bi, gi, sel].reshape(B, G, Q_BLOCK, n_sel * SLC_BLOCK, dh)
        pos = sel[..., None] * SLC_BLOCK + jnp.arange(SLC_BLOCK)
        dist = (tpos[:, None, None] - pos)[:, :, None]
        s = (jnp.einsum('bgrqd,bgqnkd->bgrqnk', qi, k_sel).astype(jnp.float32) * SCALE
             + rel_bias[head_idx, jnp.clip(dist, 0, S - 1)])
        p_s = masked_softmax(s.reshape(B, G, R, Q_BLOCK, n_sel * SLC_BLOCK),
                             (dist >= 0).reshape(B, G, 1, Q_BLOCK, n_sel * SLC_BLOCK))
        o_s = jnp.einsum('bgrqm,bgqmd->bgrqd', p_s.astype(v_sel.dtype), v_sel)
        k_win = lax.dynamic_slice_in_dim(kw_pad, t0, WINDOW + Q_BLOCK, axis=2)
        v_win = lax.dynamic_slice_in_dim(vw_pad, t0, WINDOW + Q_BLOCK, axis=2)
        wpos = t0 - WINDOW + jnp.arange(WINDOW + Q_BLOCK)
        wd = tpos[:, None] - wpos[None, :]
        wmask = (wd >= 0) & (wd < WINDOW) & (wpos[None, :] >= 0)
        wbias = rel_bias[:, jnp.clip(wd, 0, S - 1)].reshape(G, R, Q_BLOCK, WINDOW + Q_BLOCK)
        s = jnp.einsum('bgrqd,bgkd->bgrqk', qi, k_win).astype(jnp.float32) * SCALE + wbias
        p_w = masked_softmax(s, wmask)
        o_w = jnp.einsum('bgrqk,bgkd->bgrqd', p_w.astype(v_win.dtype), v_win)
        return jnp.stack([o_c, o_s, o_w])

    o = lax.map(block, (qb, jnp.arange(nq)))
    o = jnp.moveaxis(o, 0, 4).reshape(3, B, N_HEADS, S, dh)
    g = jax.nn.sigmoid(gates.reshape(B, S, N_HEADS, 3).astype(jnp.float32)).transpose(3, 0, 2, 1)[..., None]
    o = jnp.sum(g * o.astype(jnp.float32), axis=0).astype(h.dtype)
    return from_heads(o), xq

def moba_mixer(h, w_in, q_g, k_g, rel_bias):
    B, S, _ = h.shape
    H, dh, MB, QB = N_HEADS, HEAD_DIM, MOBA_BLOCK, MOBA_QBLOCK
    q, k, v, xq = split_cols(h @ w_in, [D_MODEL, D_MODEL, D_MODEL, X_WIDTH])
    q = rms_norm(to_heads(q, H), q_g)
    k = rms_norm(to_heads(k, H), k_g)
    v = to_heads(v, H)
    nb = -(-S // MB)
    pad = nb * MB - S
    kp = jnp.pad(k, ((0, 0), (0, 0), (0, pad), (0, 0)))
    vp = jnp.pad(v, ((0, 0), (0, 0), (0, pad), (0, 0)))
    kb = kp.reshape(B, H, nb, MB, dh)
    vb = vp.reshape(B, H, nb, MB, dh)
    kmean = jnp.mean(kb.astype(jnp.float32), axis=3)
    n_top = min(MOBA_TOPK, nb - 1)
    bi = jnp.arange(B)[:, None, None, None]
    hi = jnp.arange(H)[None, :, None, None]
    hi5 = jnp.arange(H)[None, :, None, None, None]
    nq = S // QB
    qb = jnp.moveaxis(q.reshape(B, H, nq, QB, dh), 2, 0)

    def block(args):
        qi, i = args
        t0 = i * QB
        tpos = t0 + jnp.arange(QB)
        cur = t0 // MB
        own_k = lax.dynamic_slice_in_dim(kp, cur * MB, MB, axis=2)
        own_v = lax.dynamic_slice_in_dim(vp, cur * MB, MB, axis=2)
        own_d = tpos[:, None] - (cur * MB + jnp.arange(MB))[None, :]
        s_own = (jnp.einsum('bhqd,bhkd->bhqk', qi, own_k).astype(jnp.float32) * SCALE
                 + rel_bias[:, jnp.clip(own_d, 0, S - 1)])
        m_own = jnp.broadcast_to(own_d >= 0, (B, H, QB, MB))
        if n_top == 0:
            p_own = masked_softmax(s_own, m_own)
            return jnp.einsum('bhqk,bhkd->bhqd', p_own.astype(v.dtype), own_v)
        gate = jnp.einsum('bhqd,bhjd->bhqj', qi.astype(jnp.float32), kmean)
        gate = jnp.where(jnp.arange(nb) < cur, gate, NEG_INF)
        _, sel = lax.top_k(gate, n_top)
        sel_ok = sel < cur
        k_sel = kb[bi, hi, sel]
        v_sel = vb[bi, hi, sel].reshape(B, H, QB, n_top * MB, dh)
        dist = tpos[:, None, None] - (sel[..., None] * MB + jnp.arange(MB))
        s_sel = (jnp.einsum('bhqd,bhqnkd->bhqnk', qi, k_sel).astype(jnp.float32) * SCALE
                 + rel_bias[hi5, jnp.clip(dist, 0, S - 1)])
        s = jnp.concatenate([s_sel.reshape(B, H, QB, n_top * MB), s_own], axis=-1)
        m_sel = jnp.broadcast_to(sel_ok[..., None], (B, H, QB, n_top, MB)).reshape(B, H, QB, n_top * MB)
        p = masked_softmax(s, jnp.concatenate([m_sel, m_own], axis=-1))
        p_sel, p_own = p[..., :n_top * MB], p[..., n_top * MB:]
        return (jnp.einsum('bhqm,bhqmd->bhqd', p_sel.astype(v.dtype), v_sel)
                + jnp.einsum('bhqk,bhkd->bhqd', p_own.astype(v.dtype), own_v))

    o = lax.map(block, (qb, jnp.arange(nq)))
    o = o.transpose(1, 2, 0, 3, 4).reshape(B, H, S, dh)
    return from_heads(o), xq

def setup_inputs(seed: int = 0) -> dict:
    key = jax.random.key(seed)
    keys = iter(jax.random.split(key, 40))

    def nrm(shape, scale):
        return scale * jax.random.normal(next(keys), shape, jnp.float32)

    def gain(shape):
        return 1.0 + 0.02 * jax.random.normal(next(keys), shape, jnp.float32)

    nA, nB, nC, nD = (len(range(t, DEPTH, N_MIXERS)) for t in range(N_MIXERS))
    D = D_MODEL
    return {
        "x": nrm((BATCH, SEQ, D), 1.0),
        "mem": nrm((BATCH, MEM_LEN, D), 1.0),
        "rel_table": nrm((NUM_BUCKETS, N_HEADS), 0.2),
        "attn_norm": gain((DEPTH, D)),
        "mem_norm": gain((DEPTH, D)),
        "w_mem_kv": nrm((DEPTH, D, 2 * X_WIDTH), D ** -0.5),
        "xq_norm": gain((DEPTH, HEAD_DIM)),
        "xk_norm": gain((DEPTH, HEAD_DIM)),
        "w_out": nrm((DEPTH, MIX_OUT, D), MIX_OUT ** -0.5),
        "ffn_norm": gain((DEPTH, D)),
        "w_gate": nrm((DEPTH, D, D_FF), D ** -0.5),
        "w_up": nrm((DEPTH, D, D_FF), D ** -0.5),
        "w_down": nrm((DEPTH, D_FF, D), D_FF ** -0.5),
        "sb_w_in": nrm((nA, D, SB_IN), D ** -0.5),
        "diff_w_in": nrm((nB, D, DIFF_IN), D ** -0.5),
        "diff_q_norm": gain((nB, HEAD_DIM)),
        "diff_k_norm": gain((nB, HEAD_DIM)),
        "diff_lambda": nrm((nB, 4, HEAD_DIM), 0.1),
        "diff_subln": gain((nB, 2 * HEAD_DIM)),
        "nsa_w_in": nrm((nC, D, NSA_IN), D ** -0.5),
        "nsa_q_norm": gain((nC, HEAD_DIM)),
        "nsa_k_norm": gain((nC, HEAD_DIM)),
        "nsa_cmp_pos": nrm((nC, 2, CMP_BLOCK, HEAD_DIM), 0.1),
        "nsa_cmp_w1": nrm((nC, 2, CMP_BLOCK * HEAD_DIM, CMP_HIDDEN), (CMP_BLOCK * HEAD_DIM) ** -0.5),
        "nsa_cmp_b1": nrm((nC, 2, CMP_HIDDEN), 0.01),
        "nsa_cmp_w2": nrm((nC, 2, CMP_HIDDEN, HEAD_DIM), CMP_HIDDEN ** -0.5),
        "moba_w_in": nrm((nD, D, MOBA_IN), D ** -0.5),
        "moba_q_norm": gain((nD, HEAD_DIM)),
        "moba_k_norm": gain((nD, HEAD_DIM)),
    }

def reference(x, mem, rel_table, attn_norm, mem_norm, w_mem_kv, xq_norm, xk_norm, w_out,
              ffn_norm, w_gate, w_up, w_down, sb_w_in, diff_w_in, diff_q_norm, diff_k_norm,
              diff_lambda, diff_subln, nsa_w_in, nsa_q_norm, nsa_k_norm, nsa_cmp_pos,
              nsa_cmp_w1, nsa_cmp_b1, nsa_cmp_w2, moba_w_in, moba_q_norm, moba_k_norm):
    S = x.shape[1]
    rel_bias = rel_table.astype(jnp.float32)[t5_bucket(jnp.arange(S))].T
    for i in range(DEPTH):
        kind, j = i % N_MIXERS, i // N_MIXERS
        hn = rms_norm(x, attn_norm[i])
        if kind == 0:
            mix, xq = stick_breaking_mixer(hn, sb_w_in[j])
        elif kind == 1:
            lam_init = 0.8 - 0.6 * math.exp(-0.3 * i)
            mix, xq = diff_mixer(hn, diff_w_in[j], diff_q_norm[j], diff_k_norm[j], diff_lambda[j],
                                 diff_subln[j], lam_init, rel_bias)
        elif kind == 2:
            mix, xq = nsa_mixer(hn, nsa_w_in[j], nsa_q_norm[j], nsa_k_norm[j], nsa_cmp_pos[j],
                                nsa_cmp_w1[j], nsa_cmp_b1[j], nsa_cmp_w2[j], rel_bias)
        else:
            mix, xq = moba_mixer(hn, moba_w_in[j], moba_q_norm[j], moba_k_norm[j], rel_bias)
        cross = cross_attention(xq, mem, mem_norm[i], w_mem_kv[i], xq_norm[i], xk_norm[i])
        x = x + jnp.concatenate([mix, cross], axis=-1) @ w_out[i]
        x = x + swiglu(rms_norm(x, ffn_norm[i]), w_gate[i], w_up[i], w_down[i])
    return x


_drawn_inputs = setup_inputs


def setup_inputs(seed=0):
    import zlib

    import numpy as np

    out = dict(_drawn_inputs(seed))
    spreads = {}
    factors = {'attn_norm': 4.549, 'mem_norm': 8.0, 'xq_norm': 8.0, 'xk_norm': 8.0, 'ffn_norm': 4.312}
    for name, (base, spread) in spreads.items():
        noise = np.random.default_rng([zlib.crc32(name.encode()), seed]).standard_normal(out[name].shape)
        drawn = base * np.exp(spread * noise) if base else spread * noise
        out[name] = __import__('jax').numpy.asarray(drawn.astype(out[name].dtype))
    for name, factor in factors.items():
        out[name] = (out[name] * factor).astype(out[name].dtype)
    return out
```

```python
from contextlib import ExitStack

import concourse.bass as bass
from concourse import mybir

ALU = mybir.AluOpType
ACT = mybir.ActivationFunctionType
AX = mybir.AxisListType
F32 = mybir.dt.float32
F32R = mybir.dt.float32r
BF16 = mybir.dt.bfloat16

P = 128
BANK = 512
HD = 64
EPS = 1e-6
FUTURE = -1e30
QSCALE = HD ** -0.5


def trunk(nc, x, mem, attn_norm, mem_norm, w_mem_kv, xq_norm, xk_norm, w_out, ffn_norm, w_gate, w_up, w_down,
          sb_w_in, out):
    _, S, D = x.shape
    NT = S // P
    KC = D // P
    NH = S // BANK
    PAIRS = D // (2 * HD)
    M = mem.shape[1]
    MT = M // P
    XW = w_mem_kv.shape[2] // 2
    XP = XW // (2 * HD)
    OC = PAIRS + XP
    FF = w_gate.shape[2]
    FB = 2
    FC = FF // (FB * P)
    assert (NT, KC, NH, PAIRS, MT, XP) == (8, 8, 2, 8, 2, 2) and FC * FB * P == FF and FC % 2 == 1

    UNITS = []
    for g in range(NT // 2):
        for c in range((2 * g + 1) * P // BANK, -1, -1):
            for i in (2 * g, 2 * g + 1):
                n = (i + 1) * P
                UNITS.append((i, c * BANK, min(n - c * BANK, BANK), n - c * BANK <= BANK))
    NU = len(UNITS)
    USES = 2 * NU
    TUSE = USES + 2
    GROUP_END = [u for u in range(1, NU, 2) if UNITS[u][1] == 0]
    CARRIES = [2 * sum(UNITS[v][1] > 0 for v in range(u)) + h * (UNITS[u][1] > 0) for u in range(NU) for h in range(2)]
    NCARRY = 2 * sum(UNITS[v][1] > 0 for v in range(NU))
    MW = KC
    CONV_AT = (2, 4, 6, 8, 9, 11)
    PIECES = ((0,), (1,), (2,), (3,), (4,), (5,), (6,), (7,), (8, 9), (10,), (11,), ())
    EVAC_AT = {4: 0, 8: 1, 11: 2}
    ZR, FR, GR, AR = 3, 4, 4, 3
    assert USES % ZR == 0 and USES % FR == 0 and USES % GR == 0 and NU % AR == 0 and TUSE % 2 == 0

    with ExitStack() as ctx:
        cursor = [-(-nc.sbuf_base // 32) * 32]
        
        def at(name, shape, dt, off):
            return nc.alloc_sbuf_tensor_at(name, shape, dt, offset=off)

        def size(shape):
            n = 4
            for s in shape[1:]:
                n *= s
            return -(-n // 32) * 32

        def take(name, shape, dt=F32, columns=None):
            t = at(name, [shape[0], columns] if columns else shape, dt, cursor[0])
            cursor[0] += size(shape)
            return t

        def sem(name):
            return ctx.enter_context(nc.semaphore(name))

        ident = take("ident", [P, P])
        ident_b = take("ident_b", [P, P // 2], BF16, P)
        future = take("future", [P, P // 2], BF16, P)
        eps_col = take("eps_col", [P, 1])
        gains = take("gains", [P, 3, KC])
        g_cross = take("g_cross", [P, 2])
        g_qk = take("g_qk", [P, 1])
        half_ones = take("half_ones", [P, 2])
        NS = MT + 2 * NT
        ssq = take("ssq", [P, NS])
        rms = take("rms", [P, NS])
        rstd = take("rstd", [P, NS])
        k_stat = take("k_stat", [P, 3, MT * 2 * XP])
        q_stat = take("q_stat", [P, 4, NT * 2 * XP])
        x_stat = take("x_stat", [P, 4, NT * 2 * XP])
        mk_at = cursor[0]
        mk_h = take("mk_h", [P, XP, M], F32R)
        mk_l = take("mk_l", [P, XP, M], F32R)
        mv = take("mv", [P, MT, XP, 4, HD], F32R)
        h_at = cursor[0]
        hh = take("hh", [P, KC, S], F32R)
        hl = take("hl", [P, KC, S], F32R)
        o_at = cursor[0]
        o_t = take("o_t", [P, PAIRS * S])
        qk_at = cursor[0]
        q_h, q_l, k_h, k_l = [], [], [], []
        for b in range(2):
            for name, to in (("q_h", q_h), ("q_l", q_l), ("k_h", k_h), ("k_l", k_l)):
                to.append(take(f"{name}{b}", [P, S], F32R))
        v_s = [None, None]
        v_s[1] = take("v_s1", [P, NT, 4, HD], F32R)
        v0_at = cursor[0]
        v_s[0] = take("v_s0", [P, NT, 4, HD], F32R)
        raw_at = cursor[0]
        w_raw = take("w_raw", [P, 2, 4, P])
        w_h = take("w_h", [P, 2, 4, P], F32R)
        wl_at = cursor[0]
        w_l = take("w_l", [P, 2, 4, P], F32R)
        fail_at = cursor[0]
        fail = take("fail", [P, FR, BANK + 4])
        x_at = cursor[0]
        succ = take("succ", [P, GR, BANK])
        a_h = take("a_h", [P, AR, 4, 2 * P], F32R)
        a_l = take("a_l", [P, AR, 4, 2 * P], F32R)
        pv_low = take("pv_low", [P, 2 * P])
        assert cursor[0] <= nc.sbuf_usable_end
        KB = 1024
        ROW = 4 * S

        v_t = [at(f"v_t{b}", [P, S], F32, qk_at + (4 * b + 1) * ROW) for b in range(2)]
        x_in = at("x_in", [P, NT, D], F32, x_at)
        m_in = at("m_in", [P, MT, D], F32, qk_at)
        m_hh = at("m_hh", [P, KC, M], F32R, qk_at + 2 * ROW)
        m_hl = at("m_hl", [P, KC, M], F32R, qk_at + 4 * ROW)
        mk_raw = at("mk_raw", [P, MT, XW], F32, qk_at + 6 * ROW)
        mk_sq = at("mk_sq", [P, MT, XW], F32, qk_at + 7 * ROW)
        junk = at("junk", [P, D], F32, v0_at)
        xq_sq = at("xq_sq", [P, XP, S], F32, v0_at)
        ox_t = at("ox_t", [P, XP, S], F32, v0_at)
        wo_h = at("wo_h", [P, OC, BANK], F32R, h_at)
        wo_l = at("wo_l", [P, OC, BANK], F32R, h_at + OC * BANK * 4)
        wo_raw = at("wo_raw", [P, 4, BANK], F32, raw_at)
        rest = h_at + 2 * OC * BANK * 4
        hi_at = [rest + k * ROW for k in range(6)] + [qk_at, qk_at + 2 * ROW, mk_at, x_at + 32 * KB - 2 * ROW]
        lo_at = [qk_at + (4 + k) * ROW for k in range(6)] + [qk_at + ROW, qk_at + 3 * ROW, mk_at + ROW,
                                                             x_at + 32 * KB - ROW]
        o_h = [at(f"o_h{k}", [P, S], F32R, hi_at[k]) for k in range(OC)]
        o_l = [at(f"o_l{k}", [P, S], F32R, lo_at[k]) for k in range(OC)]
        x2 = at("x2", [P, NT, D], F32, fail_at)
        xn = at("xn", [P, 4, D], F32, v0_at)
        f_h = [at("f_h0", [P, KC, BANK], F32R, o_at), at("f_h1", [P, KC, BANK], F32R, h_at)]
        f_l = [at("f_l0", [P, KC, BANK], F32R, o_at + 16 * KB), at("f_l1", [P, KC, BANK], F32R, h_at + 16 * KB)]
        f_raw = at("f_raw", [P, 2, BANK], F32, wl_at)
        gw_h = at("gw_h", [P, FB, 2, KC, P], F32R, h_at + 32 * KB)
        gw_l = at("gw_l", [P, FB, 2, KC, P], F32R, h_at + 48 * KB)
        dw_h = [at("dw_h0", [P, FB, D], F32R, qk_at), at("dw_h1", [P, FB, D], F32R, v0_at)]
        dw_l = [at("dw_l0", [P, FB, D], F32R, qk_at + 2 * ROW), at("dw_l1", [P, FB, D], F32R, v0_at + 2 * ROW)]
        gu_h = [at("gu_h0", [P, FB, S], F32R, qk_at + 4 * ROW), at("gu_h1", [P, FB, S], F32R, qk_at + 8 * ROW)]
        gu_l = [at("gu_l0", [P, FB, S], F32R, qk_at + 6 * ROW), at("gu_l1", [P, FB, S], F32R, mk_at)]
        sig = at("sig", [P, 2, BANK], F32, x_at + 32 * KB - 2 * ROW)
        prod = at("prod", [P, 2, BANK], F32, x_at + 32 * KB - ROW)

        ps = ctx.enter_context(nc.psum_tensor("ps", [P, 8, BANK], F32))
        t_ps, j_ps, z_ps, o_ps = ps[:, 0:2], ps[:, 2:4], ps[:, 4:7], ps[:, 7]

        s_x = [sem(f"x{t}_loaded") for t in range(NT)]
        s_g = sem("gains_loaded")
        s_id = sem("constants_made")
        s_ssq = sem("squares_summed")
        s_rms = sem("root_taken")
        s_rstd = sem("root_inverted")
        s_xn = sem("x_scaled")
        s_xt = sem("x_transposed")
        s_xh = sem("x_high_done")
        s_xl = sem("x_low_done")
        s_w = [sem("w_even_loaded"), sem("w_odd_loaded")]
        s_wh = sem("w_high_done")
        s_wl = sem("w_low_done")
        s_pj = sem("w_used")
        s_eh = sem("qkv_high_done")
        s_el = sem("qk_low_done")
        s_z = sem("scores_ready")
        s_fg = sem("fail_succ_ready")
        s_scan = sem("stick_scanned")
        s_a = sem("weights_ready")
        s_t = sem("weights_transposed")
        s_th = sem("transposed_high_done")
        s_tl = sem("transposed_low_done")
        s_pv = sem("values_summed")
        s_pl = sem("low_part_copied")
        s_o = sem("heads_written")
        s_out = sem("out_stored")

        xd = x.rearrange("b (t p) d -> p (b t) d", p=P)
        wd = sb_w_in.rearrange("l (c p) n -> p (l c) n", p=P)

        def load_w(sp, s, k, whole=True):
            n = MW + 6 * s + k
            sp.wait_ge(s_wl, n - 1)
            column = (k // 2) * D + s * P if whole else 3 * D + (k // 2) * P
            sp.dma_start(w_raw[:, k % 2], wd[:, 4 * (k % 2):4 * (k % 2) + 4, bass.ds(column, P)]
                         ).then_inc(s_w[k % 2], 16)

        def pe_piece(pe, s, k, piece):
            b = piece // 4
            hf, q = (piece % 4) // 2, piece % 2
            n = MW + 6 * s + 2 * b + hf
            if piece % 4 == 0:
                if k:
                    pe.wait_ge(s_eh, 6 * s + 2 * b)
                    if isinstance(s, int) and s == PAIRS and b:
                        pe.wait_ge(s_sq, 2)
                    pe.wait_ge(s_el, 4 * s + (0, 2, 4)[b])
            if q == 0:
                pe.wait_ge(s_wl, n + 1)
            for c in (2 * q, 2 * q + 1):
                kc = 4 * hf + c
                for i, (w, h) in enumerate(((w_h, hh), (w_h, hl), (w_l, hh))):
                    for half in range(2):
                        mm = pe.matmul(j_ps[:, half], w[:, hf, c], h[:, kc, half * BANK:(half + 1) * BANK],
                                       start=(kc == 0 and i == 0), stop=(kc == KC - 1 and i == 2))
            if q == 1:
                mm.then_inc(s_pj, 1)

        def pe_v(pe, s, par, tbase):
            for half in range(2):
                pe.wait_ge(s_eh, 6 * s + 4 + half + 1)
                pe.wait_ge(s_tl, tbase + half - 1)
                for j in range(4):
                    col = (4 * half + j) * P
                    mm = pe.transpose(t_ps[:, half, j * P:(j + 1) * P], v_t[1 - par][:, col:col + P], ident[:, :])
                mm.then_inc(s_t, 1)

        def pe_scores(pe, s, u, par, first=False):
            i, k0, w, diag = UNITS[u]
            if u == 0:
                pe.wait_ge(s_el, 4 * s + 4)
            for h in range(2):
                n = 2 * u + h
                if not (first and n < ZR):
                    pe.wait_ge(s_fg, 2 * (USES * s + n - ZR) + 2)
                if diag:
                    pe.matmul(z_ps[:, n % ZR, w - P:w], ident_b[:, :], future[:, :], start=True, stop=False,
                              skip_group_check=True)
            for t, (qq, kk) in enumerate(((q_h, k_h), (q_h, k_l), (q_l, k_h))):
                for h in range(2):
                    n = 2 * u + h
                    bank = n % ZR
                    r = slice(HD * h, HD * h + HD)
                    mm = pe.matmul(z_ps[:, bank, 0:w], qq[par][r, i * P:(i + 1) * P], kk[par][r, k0:k0 + w],
                                   start=(t == 0 and not diag), stop=(t == 2), skip_group_check=True)
                    if t == 2:
                        mm.then_inc(s_z, 1)

        def pe_transposes(pe, s, u, h):
            n = 2 * u + h
            _, _, w, _ = UNITS[u]
            pe.wait_ge(s_a, USES * s + n + 1)
            pe.wait_ge(s_tl, 2 + TUSE * s + n - 1)
            for j in range(w // P):
                mm = pe.transpose(t_ps[:, n % 2, j * P:(j + 1) * P], succ[:, n % GR, j * P:(j + 1) * P], ident[:, :])
            mm.then_inc(s_t, 1)

        def pe_values(pe, s, u, par):
            i, k0, w, _ = UNITS[u]
            w_first = UNITS[u - 1][2]
            opens = UNITS[u][3]
            up = u // 2
            for h in range(2):
                slot = (2 * up + h) % AR
                pe.wait_ge(s_tl, 2 + TUSE * s + 2 * u + h + 1)
                if opens and h == 0:
                    g = (i - 1) // 2
                    pe.wait_ge(s_o, 8 * s + 2 * g + 1)
                if up == 0 and h == 0:
                    pe.wait_ge(s_tl, 2 + TUSE * s)
                for j in range(w // P):
                    q0 = 0 if j * P < w_first else P
                    for t, a in enumerate((a_h, a_l)):
                        mm = pe.matmul(o_ps[:, h * 2 * P + q0:(h + 1) * 2 * P],
                                       v_s[par][:, k0 // P + j, 2 * h:2 * h + 2, :].rearrange("p a d -> p (a d)"),
                                       a[:, slot, j, q0:2 * P],
                                       start=(opens and h == 0 and j == 0 and t == 0), stop=False,
                                       skip_group_check=True)
                mm.then_inc(s_pv, 1)

        def pe_step(pe, s, par, cross=False):
            for u in range(NU):
                pe_transposes(pe, s, u, 0)
                pe_transposes(pe, s, u, 1)
                if u + 2 < NU:
                    pe_scores(pe, s, u + 2, par)
                elif not cross:
                    pe_scores(pe, s + 1, u + 2 - NU, 1 - par)
                if True:
                    for piece in PIECES[u]:
                        if piece < 8 or not cross:
                            pe_piece(pe, s + 1, 1, piece)
                    if u == NU - 1 and not cross:
                        pe_v(pe, s + 1, 1 - par, 2 + TUSE * s + USES)
                if u % 2:
                    pe_values(pe, s, u, par)

        def act_w(act, s, k):
            n = MW + 6 * s + k
            act.wait_ge(s_w[k % 2], 16 * (MW // 2 + 3 * s + k // 2 + 1))
            act.wait_ge(s_pj, n - 1)
            act.activation(w_h[:, k % 2], w_raw[:, k % 2], ACT.Copy).then_inc(s_wh, 1)

        def act_evac(act, s, b, par):
            act.wait_ge(s_pj, MW + 6 * s + 2 * b + 2)
            dst = (q_h[par], k_h[par], v_t[1 - par])[b]
            for half in range(2):
                c = slice(half * BANK, (half + 1) * BANK)
                act.activation(dst[:, c], j_ps[:, half], ACT.Copy).then_inc(s_eh, 1)

        def act_v(act, par, tcount):
            for half in range(2):
                act.wait_ge(s_t, tcount + half + 1)
                src = t_ps[:, half].rearrange("p (j h d) -> p j h d", j=4, h=2)
                act.activation(v_s[par][:, 4 * half:4 * half + 4, 0:4:3, :], src, ACT.Copy).then_inc(s_th, 1)

        def act_fail_succ(act, s, u, h, first=False):
            n = 2 * u + h
            w = UNITS[u][2]
            act.wait_ge(s_z, USES * s + n + 1)
            if not (first and n < FR):
                act.wait_ge(s_a, USES * s + n - FR + 1)
            act.activation(fail[:, n % FR, 0:w], z_ps[:, n % ZR, 0:w], ACT.Sigmoid, scale=-QSCALE).then_inc(s_fg, 1)
            if not (first and n < GR):
                act.wait_ge(s_t, 2 + TUSE * s + n - GR + 1 - (0 if u >= 2 else 2))
            act.activation(succ[:, n % GR, 0:w], z_ps[:, n % ZR, 0:w], ACT.Sigmoid, scale=QSCALE).then_inc(s_fg, 1)

        def act_high(act, s, u, h):
            n = 2 * u + h
            w = UNITS[u][2]
            up, col = u // 2, u % 2
            act.wait_ge(s_t, 2 + TUSE * s + n + 1)
            if col == 0:
                act.wait_ge(s_pv, NU * s + 2 * up + h + 1)
            act.activation(a_h[:, (2 * up + h) % AR, 0:w // P, col * P:(col + 1) * P],
                           t_ps[:, n % 2, 0:w].rearrange("p (j q) -> p j q", q=P), ACT.Copy).then_inc(s_th, 1)

        def act_low_rows(act, s, u):
            g = UNITS[u][0] // 2
            act.wait_ge(s_pv, AR + NU * s + u + 1)
            act.wait_ge(s_o, 8 * s + 2 * g + 1)
            act.activation(pv_low[0:HD, :], o_ps[HD:P, 0:2 * P], ACT.Copy).then_inc(s_pl, 1)
            act.activation(pv_low[HD:P, :], o_ps[0:HD, 2 * P:4 * P], ACT.Copy).then_inc(s_pl, 1)

        def act_step(act, s, par, cross=False):
            for u in range(NU):
                if u in EVAC_AT and not (cross and EVAC_AT[u] == 2):
                    act_evac(act, s + 1, EVAC_AT[u], 1 - par)
                    if cross:
                        act_squares(act, EVAC_AT[u])
                act_high(act, s, u, 0)
                if u + 2 < NU:
                    act_fail_succ(act, s, u + 2, 0)
                elif not cross:
                    act_fail_succ(act, s + 1, u + 2 - NU, 0)
                act_high(act, s, u, 1)
                if u - 1 in GROUP_END:
                    act_low_rows(act, s, u - 1)
                if u + 2 < NU:
                    act_fail_succ(act, s, u + 2, 1)
                elif not cross:
                    act_fail_succ(act, s + 1, u + 2 - NU, 1)
                if u in CONV_AT:
                    k = CONV_AT.index(u)
                    if k < 2 or not cross:
                        act_w(act, s + 1 + (k + 2) // 6, (k + 2) % 6)
                if u == NU - 1 and not cross:
                    act_v(act, 1 - par, 2 + TUSE * s + USES)
            act_low_rows(act, s, NU - 1)

        def dve_w(dve, s, k):
            dve.wait_ge(s_wh, MW + 6 * s + k + 1)
            dve.tensor_tensor(w_l[:, k % 2], w_raw[:, k % 2], w_h[:, k % 2].bitcast(F32), ALU.subtract).then_inc(s_wl, 1)

        def dve_evac(dve, s, b, par):
            hi, lo = ((q_h, q_l), (k_h, k_l))[b]
            for half in range(2):
                c = slice(half * BANK, (half + 1) * BANK)
                dve.wait_ge(s_eh, 6 * s + 2 * b + half + 1)
                dve.tensor_tensor(lo[par][:, c], j_ps[:, half], hi[par][:, c].bitcast(F32), ALU.subtract).then_inc(s_el, 1)

        def dve_v(dve, par, tcount):
            for half in range(2):
                dve.wait_ge(s_th, tcount + half + 1)
                j = slice(4 * half, 4 * half + 4)
                dve.tensor_tensor(v_s[par][:, j, 1:3, :],
                                  t_ps[:, half].rearrange("p (j h d) -> p j h d", j=4, h=2),
                                  v_s[par][:, j, 0:4:3, :].bitcast(F32), ALU.subtract).then_inc(s_tl, 1)

        def dve_scan(dve, s, u, h):
            n = 2 * u + h
            _, k0, w, diag = UNITS[u]
            f = fail[:, n % FR]
            dve.wait_ge(s_fg, 2 * (USES * s + n) + 2)
            if diag:
                init = 1.0
            else:
                init = f[:, BANK:BANK + 1]
                dve.wait_ge(s_cy, NCARRY * s + CARRIES[n])
            back = f[:, 0:w][:, ::-1]
            dve.tensor_tensor_scan(back, back, back, init, ALU.mult, ALU.bypass).then_inc(s_scan, 1)
            if k0:
                dve.wait_ge(s_scan, USES * s + n + 1)
                dve.tensor_copy(f[:, BANK:BANK + 1], f[:, 0:1]).then_inc(s_cy, 1)

        def dve_weights(dve, s, u, h):
            n = 2 * u + h
            w = UNITS[u][2]
            dve.wait_ge(s_scan, USES * s + n + 1)
            if w == BANK and UNITS[u][0] * P >= BANK:
                dve.wait_ge(s_cy, NCARRY * s + CARRIES[n] + (UNITS[u][1] > 0))
            g = succ[:, n % GR, 0:w]
            dve.tensor_tensor(g, fail[:, n % FR, 1:w + 1], g, ALU.mult).then_inc(s_a, 1)

        def dve_low(dve, s, u, h):
            n = 2 * u + h
            w = UNITS[u][2]
            up, col = u // 2, u % 2
            dve.wait_ge(s_th, 2 + TUSE * s + n + 1)
            slot = (2 * up + h) % AR
            c = slice(col * P, (col + 1) * P)
            dve.tensor_tensor(a_l[:, slot, 0:w // P, c], t_ps[:, n % 2, 0:w].rearrange("p (j q) -> p j q", q=P),
                              a_h[:, slot, 0:w // P, c].bitcast(F32), ALU.subtract).then_inc(s_tl, 1)

        def dve_heads(dve, s, u):
            g = UNITS[u][0] // 2
            dve.wait_ge(s_pl, 8 * s + 2 * g + 2)
            for h in range(2):
                r = slice(HD * h, HD * h + HD)
                dve.tensor_tensor(o_t[r, bass.ds(s * S + g * 2 * P, 2 * P)], o_ps[r, h * 2 * P:(h + 1) * 2 * P],
                                  pv_low[r, :], ALU.add).then_inc(s_o, 1)

        def dve_step(dve, s, par, cross=False):
            for u in range(NU):
                nxt = (s, u + 1) if u + 1 < NU else (s + 1, 0) if not cross else None
                if u in EVAC_AT and EVAC_AT[u] < 2:
                    dve_evac(dve, s + 1, EVAC_AT[u], 1 - par)
                for h in range(2):
                    if nxt:
                        dve_scan(dve, *nxt, h)
                    dve_low(dve, s, u, h)
                    if nxt:
                        dve_weights(dve, *nxt, h)
                if u - 1 in GROUP_END:
                    dve_heads(dve, s, u - 1)
                if u in CONV_AT:
                    k = CONV_AT.index(u)
                    if k < 2 or not cross:
                        dve_w(dve, s + 1 + (k + 2) // 6, (k + 2) % 6)
                if u == NU - 1 and not cross:
                    dve_v(dve, 1 - par, 2 + TUSE * s + USES)
            dve_heads(dve, s, NU - 1)

        s_cy = sem("stick_carried")
        s_m = [sem(f"mem{t}_loaded") for t in range(MT)]
        s_mk = sem("mem_keys_done")
        s_mka = sem("mem_keys_copied")
        s_mv = sem("mem_values_low_done")
        s_gq = sem("cross_gains_multiplied")
        s_sq = sem("cross_q_squared")
        s_qs = sem("cross_q_squares_summed")
        s_qr = sem("cross_q_roots")
        s_qi = sem("cross_q_scales")
        s_cs = sem("cross_scores_ready")
        s_cm = sem("cross_max_taken")
        s_cb = sem("cross_bias_ready")
        s_ce = sem("cross_exp_done")
        s_cr = sem("cross_sum_inverted")
        s_cp = sem("cross_weights_ready")
        s_cv = sem("cross_values_summed")
        s_cl = sem("cross_low_copied")
        s_co = sem("cross_heads_written")
        s_wo = [sem(f"w_out_slot{k}_loaded") for k in range(4)]
        s_woh = sem("w_out_high_done")
        s_wol = [sem("w_out_low_first_half"), sem("w_out_low_second_half")]
        s_wou = sem("w_out_first_half_used")
        s_oh = sem("heads_high_done")
        s_ol = [sem("heads_low_done_by_gpsimd"), sem("heads_low_done_by_vector")]
        s_op = sem("projection_ready")
        s_x2l = [sem(f"residual{t}_loaded") for t in range(NT)]
        s_x2 = sem("residual_added")
        s_fw = [sem("ffn_w_even_loaded"), sem("ffn_w_odd_loaded")]
        s_fh = sem("ffn_w_high_done")
        s_fl = sem("ffn_w_low_done")
        s_gp = sem("gate_up_ready")
        s_sg = sem("sigmoid_done")
        s_t1 = sem("silu_done")
        s_pr = sem("product_done")
        s_gh = sem("product_high_done")
        s_gl = sem("product_low_done")
        s_dn = sem("down_ready")

        memd = mem.rearrange("b (t p) d -> p (b t) d", p=P)
        mwd = w_mem_kv.rearrange("l (c p) n -> p (l c) n", p=P)
        wod = w_out.rearrange("l (c p) n -> p (l c) n", p=P)
        gud = [w.rearrange("l (c p) n -> p (l c) n", p=P) for w in (w_gate, w_up)]
        dnd = w_down.rearrange("l (f p) n -> p (l f) n", p=P)
        outd = out.rearrange("b (t p) d -> p (b t) d", p=P)
        flat = "p c n -> p (c n)"

        XU0 = 4 + 2 * KC + 1
        T1 = 2 + TUSE * PAIRS - 2
        W1 = MW + 6 * PAIRS + 4
        CU = XP * NT
        LAST_ORDER = (6, 7, 8, 9, 2, 3, 0, 1, 4, 5)
        EARLY = 6
        CQ = HD ** -0.5
        pt_h = a_h[:, 0:2].rearrange("p s j q -> p (s j q)").rearrange("p (h m q) -> p h m q", h=2, m=MT)
        pt_l = a_l[:, 0:2].rearrange("p s j q -> p (s j q)").rearrange("p (h m q) -> p h m q", h=2, m=MT)
        pt_hf = pt_h.bitcast(F32)

        def act_root(act, k, src, dst):
            if k:
                act.wait_ge(s_ssq, k)
            act.activation(dst, src, ACT.Square, accum_out=ssq[:, k:k + 1]).then_inc(s_ssq, 1)
            act.wait_ge(s_ssq, k + 1)
            act.activation(rms[:, k:k + 1], ssq[:, k:k + 1], ACT.Sqrt, bias=eps_col[:, :], scale=1.0 / D
                           ).then_inc(s_rms, 1)

        def dve_scale(dve, k, src, dst):
            dve.wait_ge(s_rms, k + 1)
            dve.reciprocal(rstd[:, k:k + 1], rms[:, k:k + 1]).then_inc(s_rstd, 1)
            dve.wait_ge(s_rstd, k + 1)
            dve.tensor_scalar(dst, src, rstd[:, k:k + 1], None, ALU.mult).then_inc(s_xn, 1)

        def pe_turn(pe, g, src, rows, c, scaled):
            if g >= 2:
                pe.wait_ge(s_xl, g - 1)
            pe.wait_ge(s_xn, scaled)
            for t in range(4):
                mm = pe.transpose(t_ps[:, g % 2, t * P:(t + 1) * P], src[:, rows + t, c * P:(c + 1) * P], ident[:, :])
                if g == XU0 and t == 0:
                    mm.then_inc(s_dn, 1)
            mm.then_inc(s_xt, 1)

        def act_turned(act, g, dst, gain):
            act.wait_ge(s_xt, g + 1)
            act.activation(dst, t_ps[:, g % 2], ACT.Copy, scale=gain).then_inc(s_xh, 1)

        def dve_turned(dve, g, dst, high, gain):
            dve.wait_ge(s_xh, g + 1)
            dve.scalar_tensor_tensor(dst, t_ps[:, g % 2], gain, high.bitcast(F32), ALU.mult, ALU.subtract
                                     ).then_inc(s_xl, 1)

        def act_mem_w(act, k):
            act.wait_ge(s_w[k % 2], 16 * (k // 2 + 1))
            if k >= 2:
                act.wait_ge(s_pj, k - 1)
            act.activation(w_h[:, k % 2], w_raw[:, k % 2], ACT.Copy).then_inc(s_wh, 1)

        def dve_mem_w(dve, k):
            dve.wait_ge(s_wh, k + 1)
            dve.tensor_tensor(w_l[:, k % 2], w_raw[:, k % 2], w_h[:, k % 2].bitcast(F32), ALU.subtract
                              ).then_inc(s_wl, 1)

        def act_wo(act, n, k):
            N = OC * n + k
            act.wait_ge(s_wo[N % 4], 16 * (N // 4 + 1))
            if n == 0 and k == 0:
                act.wait_ge(s_pj, W1)
            if n:
                act.wait_ge(s_wou, k + 1)
            act.activation(wo_h[:, k], wo_raw[:, N % 4], ACT.Copy).then_inc(s_woh, 1)

        def sub_wo(eng, n, k):
            eng.wait_ge(s_woh, OC * n + k + 1)
            eng.tensor_tensor(wo_l[:, k], wo_raw[:, (OC * n + k) % 4], wo_h[:, k].bitcast(F32), ALU.subtract
                              ).then_inc(s_wol[n], 1)

        def heads(k, half):
            c = slice(half * BANK, (half + 1) * BANK)
            return o_t[:, k * S + half * BANK:k * S + (half + 1) * BANK] if k < PAIRS else ox_t[:, k - PAIRS, c]

        def act_oh(act, k, half):
            act.activation(o_h[k][:, half * BANK:(half + 1) * BANK], heads(k, half), ACT.Copy).then_inc(s_oh, 1)

        def sub_ol(eng, k, half):
            c = slice(half * BANK, (half + 1) * BANK)
            eng.wait_ge(s_oh, 2 * k + half + 1)
            eng.tensor_tensor(o_l[k][:, c], heads(k, half), o_h[k][:, c].bitcast(F32), ALU.subtract
                              ).then_inc(s_ol[k >= EARLY], 1)

        SIDE = []
        for k in range(OC):
            SIDE.append(("w", k, 0))
            if k < EARLY:
                SIDE += [("o", k, 0), ("o", k, 1)]

        def act_squares(act, b):
            for half in range(2):
                c = slice(half * BANK, (half + 1) * BANK)
                act.wait_ge(s_el, 4 * PAIRS + 2 * b + half + 1)
                act.activation(xq_sq[:, b, c], j_ps[:, half], ACT.Square).then_inc(s_sq, 1)

        def pe_cross_scores(pe, c):
            x_, t = c // NT, c % NT
            qh, ql = (q_h[0], q_l[0]) if x_ == 0 else (k_h[0], k_l[0])
            if c >= 2:
                pe.wait_ge(s_ce, 2 * (c - 2) + 2)
            for i, (q, kk) in enumerate(((qh, mk_h), (qh, mk_l), (ql, mk_h))):
                for h in range(2):
                    r = slice(HD * h, HD * h + HD)
                    mm = pe.matmul(ps[:, 4 + 2 * (c % 2) + h, 0:M], q[r, t * P:(t + 1) * P], kk[r, x_],
                                   start=(i == 0), stop=(i == 2))
            mm.then_inc(s_cs, 1)

        def dve_cross_max(dve, c):
            dve.wait_ge(s_cs, c + 1)
            p = slice(2 * c, 2 * c + 2)
            z = ps[:, 4 + 2 * (c % 2):6 + 2 * (c % 2), 0:M]
            dve.tensor_reduce(x_stat[:, 0, p], z, AX.X, ALU.max).then_inc(s_cm, 1)
            dve.wait_ge(s_cm, c + 1)
            dve.tensor_tensor(x_stat[:, 1, p], x_stat[:, 0, p], q_stat[:, 3, p], ALU.mult).then_inc(s_cb, 1)

        def act_cross_exp(act, c):
            act.wait_ge(s_cb, c + 1)
            if c >= GR:
                act.wait_ge(s_t, T1 + c - GR + 1)
            for h in range(2):
                k = 2 * c + h
                act.activation(succ[:, c % GR, h * M:(h + 1) * M], ps[:, 4 + 2 * (c % 2) + h, 0:M], ACT.Exp,
                               bias=x_stat[:, 1, k:k + 1], scale=q_stat[:, 2, k:k + 1],
                               accum_out=x_stat[:, 2, k:k + 1]).then_inc(s_ce, 1)

        def dve_cross_weights(dve, c):
            p = slice(2 * c, 2 * c + 2)
            dve.wait_ge(s_ce, 2 * c + 2)
            dve.reciprocal(x_stat[:, 3, p], x_stat[:, 2, p]).then_inc(s_cr, 1)
            dve.wait_ge(s_cr, c + 1)
            for h in range(2):
                w = succ[:, c % GR, h * M:(h + 1) * M]
                dve.tensor_scalar(w, w, x_stat[:, 3, 2 * c + h:2 * c + h + 1], None, ALU.mult).then_inc(s_cp, 1)

        def pe_cross_turn(pe, c):
            pe.wait_ge(s_cp, 2 * c + 2)
            pe.wait_ge(s_tl, T1 + c - 1)
            for b in range(4):
                mm = pe.transpose(t_ps[:, c % 2, b * P:(b + 1) * P], succ[:, c % GR, b * P:(b + 1) * P], ident[:, :])
            mm.then_inc(s_t, 1)

        def act_cross_high(act, c):
            act.wait_ge(s_t, T1 + c + 1)
            if c % 4 == 0 and c:
                act.wait_ge(s_cv, c // 4)
            q = slice((c % 4) * P, (c % 4 + 1) * P)
            act.activation(pt_h[:, :, :, q], t_ps[:, c % 2].rearrange("p (h m q) -> p h m q", h=2, m=MT), ACT.Copy
                           ).then_inc(s_th, 1)

        def dve_cross_low(dve, c):
            dve.wait_ge(s_th, T1 + c + 1)
            q = slice((c % 4) * P, (c % 4 + 1) * P)
            dve.tensor_tensor(pt_l[:, :, :, q], t_ps[:, c % 2].rearrange("p (h m q) -> p h m q", h=2, m=MT),
                              pt_hf[:, :, :, q], ALU.subtract).then_inc(s_tl, 1)

        def pe_cross_values(pe, y):
            x_ = y // 2
            pe.wait_ge(s_tl, T1 + 4 * y + 4)
            pe.wait_ge(s_co, 2 * y)
            for h in range(2):
                for m in range(MT):
                    for i, a in enumerate((pt_h, pt_l)):
                        mm = pe.matmul(j_ps[:, h], mv[:, m, x_, 2 * h:2 * h + 2, :].rearrange("p a d -> p (a d)"),
                                       a[:, h, m], start=(m == 0 and i == 0), stop=(m == MT - 1 and i == 1))
            mm.then_inc(s_cv, 1)

        def act_cross_low_rows(act, y):
            act.wait_ge(s_cv, y + 1)
            act.wait_ge(s_co, 2 * y)
            act.activation(fail[0:HD, 0, 0:BANK], j_ps[HD:P, 0], ACT.Copy).then_inc(s_cl, 1)
            act.activation(fail[HD:P, 0, 0:BANK], j_ps[0:HD, 1], ACT.Copy).then_inc(s_cl, 1)

        def dve_cross_heads(dve, y):
            x_, half = y // 2, y % 2
            dve.wait_ge(s_cl, 2 * y + 2)
            for h in range(2):
                r = slice(HD * h, HD * h + HD)
                dve.tensor_tensor(ox_t[r, x_, half * BANK:(half + 1) * BANK], j_ps[r, h], fail[r, 0, 0:BANK], ALU.add
                                  ).then_inc(s_co, 1)

        def pe_project(pe, n, t, turns=()):
            i = NT * n + t
            if i < 2:
                pe.wait_ge(s_co, 2 * 2 * XP)
            else:
                pe.wait_ge(s_x2, i - 1)
            last = n == 1 and t == NT - 1
            order = LAST_ORDER if last else range(OC)
            for at_, k in enumerate(order):
                if t == 0:
                    pe.wait_ge(s_wol[n], k + 1)
                    if n == 0:
                        pe.wait_ge(s_ol[k >= EARLY], 2 * (k - EARLY * (k >= EARLY)) + 2)
                for j, (o, w) in enumerate(((o_h, wo_h), (o_h, wo_l), (o_l, wo_h))):
                    mm = pe.matmul(j_ps[:, i % 2], o[k][:, t * P:(t + 1) * P], w[:, k],
                                   start=(at_ == 0 and j == 0), stop=(at_ == OC - 1 and j == 2))
                if n == 0 and t == NT - 1:
                    mm.then_inc(s_wou, 1)
                if last and at_ == 5:
                    mm.then_inc(s_op, 1)
                if at_ in (2, 5, 8):
                    for c in turns[at_ // 3:at_ // 3 + 1]:
                        if c == 0:
                            pe.wait_ge(s_tl, T1 + CU)
                        pe_turn(pe, XU0 + c, xn, 0, c, MT + NT + 4)
            if n == 0 and t == NT - 1:
                return
            mm.then_inc(s_op, 1)

        def dve_add(dve, n, t):
            i = NT * n + t
            if i == NT - 1:
                dve.wait_ge(s_wou, OC)
            else:
                dve.wait_ge(s_op, i + 1 - (i > NT - 1) + (i == 2 * NT - 1))
            if n == 0:
                dve.wait_ge(s_x2l[t], 16)
            c = x2[:, t, n * BANK:(n + 1) * BANK]
            dve.tensor_tensor(c, j_ps[:, i % 2], c, ALU.add).then_inc(s_x2, 1)

        PROJECTED = 2 * NT

        def sp_ffn(sp, r, kind, c, j):
            if not (isinstance(r, int) and r < 2):
                sp.wait_ge(s_fl, r - 1)
            slot = j % 2
            if kind == "gate":
                fb, mat, kh = j // 4, j // 2 % 2, j % 2
                src = gud[mat][:, 4 * kh:4 * kh + 4, bass.ds((c * FB + fb) * P, P)]
                dst = f_raw[:, slot].rearrange("p (c n) -> p c n", c=4)
            else:
                fb, n = j // 2, j % 2
                src = dnd[:, bass.ds(c * FB + fb, 1), n * BANK:(n + 1) * BANK]
                dst = f_raw[:, slot:slot + 1]
            sp.dma_start(dst, src).then_inc(s_fw[slot], 16)

        def ffn_w(kind, par, j, high):
            if kind == "gate":
                fb, mat, kh = j // 4, j // 2 % 2, j % 2
                return (gw_h if high else gw_l)[:, fb, mat, 4 * kh:4 * kh + 4].rearrange(flat)
            return (dw_h if high else dw_l)[par][:, j // 2, (j % 2) * BANK:(j % 2 + 1) * BANK]

        def row_of(kind, c, j):
            if kind == "gate":
                return j if isinstance(c, int) and c == 0 else 12 * c - 4 + j
            return 16 + 12 * c + j - (8 if isinstance(c, int) and c == FC - 1 else 0)

        def act_ffn_w(act, kind, c, j, par=0):
            r = row_of(kind, c, j)
            rr = r - j % 2
            act.wait_ge(s_fw[j % 2], rr * 8 + 16)
            if kind == "gate":
                if isinstance(c, int) and c == 0:
                    act.wait_ge(s_op, PROJECTED - (j < 4))
                else:
                    act.wait_ge(s_gp, 8 * c - 4 + j // 2 + 1)
            act.activation(ffn_w(kind, par, j, True), f_raw[:, j % 2], ACT.Copy).then_inc(s_fh, 1)

        def dve_ffn_w(dve, kind, c, j, par=0):
            r = row_of(kind, c, j)
            dve.wait_ge(s_fh, r + 1)
            dve.tensor_tensor(ffn_w(kind, par, j, False), f_raw[:, j % 2], ffn_w(kind, par, j, True).bitcast(F32),
                              ALU.subtract).then_inc(s_fl, 1)

        def pe_gate_up(pe, c, half, fb, turns=False):
            first = isinstance(c, int) and c == 0
            q = 4 * c + 2 * half + fb
            if not (first and half == 0):
                pe.wait_ge(s_pr, q - 1)
            if first:
                pe.wait_ge(s_xl, XU0 + KC * (half + 1))
                pe.wait_ge(s_ssq, NS)
            for mat in range(2):
                for kh in range(2):
                    if half == 0:
                        pe.wait_ge(s_fl, row_of("gate", c, 4 * fb + 2 * mat + kh) + 1)
                    for k in range(4 * kh, 4 * kh + 4):
                        for i, (w, f) in enumerate(((gw_h, f_h), (gw_h, f_l), (gw_l, f_h))):
                            mm = pe.matmul(ps[:, 4 + 2 * fb + mat], w[:, fb, mat, k], f[half][:, k],
                                           start=(k == 0 and i == 0), stop=(k == KC - 1 and i == 2))
                        if turns and k % 2 and k < KC - 1:
                            pe_turn(pe, XU0 + KC + 3 * mat + k // 2, xn, 0, 3 * mat + k // 2, NS)
                mm.then_inc(s_gp, 1)
            if turns:
                for c_ in range(6, KC):
                    pe_turn(pe, XU0 + KC + c_, xn, 0, c_, NS)

        def act_sigmoid(act, c, half, fb):
            q = 4 * c + 2 * half + fb
            act.wait_ge(s_gp, 2 * q + 1)
            if not (isinstance(c, int) and c == 0 and half == 0):
                act.wait_ge(s_pr, q - 1)
            act.activation(sig[:, fb], ps[:, 4 + 2 * fb], ACT.Sigmoid).then_inc(s_sg, 1)

        def dve_product(dve, c, half, fb):
            q = 4 * c + 2 * half + fb
            dve.wait_ge(s_sg, q + 1)
            dve.tensor_tensor(sig[:, fb], ps[:, 4 + 2 * fb], sig[:, fb], ALU.mult).then_inc(s_t1, 1)
            dve.wait_ge(s_t1, q + 1)
            dve.wait_ge(s_gp, 2 * q + 2)
            if not (isinstance(c, int) and c == 0 and half == 0):
                dve.wait_ge(s_gl, q - 1)
            dve.tensor_tensor(prod[:, fb], ps[:, 5 + 2 * fb], sig[:, fb], ALU.mult).then_inc(s_pr, 1)

        def act_product_high(act, c, half, fb, par):
            q = 4 * c + 2 * half + fb
            act.wait_ge(s_pr, q + 1)
            if not (isinstance(c, int) and c == 0):
                act.wait_ge(s_dn, 2 * NT * (c - 1) + 1)
            act.activation(gu_h[par][:, fb, half * BANK:(half + 1) * BANK], prod[:, fb], ACT.Copy).then_inc(s_gh, 1)

        def dve_product_low(dve, c, half, fb, par):
            q = 4 * c + 2 * half + fb
            cols = slice(half * BANK, (half + 1) * BANK)
            dve.wait_ge(s_gh, q + 1)
            dve.tensor_tensor(gu_l[par][:, fb, cols], prod[:, fb], gu_h[par][:, fb, cols].bitcast(F32), ALU.subtract
                              ).then_inc(s_gl, 1)

        def pe_down(pe, c, par):
            pe.wait_ge(s_fl, row_of("down", c, 3) + 1)
            for t in range(NT):
                if t % 4 == 0:
                    pe.wait_ge(s_gl, 4 * c + 2 * (t // 4) + 2)
                for n in range(2):
                    d = 2 * t + n
                    pe.wait_ge(s_x2, 2 * NT + 2 * NT * c + d - 3)
                    for fb in range(FB):
                        for i, (g, w) in enumerate(((gu_h, dw_h[par]), (gu_h, dw_l[par]), (gu_l, dw_h[par]))):
                            mm = pe.matmul(ps[:, (2, 3, 0, 1)[d % 4]], g[par][:, fb, t * P:(t + 1) * P],
                                           w[:, fb, n * BANK:(n + 1) * BANK],
                                           start=(fb == 0 and i == 0), stop=(fb == FB - 1 and i == 2))
                    mm.then_inc(s_dn, 1)

        def dve_down(dve, c, ahead, last_w):
            for t in range(NT):
                if ahead and 0 < t < 5:
                    dve_ffn_w(dve, "gate", c + 2, 3 + t)
                if last_w and t % 2 == 0:
                    dve_ffn_w(dve, "down", c + 1, t // 2, 1 - c % 2)
                for n in range(2):
                    d = 2 * t + n
                    dve.wait_ge(s_dn, 2 * NT * c + d + 2)
                    dve.wait_ge(s_x2, 2 * NT * c + d + 1)
                    o = x2[:, t, n * BANK:(n + 1) * BANK]
                    dve.tensor_tensor(o, ps[:, (2, 3, 0, 1)[d % 4]], o, ALU.add).then_inc(s_x2, 1)

        def sp_step(sp, c, ahead=True):
            for j in range(4):
                sp_ffn(sp, row_of("down", c, j), "down", c, j)
            if ahead:
                for j in range(8):
                    sp_ffn(sp, row_of("gate", c + 2, j), "gate", c + 2, j)

        def act_ffn(act, c, par, nxt=True, ahead=True, last_w=False):
            if nxt:
                for j in range(4):
                    act_ffn_w(act, "down", c, j, par)
            if nxt:
                for half in range(2):
                    for fb in range(FB):
                        act_sigmoid(act, c + 1, half, fb)
                        act_product_high(act, c + 1, half, fb, 1 - par)
                        if half == 1 and ahead:
                            for j in range(4 * fb, 4 * fb + 4):
                                act_ffn_w(act, "gate", c + 2, j)
            if last_w:
                for j in range(4):
                    act_ffn_w(act, "down", c + 1, j, 1 - par)

        def dve_ffn(dve, c, par, nxt=True, ahead=True, last_w=False):
            if nxt:
                for j in range(4):
                    dve_ffn_w(dve, "down", c, j, par)
            if nxt:
                for half in range(2):
                    for fb in range(FB):
                        dve_product(dve, c + 1, half, fb)
                        dve_product_low(dve, c + 1, half, fb, 1 - par)
                        if half == 1 and fb == 0 and ahead:
                            for j in range(4):
                                dve_ffn_w(dve, "gate", c + 2, j)
            dve_down(dve, c, ahead, last_w)

        def pe_ffn(pe, c, par, nxt=True):
            if nxt:
                for half in range(2):
                    for fb in range(FB):
                        pe_gate_up(pe, c + 1, half, fb)
            pe_down(pe, c, par)

        TURN_AT = [(), (), (), (), (), (0, 1, 2), (3, 4, 5), (6, 7)]
        FLOOPS = (FC - 3) // 2
        block = ctx.enter_context(nc.Block())
        LOOPS = (PAIRS - 2) // 2

        @block.sync
        def _(sp):
            for t in range(MT):
                sp.dma_start(m_in[:, t], memd[:, t]).then_inc(s_m[t], 16)
            with nc.allow_non_contiguous_dma("gains, one per partition"):
                for i, g in enumerate((attn_norm, mem_norm, ffn_norm)):
                    sp.dma_start(gains[:, i], g.rearrange("l (c p) -> p (l c)", p=P)).then_inc(s_g, 16)
                for i, g in enumerate((xq_norm, xk_norm)):
                    for h in range(2):
                        sp.dma_start(g_cross[HD * h:HD * h + HD, i:i + 1], g.rearrange("l d -> d l")
                                     ).then_inc(s_g, 16)
            for t in range(4):
                sp.dma_start(x_in[:, t], xd[:, t]).then_inc(s_x[t], 16)
            for k in range(MW):
                if k >= 2:
                    sp.wait_ge(s_wl, k - 1)
                sp.dma_start(w_raw[:, k % 2].rearrange(flat), mwd[:, k]).then_inc(s_w[k % 2], 16)
                if k % 2:
                    t = 4 + k // 2
                    sp.dma_start(x_in[:, t], xd[:, t]).then_inc(s_x[t], 16)
            for k in range(6):
                load_w(sp, 0, k)
            with sp.Fori(0, LOOPS) as m:
                for par in range(2):
                    for k in range(6):
                        load_w(sp, 2 * m + par + 1, k)
            for k in range(6):
                load_w(sp, PAIRS - 1, k)
            for k in range(4):
                load_w(sp, PAIRS, k, whole=False)
            for n in range(2):
                for k in range(OC):
                    N = OC * n + k
                    if N == 0:
                        sp.wait_ge(s_wl, W1)
                        sp.wait_ge(s_pj, W1)
                    elif 4 <= N < OC + 4:
                        sp.wait_ge(s_wol[0], N - 3)
                    elif N >= OC + 4:
                        sp.wait_ge(s_wol[1], k - 3)
                    sp.dma_start(wo_raw[:, N % 4], wod[:, k, n * BANK:(n + 1) * BANK]).then_inc(s_wo[N % 4], 16)
                if n == 0:
                    sp.wait_ge(s_co, 2 * 2 * XP)
                    for t in range(NT):
                        sp.dma_start(x2[:, t], xd[:, t]).then_inc(s_x2l[t], 16)
                    for j in range(2):
                        sp_ffn(sp, j, "gate", 0, j)
            for j in range(2, 8):
                sp_ffn(sp, j, "gate", 0, j)
            for j in range(8):
                sp_ffn(sp, 8 + j, "gate", 1, j)
            with sp.Fori(0, FLOOPS) as m:
                for par in range(2):
                    sp_step(sp, 2 * m + par)
            sp_step(sp, FC - 3)
            sp_step(sp, FC - 2, ahead=False)
            sp_step(sp, FC - 1, ahead=False)
            for t in range(NT):
                sp.wait_ge(s_x2, 2 * NT + 2 * NT * (FC - 1) + 2 * t + 2)
                sp.dma_start(outd[:, t], x2[:, t]).then_inc(s_out, 16)
            sp.wait_ge(s_out, 16 * NT)

        @block.gpsimd
        def _(pool):
            pool.memset(ident[:, :], 0.0).then_inc(s_id, 1)
            pool.memset(eps_col[:, :], EPS).then_inc(s_id, 1)
            pool.memset(fail[:, :, :], 1.0).then_inc(s_id, 1)
            pool.memset(ident_b[:, :], 0.0).then_inc(s_id, 1)
            pool.memset(future[:, :], FUTURE).then_inc(s_id, 1)
            pool.memset(half_ones[:, :], 0.0).then_inc(s_id, 1)
            pool.wait_ge(s_id, 6)
            for h in range(2):
                pool.memset(half_ones[HD * h:HD * h + HD, h:h + 1], 1.0).then_inc(s_id, 1)
                pool.wait_ge(s_id, 7 + h)
            for i in (ident, ident_b):
                pool.affine_select(out=i[:, :], in_=i[:, :], compare_op=ALU.not_equal, fill=1.0, base=0,
                                   pattern=[[-1, P]], channel_multiplier=1).then_inc(s_id, 1)
            pool.affine_select(out=future[:, :], in_=future[:, :], compare_op=ALU.is_ge, fill=0.0, base=0,
                               pattern=[[1, P]], channel_multiplier=-1).then_inc(s_id, 1)
            pool.wait_ge(s_o, 8 * PAIRS + 1)
            for what, k, half in SIDE:
                if what == "w":
                    sub_wo(pool, 0, k)
                else:
                    sub_ol(pool, k, half)

        MADE = 11

        @block.scalar
        def _(act):
            act.wait_ge(s_id, MADE)
            for t in range(MT):
                act.wait_ge(s_m[t], 16)
                act_root(act, t, m_in[:, t], junk[:, :])
            for t in range(4):
                act.wait_ge(s_x[t], 16)
                act_root(act, MT + t, x_in[:, t], junk[:, :])
            act.wait_ge(s_g, 16 * 7)
            for g in range(4):
                act.wait_ge(s_xt, g + 1)
                for i in range(2):
                    last = act.activation(m_hh[:, 2 * g + i], t_ps[:, g % 2, i * M:(i + 1) * M], ACT.Copy,
                                          scale=gains[:, 1, 2 * g + i:2 * g + i + 1])
                last.then_inc(s_xh, 1)
            for k in range(2):
                act_mem_w(act, k)
            for c in range(KC):
                act_turned(act, 4 + c, hh[:, c, 0:BANK], gains[:, 0, c:c + 1])
            for k in range(2, MW):
                act_mem_w(act, k)
            for t in range(4, NT):
                act.wait_ge(s_x[t], 16)
                act_root(act, MT + t, x_in[:, t], junk[:, :])
            act.wait_ge(s_pj, MW)
            for m in range(MT):
                act.activation(mk_raw[:, m], j_ps[:, m, 0:XW], ACT.Copy).then_inc(s_mka, 1)
                act.activation(mv[:, m, :, 0:4:3, :], j_ps[:, m, XW:2 * XW].rearrange("p (x h d) -> p x h d", x=XP, h=2),
                               ACT.Copy).then_inc(s_mka, 1)
            act.wait_ge(s_mk, 2)
            act.activation(k_stat[:, 1], k_stat[:, 0], ACT.Sqrt, bias=eps_col[:, :], scale=1.0 / HD).then_inc(s_mka, 1)
            for c in range(KC):
                act_turned(act, 4 + KC + c, hh[:, c, BANK:2 * BANK], gains[:, 0, c:c + 1])
            act.wait_ge(s_gq, 1)
            act_turned(act, XU0 - 1, mk_h[:, :, :].rearrange("p x m -> p (x m)"), g_qk[:, :])
            for k in range(6):
                act_w(act, 0, k)
                if k % 2 and k > 2:
                    act_evac(act, 0, k // 2 - 1, 0)
            for k in range(2):
                act_w(act, 1, k)
            act_evac(act, 0, 2, 0)
            act_fail_succ(act, 0, 0, 0, first=True)
            act_fail_succ(act, 0, 0, 1, first=True)
            act_v(act, 0, 0)
            act_fail_succ(act, 0, 1, 0, first=True)
            act_fail_succ(act, 0, 1, 1, first=True)
            with act.Fori(0, LOOPS) as m:
                for par in range(2):
                    act_step(act, 2 * m + par, par)
            act_step(act, PAIRS - 2, 0)
            act_step(act, PAIRS - 1, 1, cross=True)
            act.wait_ge(s_qs, 1)
            act.activation(q_stat[:, 0], o_ps[:, 0:2 * CU], ACT.Sqrt, bias=eps_col[:, :], scale=1.0 / HD
                           ).then_inc(s_qr, 1)
            side = iter(SIDE)

            def split(count):
                for _ in range(count):
                    what, k, half = next(side, (None, 0, 0))
                    if what == "w":
                        act_wo(act, 0, k)
                    elif what == "o":
                        act_oh(act, k, half)
            split(4)
            act_cross_exp(act, 0)
            act_cross_exp(act, 1)
            for c in range(CU):
                act_cross_high(act, c)
                if c + 2 < CU:
                    act_cross_exp(act, c + 2)
                if c % 4 == 3:
                    act_cross_low_rows(act, c // 4)
                if c < CU - 2:
                    split(2)
            act.wait_ge(s_co, 2 * 2 * XP)
            for k in range(EARLY, OC):
                for half in range(2):
                    act_oh(act, k, half)
            for k in range(OC):
                act_wo(act, 1, k)
            for t in range(NT):
                for c in TURN_AT[t]:
                    if c == 0:
                        act.wait_ge(s_ol[0], 2 * EARLY)
                        act.wait_ge(s_ol[1], 2 * (OC - EARLY))
                    act_turned(act, XU0 + c, f_h[0][:, c], gains[:, 2, c:c + 1])
                if t == NT - 1:
                    for j in range(4):
                        act_ffn_w(act, "gate", 0, j)
                act.wait_ge(s_x2, NT + t + 1)
                act_root(act, MT + NT + t, x2[:, t], ps[:, 4:6].rearrange("p b n -> p (b n)"))
            for j in range(4, 8):
                act_ffn_w(act, "gate", 0, j)
            for half in range(2):
                for fb in range(FB):
                    act_sigmoid(act, 0, half, fb)
                    act_product_high(act, 0, half, fb, 0)
                    if half == 0 and fb == 0:
                        for c in range(KC):
                            act_turned(act, XU0 + KC + c, f_h[1][:, c], gains[:, 2, c:c + 1])
                    if half == 1:
                        for j in range(4 * fb, 4 * fb + 4):
                            act_ffn_w(act, "gate", 1, j)
            with act.Fori(0, FLOOPS) as m:
                for par in range(2):
                    act_ffn(act, 2 * m + par, par)
            act_ffn(act, FC - 3, 0)
            act_ffn(act, FC - 2, 1, ahead=False, last_w=True)

        @block.vector
        def _(dve):
            for t in range(MT):
                dve_scale(dve, t, m_in[:, t], m_in[:, t])
            for t in range(4):
                dve_scale(dve, MT + t, x_in[:, t], x_in[:, t])
            dve.wait_ge(s_g, 16 * 7)
            dve.tensor_tensor(g_qk[:, :], g_cross[:, 0:1], g_cross[:, 1:2], ALU.mult).then_inc(s_gq, 1)
            for g in range(4):
                dve.wait_ge(s_xh, g + 1)
                for i in range(2):
                    c = 2 * g + i
                    last = dve.scalar_tensor_tensor(m_hl[:, c], t_ps[:, g % 2, i * M:(i + 1) * M],
                                                    gains[:, 1, c:c + 1], m_hh[:, c].bitcast(F32),
                                                    ALU.mult, ALU.subtract)
                    if c == 0:
                        last.then_inc(s_o, 1)
                last.then_inc(s_xl, 1)
            for k in range(2):
                dve_mem_w(dve, k)
            for c in range(KC):
                dve_turned(dve, 4 + c, hl[:, c, 0:BANK], hh[:, c, 0:BANK], gains[:, 0, c:c + 1])
            for k in range(2, MW):
                dve_mem_w(dve, k)
            for t in range(4, NT):
                dve_scale(dve, MT + t, x_in[:, t], x_in[:, t])
            dve.wait_ge(s_mka, 2 * MT)
            for m in range(MT):
                dve.tensor_tensor(mv[:, m, :, 1:3, :], j_ps[:, m, XW:2 * XW].rearrange("p (x h d) -> p x h d", x=XP, h=2),
                                  mv[:, m, :, 0:4:3, :].bitcast(F32), ALU.subtract).then_inc(s_mv, 1)
            allk = mk_raw[:, :, :].rearrange("p m n -> p (m n)")
            allsq = mk_sq[:, :, :].rearrange("p m n -> p (m n)")
            dve.tensor_tensor(allsq, allk, allk, ALU.mult).then_inc(s_mk, 1)
            dve.wait_ge(s_mk, 1)
            dve.tensor_reduce(k_stat[:, 0], allsq.rearrange("p (g d) -> p g d", d=HD), AX.X, ALU.add).then_inc(s_mk, 1)
            dve.wait_ge(s_mka, 2 * MT + 1)
            dve.reciprocal(k_stat[:, 2], k_stat[:, 1]).then_inc(s_mk, 1)
            dve.wait_ge(s_mk, 3)
            for g in range(MT * 2 * XP):
                kk = allk[:, g * HD:(g + 1) * HD]
                dve.tensor_scalar(kk, kk, k_stat[:, 2, g:g + 1], None, ALU.mult).then_inc(s_mk, 1)
            for c in range(KC):
                dve_turned(dve, 4 + KC + c, hl[:, c, BANK:2 * BANK], hh[:, c, BANK:2 * BANK], gains[:, 0, c:c + 1])
            dve_turned(dve, XU0 - 1, mk_l[:, :, :].rearrange("p x m -> p (x m)"),
                       mk_h[:, :, :].rearrange("p x m -> p (x m)"), g_qk[:, :])
            for k in range(6):
                dve_w(dve, 0, k)
                if k % 2 and k > 2:
                    dve_evac(dve, 0, k // 2 - 1, 0)
            for k in range(2):
                dve_w(dve, 1, k)
            dve_scan(dve, 0, 0, 0)
            dve_scan(dve, 0, 0, 1)
            dve_weights(dve, 0, 0, 0)
            dve_weights(dve, 0, 0, 1)
            dve_v(dve, 0, 0)
            with dve.Fori(0, LOOPS) as m:
                for par in range(2):
                    dve_step(dve, 2 * m + par, par)
            dve_step(dve, PAIRS - 2, 0)
            dve_step(dve, PAIRS - 1, 1, cross=True)
            dve.wait_ge(s_qr, 1)
            dve.reciprocal(q_stat[:, 1], q_stat[:, 0]).then_inc(s_qi, 1)
            dve.wait_ge(s_qi, 1)
            dve.tensor_scalar(q_stat[:, 2], q_stat[:, 1], CQ, None, ALU.mult).then_inc(s_qi, 1)
            dve.tensor_scalar(q_stat[:, 3], q_stat[:, 1], -CQ, None, ALU.mult).then_inc(s_qi, 1)
            dve.wait_ge(s_qi, 3)
            dve_cross_max(dve, 0)
            dve_cross_max(dve, 1)
            dve_cross_weights(dve, 0)
            for c in range(CU):
                if c + 1 < CU:
                    dve_cross_weights(dve, c + 1)
                dve_cross_low(dve, c)
                if c + 2 < CU:
                    dve_cross_max(dve, c + 2)
                if c % 4 == 3:
                    dve_cross_heads(dve, c // 4)
            for k in range(EARLY, OC):
                for half in range(2):
                    sub_ol(dve, k, half)
            for t in range(NT - 1):
                dve_add(dve, 0, t)
            dve.wait_ge(s_wol[0], OC)
            for k in range(OC):
                sub_wo(dve, 1, k)
            dve_add(dve, 0, NT - 1)
            for t in range(NT):
                for c in TURN_AT[t]:
                    dve_turned(dve, XU0 + c, f_l[0][:, c], f_h[0][:, c], gains[:, 2, c:c + 1])
                if t == NT - 1:
                    for j in range(2):
                        dve_ffn_w(dve, "gate", 0, j)
                dve_add(dve, 1, t)
                if t < 4:
                    dve_scale(dve, MT + NT + t, x2[:, t], xn[:, t])
            for j in range(2, 4):
                dve_ffn_w(dve, "gate", 0, j)
            dve.wait_ge(s_xt, XU0 + KC)
            for t in range(4, NT):
                dve_scale(dve, MT + NT + t, x2[:, t], xn[:, t - 4])
            for j in range(4, 8):
                dve_ffn_w(dve, "gate", 0, j)
            for half in range(2):
                for fb in range(FB):
                    dve_product(dve, 0, half, fb)
                    dve_product_low(dve, 0, half, fb, 0)
                    if half == 0 and fb == 0:
                        for c in range(KC):
                            dve_turned(dve, XU0 + KC + c, f_l[1][:, c], f_h[1][:, c], gains[:, 2, c:c + 1])
                    if half == 1:
                        for j in range(4 * fb, 4 * fb + 4):
                            dve_ffn_w(dve, "gate", 1, j)
            with dve.Fori(0, FLOOPS) as m:
                for par in range(2):
                    dve_ffn(dve, 2 * m + par, par)
            dve_ffn(dve, FC - 3, 0)
            dve_ffn(dve, FC - 2, 1, ahead=False, last_w=True)
            dve_ffn(dve, FC - 1, 0, nxt=False, ahead=False)

        @block.tensor
        def _(pe):
            pe.wait_ge(s_id, MADE)
            for g in range(4):
                if g >= 2:
                    pe.wait_ge(s_xl, g - 1)
                for i in range(2):
                    for t in range(MT):
                        pe.wait_ge(s_xn, t + 1)
                        mm = pe.transpose(t_ps[:, g % 2, (MT * i + t) * P:(MT * i + t + 1) * P],
                                          m_in[:, t, (2 * g + i) * P:(2 * g + i + 1) * P], ident[:, :])
                        if g == 0 and i == 0 and t == 0:
                            mm.then_inc(s_pv, AR)
                mm.then_inc(s_xt, 1)
            for c in range(KC):
                pe_turn(pe, 4 + c, x_in, 0, c, MT + 4)
            pe.wait_ge(s_xl, 4)
            for k in range(MW):
                pe.wait_ge(s_wl, k + 1)
                for i, (a, w) in enumerate(((m_hh, w_h), (m_hh, w_l), (m_hl, w_h))):
                    for m in range(MT):
                        mm = pe.matmul(j_ps[:, m], a[:, k, m * P:(m + 1) * P], w[:, k % 2].rearrange(flat),
                                       start=(k == 0 and i == 0), stop=(k == KC - 1 and i == 2))
                mm.then_inc(s_pj, 1)
            for c in range(KC):
                pe_turn(pe, 4 + KC + c, x_in, 4, c, MT + NT)
            pe.wait_ge(s_mk, 3 + MT * 2 * XP)
            pe.wait_ge(s_xl, XU0 - 2)
            for x_ in range(XP):
                for m in range(MT):
                    mm = pe.transpose(t_ps[:, (XU0 - 1) % 2, (MT * x_ + m) * P:(MT * x_ + m + 1) * P],
                                      mk_raw[:, m, x_ * P:(x_ + 1) * P], ident[:, :])
            mm.then_inc(s_xt, 1)
            pe.wait_ge(s_mv, MT)
            pe.wait_ge(s_mka, 2 * MT)
            pe.wait_ge(s_xl, XU0)
            for piece in range(12):
                pe_piece(pe, 0, piece // 4, piece)
            pe_scores(pe, 0, 0, 0, first=True)
            for half in range(2):
                pe.wait_ge(s_eh, 4 + half + 1)
                for j in range(4):
                    col = (4 * half + j) * P
                    mm = pe.transpose(t_ps[:, half, j * P:(j + 1) * P], v_t[1][:, col:col + P], ident[:, :])
                mm.then_inc(s_t, 1)
            pe_scores(pe, 0, 1, 0, first=True)
            with pe.Fori(0, LOOPS) as m:
                for par in range(2):
                    pe_step(pe, 2 * m + par, par)
            pe_step(pe, PAIRS - 2, 0)
            pe_step(pe, PAIRS - 1, 1, cross=True)
            pe.wait_ge(s_sq, 2 * XP)
            pe.wait_ge(s_o, 8 * PAIRS + 1)
            for c in range(CU):
                x_, t = c // NT, c % NT
                mm = pe.matmul(o_ps[:, 2 * c:2 * c + 2], xq_sq[:, x_, t * P:(t + 1) * P], half_ones[:, :],
                               start=True, stop=True)
            mm.then_inc(s_qs, 1)
            pe.wait_ge(s_eh, 6 * PAIRS + 4)
            pe.wait_ge(s_el, 4 * PAIRS + 4)
            pe.wait_ge(s_fg, 2 * USES * PAIRS)
            pe_cross_scores(pe, 0)
            pe.wait_ge(s_qr, 1)
            pe_cross_scores(pe, 1)
            for c in range(CU):
                pe_cross_turn(pe, c)
                if c + 2 < CU:
                    pe_cross_scores(pe, c + 2)
                if c % 4 == 3:
                    pe_cross_values(pe, c // 4)
            for t in range(NT):
                pe_project(pe, 0, t)
            for t in range(NT):
                pe_project(pe, 1, t, TURN_AT[t])
            pe_gate_up(pe, 0, 0, 0)
            pe_gate_up(pe, 0, 0, 1, turns=True)
            pe_gate_up(pe, 0, 1, 0)
            pe_gate_up(pe, 0, 1, 1)
            with pe.Fori(0, FLOOPS) as m:
                for par in range(2):
                    pe_ffn(pe, 2 * m + par, par)
            pe_ffn(pe, FC - 3, 0)
            pe_ffn(pe, FC - 2, 1)
            pe_ffn(pe, FC - 1, 0, nxt=False)


INPUTS = ["x", "mem", "attn_norm", "mem_norm", "w_mem_kv", "xq_norm", "xk_norm", "w_out", "ffn_norm",
          "w_gate", "w_up", "w_down", "sb_w_in"]


def kernel(**inputs):
    import numpy as np
    import concourse.bacc as bacc
    from concourse.bass_utils import run_bass_kernel_spmd

    nc = bacc.Bacc("TRN2", target_bir_lowering=False, num_devices=1)
    arrays, args = {}, []
    for name in INPUTS:
        a = np.ascontiguousarray(inputs[name])
        arrays[f"in_{name}"] = a
        args.append(nc.dram_tensor(f"in_{name}", a.shape, mybir.dt.from_np(a.dtype), kind="ExternalInput").ap())
    args.append(nc.dram_tensor("out", inputs["x"].shape, F32, kind="ExternalOutput").ap())
    trunk(nc, *args)
    return run_bass_kernel_spmd(nc, [arrays], core_ids=[0]).results[0]["out"]
```

```python
from contextlib import ExitStack

import concourse.bass as bass
from concourse import mybir

ALU = mybir.AluOpType
ACT = mybir.ActivationFunctionType
AX = mybir.AxisListType
F32 = mybir.dt.float32
F32R = mybir.dt.float32r
BF16 = mybir.dt.bfloat16

P = 128
BANK = 512
HD = 64
EPS = 1e-6
FUTURE = -1e30
QSCALE = HD ** -0.5


def trunk(nc, x, mem, attn_norm, mem_norm, w_mem_kv, xq_norm, xk_norm, w_out, ffn_norm, w_gate, w_up, w_down,
          sb_w_in, out):
    _, S, D = x.shape
    NT = S // P
    KC = D // P
    NH = S // BANK
    PAIRS = D // (2 * HD)
    M = mem.shape[1]
    MT = M // P
    XW = w_mem_kv.shape[2] // 2
    XP = XW // (2 * HD)
    OC = PAIRS + XP
    FF = w_gate.shape[2]
    FB = 2
    FC = FF // (FB * P)
    assert (NT, KC, NH, PAIRS, MT, XP) == (8, 8, 2, 8, 2, 2) and FC * FB * P == FF and FC % 2 == 1

    UNITS = []
    for g in range(NT // 2):
        for c in range((2 * g + 1) * P // BANK, -1, -1):
            for i in (2 * g, 2 * g + 1):
                n = (i + 1) * P
                UNITS.append((i, c * BANK, min(n - c * BANK, BANK), n - c * BANK <= BANK))
    NU = len(UNITS)
    USES = 2 * NU
    TUSE = USES + 2
    GROUP_END = [u for u in range(1, NU, 2) if UNITS[u][1] == 0]
    CARRIES = [2 * sum(UNITS[v][1] > 0 for v in range(u)) + h * (UNITS[u][1] > 0) for u in range(NU) for h in range(2)]
    NCARRY = 2 * sum(UNITS[v][1] > 0 for v in range(NU))
    MW = KC
    W0 = MW + 2 * XP
    CONV_AT = (2, 4, 6, 8, 9, 11)
    PIECES = ((0,), (1,), (2,), (3,), (4,), (5,), (6,), (7,), (8, 9), (10,), (11,), ())
    EVAC_AT = {4: 0, 8: 1, 11: 2}
    ZR, FR, GR, AR = 3, 4, 4, 3
    assert USES % ZR == 0 and USES % FR == 0 and USES % GR == 0 and NU % AR == 0 and TUSE % 2 == 0

    with ExitStack() as ctx:
        cursor = [-(-nc.sbuf_base // 32) * 32]
        
        def at(name, shape, dt, off):
            return nc.alloc_sbuf_tensor_at(name, shape, dt, offset=off)

        def size(shape):
            n = 4
            for s in shape[1:]:
                n *= s
            return -(-n // 32) * 32

        def take(name, shape, dt=F32, columns=None):
            t = at(name, [shape[0], columns] if columns else shape, dt, cursor[0])
            cursor[0] += size(shape)
            return t

        def sem(name):
            return ctx.enter_context(nc.semaphore(name))

        ident = take("ident", [P, P])
        ident_b = take("ident_b", [P, P // 2], BF16, P)
        future = take("future", [P, P // 2], BF16, P)
        eps_col = take("eps_col", [P, 1])
        gains = take("gains", [P, 3, KC])
        g_cross = take("g_cross", [P, 2])
        g_qk = take("g_qk", [P, 1])
        half_ones = take("half_ones", [P, 2])
        NS = MT + 2 * NT
        ssq = take("ssq", [P, NS])
        rms = take("rms", [P, NS])
        rstd = take("rstd", [P, NS])
        k_stat = take("k_stat", [P, 3, MT * 2 * XP])
        q_stat = take("q_stat", [P, 4, NT * 2 * XP])
        x_stat = take("x_stat", [P, 4, NT * 2 * XP])
        mk_at = cursor[0]
        mk_h = take("mk_h", [P, XP, M], F32R)
        mk_l = take("mk_l", [P, XP, M], F32R)
        mv = take("mv", [P, MT, XP, 4, HD], F32R)
        h_at = cursor[0]
        hh = take("hh", [P, KC, S], F32R)
        hl = take("hl", [P, KC, S], F32R)
        o_at = cursor[0]
        o_t = take("o_t", [P, PAIRS * S])
        qk_at = cursor[0]
        q_h, q_l, k_h, k_l = [], [], [], []
        for b in range(2):
            for name, to in (("q_h", q_h), ("q_l", q_l), ("k_h", k_h), ("k_l", k_l)):
                to.append(take(f"{name}{b}", [P, S], F32R))
        v_s = [None, None]
        v_s[1] = take("v_s1", [P, NT, 4, HD], F32R)
        v0_at = cursor[0]
        v_s[0] = take("v_s0", [P, NT, 4, HD], F32R)
        raw_at = cursor[0]
        w_raw = take("w_raw", [P, 2, 4, P])
        w_h = take("w_h", [P, 2, 4, P], F32R)
        wl_at = cursor[0]
        w_l = take("w_l", [P, 2, 4, P], F32R)
        fail_at = cursor[0]
        fail = take("fail", [P, FR, BANK + 4])
        x_at = cursor[0]
        succ = take("succ", [P, GR, BANK])
        a_h = take("a_h", [P, AR, 4, 2 * P], F32R)
        a_l = take("a_l", [P, AR, 4, 2 * P], F32R)
        pv_low = take("pv_low", [P, 2 * P])
        assert cursor[0] <= nc.sbuf_usable_end
        KB = 1024
        ROW = 4 * S

        v_t = [at(f"v_t{b}", [P, S], F32, qk_at + (4 * b + 1) * ROW) for b in range(2)]
        x_in = at("x_in", [P, NT, D], F32, x_at)
        m_in = at("m_in", [P, MT, D], F32, qk_at)
        m_hh = at("m_hh", [P, KC, M], F32R, qk_at + 2 * ROW)
        m_hl = at("m_hl", [P, KC, M], F32R, qk_at + 4 * ROW)
        mk_raw = at("mk_raw", [P, MT, XW], F32, qk_at + 6 * ROW)
        mk_sq = at("mk_sq", [P, MT, XW], F32, qk_at + 7 * ROW)
        junk = at("junk", [P, D], F32, v0_at)
        xq_sq = at("xq_sq", [P, XP, S], F32, v0_at)
        om_t = at("om_t", [P, 2 * S], F32, mk_at)
        wo_h = at("wo_h", [P, OC, BANK], F32R, h_at)
        wo_l = at("wo_l", [P, OC, BANK], F32R, h_at + OC * BANK * 4)
        wo_raw = at("wo_raw", [P, 4, BANK], F32, raw_at)
        rest = h_at + 2 * OC * BANK * 4
        hi_at = [rest + k * ROW for k in range(6)] + [qk_at + (4 + 2 * k) * ROW for k in range(3)] + [x_at + 32 * KB - 2 * ROW]
        lo_at = ([qk_at + k * ROW for k in range(4)] + [v0_at, v0_at + ROW] + [qk_at + (5 + 2 * k) * ROW for k in range(3)]
                 + [x_at + 32 * KB - ROW])
        o_h = [at(f"o_h{k}", [P, S], F32R, hi_at[k]) for k in range(OC)]
        o_l = [at(f"o_l{k}", [P, S], F32R, lo_at[k]) for k in range(OC)]
        x2 = at("x2", [P, NT, D], F32, fail_at)
        part = at("part", [P, NT, BANK], F32, o_at)
        xn = [at(f"xn{t}", [P, D], F32, (mk_at, mk_at + ROW, raw_at, raw_at + ROW)[t]) for t in range(4)]
        f_h = [at("f_h0", [P, KC, BANK], F32R, o_at), at("f_h1", [P, KC, BANK], F32R, h_at)]
        f_l = [at("f_l0", [P, KC, BANK], F32R, o_at + 16 * KB), at("f_l1", [P, KC, BANK], F32R, h_at + 16 * KB)]
        f_raw = at("f_raw", [P, 2, BANK], F32, wl_at)
        gw_h = at("gw_h", [P, FB, 2, KC, P], F32R, h_at + 32 * KB)
        gw_l = at("gw_l", [P, FB, 2, KC, P], F32R, h_at + 48 * KB)
        dw_h = [at("dw_h0", [P, FB, D], F32R, qk_at), at("dw_h1", [P, FB, D], F32R, v0_at)]
        dw_l = [at("dw_l0", [P, FB, D], F32R, qk_at + 2 * ROW), at("dw_l1", [P, FB, D], F32R, v0_at + 2 * ROW)]
        gu_h = [at("gu_h0", [P, FB, S], F32R, qk_at + 4 * ROW), at("gu_h1", [P, FB, S], F32R, qk_at + 8 * ROW)]
        gu_l = [at("gu_l0", [P, FB, S], F32R, qk_at + 6 * ROW), at("gu_l1", [P, FB, S], F32R, mk_at)]
        sig = at("sig", [P, 2, BANK], F32, x_at + 32 * KB - 2 * ROW)
        prod = at("prod", [P, 2, BANK], F32, x_at + 32 * KB - ROW)

        ps = ctx.enter_context(nc.psum_tensor("ps", [P, 8, BANK], F32))
        t_ps, j_ps, z_ps, o_ps = ps[:, 0:2], ps[:, 2:4], ps[:, 4:7], ps[:, 7]

        s_x = [sem(f"x{t}_loaded") for t in range(NT)]
        s_g = sem("gains_loaded")
        s_id = sem("constants_made")
        s_ssq = sem("squares_summed")
        s_rms = sem("root_taken")
        s_rstd = sem("root_inverted")
        s_xn = sem("x_scaled")
        s_xt = sem("x_transposed")
        s_xh = sem("x_high_done")
        s_xl = sem("x_low_done")
        s_w = [sem("w_even_loaded"), sem("w_odd_loaded")]
        s_wh = sem("w_high_done")
        s_wl = sem("w_low_done")
        s_pj = sem("w_used")
        s_eh = sem("qkv_high_done")
        s_el = sem("qk_low_done")
        s_z = sem("scores_ready")
        s_fg = sem("fail_succ_ready")
        s_scan = sem("stick_scanned")
        s_a = sem("weights_ready")
        s_t = sem("weights_transposed")
        s_th = sem("transposed_high_done")
        s_tl = sem("transposed_low_done")
        s_pv = sem("values_summed")
        s_pl = sem("low_part_copied")
        s_o = sem("heads_written")
        s_out = sem("out_stored")

        xd = x.rearrange("b (t p) d -> p (b t) d", p=P)
        wd = sb_w_in.rearrange("l (c p) n -> p (l c) n", p=P)

        def load_half(sp, n, column, k):
            sp.wait_ge(s_wl, n - 1)
            sp.dma_start(w_raw[:, k % 2], wd[:, 4 * (k % 2):4 * (k % 2) + 4, bass.ds(column, P)]
                         ).then_inc(s_w[k % 2], 16)

        def load_w(sp, s, k):
            load_half(sp, W0 + 6 * s + k, (k // 2) * D + s * P, k)

        def pe_project_in(pe, n, piece):
            hf, q = (piece % 4) // 2, piece % 2
            if q == 0:
                pe.wait_ge(s_wl, n + hf + 1)
            for c in (2 * q, 2 * q + 1):
                kc = 4 * hf + c
                for i, (w, h) in enumerate(((w_h, hh), (w_h, hl), (w_l, hh))):
                    for half in range(2):
                        mm = pe.matmul(j_ps[:, half], w[:, hf, c], h[:, kc, half * BANK:(half + 1) * BANK],
                                       start=(kc == 0 and i == 0), stop=(kc == KC - 1 and i == 2))
            if q == 1:
                mm.then_inc(s_pj, 1)

        def pe_piece(pe, s, piece, first=False):
            b = piece // 4
            if piece % 4 == 0 and not (first and b == 0):
                pe.wait_ge(s_eh, 6 * s + 2 * b)
                if b or not first:
                    pe.wait_ge(s_el, 4 * s + (0, 2, 4)[b])
            pe_project_in(pe, W0 + 6 * s + 2 * b, piece)

        def pe_v(pe, s, par, tbase):
            for half in range(2):
                pe.wait_ge(s_eh, 6 * s + 4 + half + 1)
                pe.wait_ge(s_tl, tbase + half - 1)
                for j in range(4):
                    col = (4 * half + j) * P
                    mm = pe.transpose(t_ps[:, half, j * P:(j + 1) * P], v_t[1 - par][:, col:col + P], ident[:, :])
                mm.then_inc(s_t, 1)

        def pe_scores(pe, s, u, par, first=False):
            i, k0, w, diag = UNITS[u]
            if u == 0:
                pe.wait_ge(s_el, 4 * s + 4)
            for h in range(2):
                n = 2 * u + h
                if first and n < ZR:
                    pe.wait_ge(s_ce, 2 * CU)
                else:
                    pe.wait_ge(s_fg, 2 * (USES * s + n - ZR) + 2)
                if diag:
                    pe.matmul(z_ps[:, n % ZR, w - P:w], ident_b[:, :], future[:, :], start=True, stop=False,
                              skip_group_check=True)
            for t, (qq, kk) in enumerate(((q_h, k_h), (q_h, k_l), (q_l, k_h))):
                for h in range(2):
                    n = 2 * u + h
                    bank = n % ZR
                    r = slice(HD * h, HD * h + HD)
                    mm = pe.matmul(z_ps[:, bank, 0:w], qq[par][r, i * P:(i + 1) * P], kk[par][r, k0:k0 + w],
                                   start=(t == 0 and not diag), stop=(t == 2), skip_group_check=True)
                    if t == 2:
                        mm.then_inc(s_z, 1)

        def pe_transposes(pe, s, u, h):
            n = 2 * u + h
            _, _, w, _ = UNITS[u]
            pe.wait_ge(s_a, USES * s + n + 1)
            pe.wait_ge(s_tl, 2 + TUSE * s + n - 1)
            for j in range(w // P):
                mm = pe.transpose(t_ps[:, n % 2, j * P:(j + 1) * P], succ[:, n % GR, j * P:(j + 1) * P], ident[:, :])
            mm.then_inc(s_t, 1)

        def pe_values(pe, s, u, par):
            i, k0, w, _ = UNITS[u]
            w_first = UNITS[u - 1][2]
            opens = UNITS[u][3]
            up = u // 2
            for h in range(2):
                slot = (2 * up + h) % AR
                pe.wait_ge(s_tl, 2 + TUSE * s + 2 * u + h + 1)
                if opens and h == 0:
                    g = (i - 1) // 2
                    pe.wait_ge(s_o, 8 * s + 2 * g + 1)
                if up == 0 and h == 0:
                    pe.wait_ge(s_tl, 2 + TUSE * s)
                for j in range(w // P):
                    q0 = 0 if j * P < w_first else P
                    for t, a in enumerate((a_h, a_l)):
                        mm = pe.matmul(o_ps[:, h * 2 * P + q0:(h + 1) * 2 * P],
                                       v_s[par][:, k0 // P + j, 2 * h:2 * h + 2, :].rearrange("p a d -> p (a d)"),
                                       a[:, slot, j, q0:2 * P],
                                       start=(opens and h == 0 and j == 0 and t == 0), stop=False,
                                       skip_group_check=True)
                mm.then_inc(s_pv, 1)

        def pe_step(pe, s, par, last=False):
            for u in range(NU):
                pe_transposes(pe, s, u, 0)
                pe_transposes(pe, s, u, 1)
                if u + 2 < NU:
                    pe_scores(pe, s, u + 2, par)
                elif not last:
                    pe_scores(pe, s + 1, u + 2 - NU, 1 - par)
                if last:
                    if u >= FILL_AT:
                        pe_project(pe, u - FILL_AT)
                else:
                    for piece in PIECES[u]:
                        pe_piece(pe, s + 1, piece)
                    if u == NU - 1:
                        pe_v(pe, s + 1, 1 - par, 2 + TUSE * s + USES)
                if u % 2:
                    pe_values(pe, s, u, par)

        def act_w(act, s, k):
            act_w_high(act, W0 + 6 * s + k, W0 // 2 + 3 * s + k // 2, k)

        def act_w_high(act, n, loads, k):
            act.wait_ge(s_w[k % 2], 16 * (loads + 1))
            act.wait_ge(s_pj, n - 1)
            act.activation(w_h[:, k % 2], w_raw[:, k % 2], ACT.Copy).then_inc(s_wh, 1)

        def act_evac(act, s, b, par):
            act.wait_ge(s_pj, W0 + 6 * s + 2 * b + 2)
            dst = (q_h[par], k_h[par], v_t[1 - par])[b]
            for half in range(2):
                c = slice(half * BANK, (half + 1) * BANK)
                act.activation(dst[:, c], j_ps[:, half], ACT.Copy).then_inc(s_eh, 1)

        def act_v(act, par, tcount):
            for half in range(2):
                act.wait_ge(s_t, tcount + half + 1)
                src = t_ps[:, half].rearrange("p (j h d) -> p j h d", j=4, h=2)
                act.activation(v_s[par][:, 4 * half:4 * half + 4, 0:4:3, :], src, ACT.Copy).then_inc(s_th, 1)

        def act_fail_succ(act, s, u, h, first=False):
            n = 2 * u + h
            w = UNITS[u][2]
            act.wait_ge(s_z, USES * s + n + 1)
            if not (first and n < FR):
                act.wait_ge(s_a, USES * s + n - FR + 1)
            act.activation(fail[:, n % FR, 0:w], z_ps[:, n % ZR, 0:w], ACT.Sigmoid, scale=-QSCALE).then_inc(s_fg, 1)
            if not (first and n < GR):
                act.wait_ge(s_t, 2 + TUSE * s + n - GR + 1 - (0 if u >= 2 else 2))
            act.activation(succ[:, n % GR, 0:w], z_ps[:, n % ZR, 0:w], ACT.Sigmoid, scale=QSCALE).then_inc(s_fg, 1)

        def act_high(act, s, u, h):
            n = 2 * u + h
            w = UNITS[u][2]
            up, col = u // 2, u % 2
            act.wait_ge(s_t, 2 + TUSE * s + n + 1)
            if col == 0:
                act.wait_ge(s_pv, NU * s + 2 * up + h + 1)
            act.activation(a_h[:, (2 * up + h) % AR, 0:w // P, col * P:(col + 1) * P],
                           t_ps[:, n % 2, 0:w].rearrange("p (j q) -> p j q", q=P), ACT.Copy).then_inc(s_th, 1)

        def act_low_rows(act, s, u):
            g = UNITS[u][0] // 2
            act.wait_ge(s_pv, AR + NU * s + u + 1)
            act.wait_ge(s_o, 8 * s + 2 * g + 1)
            act.activation(pv_low[0:HD, :], o_ps[HD:P, 0:2 * P], ACT.Copy).then_inc(s_pl, 1)
            act.activation(pv_low[HD:P, :], o_ps[0:HD, 2 * P:4 * P], ACT.Copy).then_inc(s_pl, 1)

        def act_step(act, s, par, last=False):
            side = iter(SPLITS) if last else None
            for u in range(NU):
                if u in EVAC_AT and not last:
                    act_evac(act, s + 1, EVAC_AT[u], 1 - par)
                act_high(act, s, u, 0)
                if u + 2 < NU:
                    act_fail_succ(act, s, u + 2, 0)
                elif not last:
                    act_fail_succ(act, s + 1, u + 2 - NU, 0)
                if last:
                    for _ in range(SPLIT_RATE[u] // 2):
                        act_split(act, next(side))
                act_high(act, s, u, 1)
                if u - 1 in GROUP_END:
                    act_low_rows(act, s, u - 1)
                if u + 2 < NU:
                    act_fail_succ(act, s, u + 2, 1)
                elif not last:
                    act_fail_succ(act, s + 1, u + 2 - NU, 1)
                if last:
                    for _ in range(SPLIT_RATE[u] - SPLIT_RATE[u] // 2):
                        act_split(act, next(side))
                if u in CONV_AT and not last:
                    k = CONV_AT.index(u)
                    if k < 4 or not (isinstance(s, int) and s == PAIRS - 2):
                        act_w(act, s + 1 + (k + 2) // 6, (k + 2) % 6)
                if u == NU - 1 and not last:
                    act_v(act, 1 - par, 2 + TUSE * s + USES)
            act_low_rows(act, s, NU - 1)

        def dve_w(dve, s, k):
            dve_w_low(dve, W0 + 6 * s + k, k)

        def dve_w_low(dve, n, k):
            dve.wait_ge(s_wh, n + 1)
            dve.tensor_tensor(w_l[:, k % 2], w_raw[:, k % 2], w_h[:, k % 2].bitcast(F32), ALU.subtract).then_inc(s_wl, 1)

        def dve_evac(dve, s, b, par):
            hi, lo = ((q_h, q_l), (k_h, k_l))[b]
            for half in range(2):
                c = slice(half * BANK, (half + 1) * BANK)
                dve.wait_ge(s_eh, 6 * s + 2 * b + half + 1)
                dve.tensor_tensor(lo[par][:, c], j_ps[:, half], hi[par][:, c].bitcast(F32), ALU.subtract).then_inc(s_el, 1)

        def dve_v(dve, par, tcount):
            for half in range(2):
                dve.wait_ge(s_th, tcount + half + 1)
                j = slice(4 * half, 4 * half + 4)
                dve.tensor_tensor(v_s[par][:, j, 1:3, :],
                                  t_ps[:, half].rearrange("p (j h d) -> p j h d", j=4, h=2),
                                  v_s[par][:, j, 0:4:3, :].bitcast(F32), ALU.subtract).then_inc(s_tl, 1)

        def dve_scan(dve, s, u, h):
            n = 2 * u + h
            _, k0, w, diag = UNITS[u]
            f = fail[:, n % FR]
            dve.wait_ge(s_fg, 2 * (USES * s + n) + 2)
            if diag:
                init = 1.0
            else:
                init = f[:, BANK:BANK + 1]
                dve.wait_ge(s_cy, NCARRY * s + CARRIES[n])
            back = f[:, 0:w][:, ::-1]
            dve.tensor_tensor_scan(back, back, back, init, ALU.mult, ALU.bypass).then_inc(s_scan, 1)
            if k0:
                dve.wait_ge(s_scan, USES * s + n + 1)
                dve.tensor_copy(f[:, BANK:BANK + 1], f[:, 0:1]).then_inc(s_cy, 1)

        def dve_weights(dve, s, u, h):
            n = 2 * u + h
            w = UNITS[u][2]
            dve.wait_ge(s_scan, USES * s + n + 1)
            if w == BANK and UNITS[u][0] * P >= BANK:
                dve.wait_ge(s_cy, NCARRY * s + CARRIES[n] + (UNITS[u][1] > 0))
            g = succ[:, n % GR, 0:w]
            dve.tensor_tensor(g, fail[:, n % FR, 1:w + 1], g, ALU.mult).then_inc(s_a, 1)

        def dve_low(dve, s, u, h):
            n = 2 * u + h
            w = UNITS[u][2]
            up, col = u // 2, u % 2
            dve.wait_ge(s_th, 2 + TUSE * s + n + 1)
            slot = (2 * up + h) % AR
            c = slice(col * P, (col + 1) * P)
            dve.tensor_tensor(a_l[:, slot, 0:w // P, c], t_ps[:, n % 2, 0:w].rearrange("p (j q) -> p j q", q=P),
                              a_h[:, slot, 0:w // P, c].bitcast(F32), ALU.subtract).then_inc(s_tl, 1)

        def dve_heads(dve, s, u):
            g = UNITS[u][0] // 2
            dve.wait_ge(s_pl, 8 * s + 2 * g + 2)
            for h in range(2):
                r = slice(HD * h, HD * h + HD)
                if isinstance(s, int) and s >= PAIRS - 2:
                    dst = om_t[r, (s - PAIRS + 2) * S + g * 2 * P:(s - PAIRS + 2) * S + (g + 1) * 2 * P]
                else:
                    dst = o_t[r, bass.ds(s * S + g * 2 * P, 2 * P)]
                dve.tensor_tensor(dst, o_ps[r, h * 2 * P:(h + 1) * 2 * P],
                                  pv_low[r, :], ALU.add).then_inc(s_o, 1)

        def dve_step(dve, s, par, last=False):
            side = iter([i for i in SPLITS if LOW[i][0] == 1])
            for u in range(NU):
                nxt = (s, u + 1) if u + 1 < NU else (s + 1, 0) if not last else None
                if u in EVAC_AT and EVAC_AT[u] < 2 and not last:
                    dve_evac(dve, s + 1, EVAC_AT[u], 1 - par)
                for h in range(2):
                    if nxt:
                        dve_scan(dve, *nxt, h)
                    dve_low(dve, s, u, h)
                    if nxt:
                        dve_weights(dve, *nxt, h)
                if u - 1 in GROUP_END:
                    dve_heads(dve, s, u - 1)
                if last:
                    for _ in range(DVE_RATE[u]):
                        split_low(dve, next(side))
                    if u > FILL_AT:
                        dve_add(dve, u - 1 - FILL_AT)
                if u in CONV_AT and not last:
                    k = CONV_AT.index(u)
                    if k < 4 or not (isinstance(s, int) and s == PAIRS - 2):
                        dve_w(dve, s + 1 + (k + 2) // 6, (k + 2) % 6)
                if u == NU - 1 and not last:
                    dve_v(dve, 1 - par, 2 + TUSE * s + USES)
            dve_heads(dve, s, NU - 1)

        s_cy = sem("stick_carried")
        s_m = [sem(f"mem{t}_loaded") for t in range(MT)]
        s_mk = sem("mem_keys_done")
        s_mka = sem("mem_keys_copied")
        s_mv = sem("mem_values_low_done")
        s_gq = sem("cross_gains_multiplied")
        s_sq = sem("cross_q_squared")
        s_qs = sem("cross_q_squares_summed")
        s_qr = sem("cross_q_roots")
        s_qi = sem("cross_q_scales")
        s_cs = sem("cross_scores_ready")
        s_cm = sem("cross_max_taken")
        s_cb = sem("cross_bias_ready")
        s_ce = sem("cross_exp_done")
        s_cr = sem("cross_sum_inverted")
        s_cp = sem("cross_weights_ready")
        s_cv = sem("cross_values_summed")
        s_cl = sem("cross_low_copied")
        s_co = sem("cross_heads_written")
        s_wo = [sem(f"w_out_slot{k}_loaded") for k in range(4)]
        s_qh = sem("cross_q_high_done")
        s_ql = sem("cross_q_low_done")
        s_ct = sem("cross_weights_transposed")
        s_cth = sem("cross_transposed_high_done")
        s_ctl = sem("cross_transposed_low_done")
        s_sh = sem("split_high_done")
        s_sl = [sem("split_low_done_by_gpsimd"), sem("split_low_done_by_vector")]
        s_op = sem("projection_ready")
        s_x2l = [[sem(f"residual{t}_{side}_loaded") for t in range(NT)] for side in ("left", "right")]
        s_x2 = sem("residual_added")
        s_fw = [sem("ffn_w_even_loaded"), sem("ffn_w_odd_loaded")]
        s_fh = sem("ffn_w_high_done")
        s_fl = sem("ffn_w_low_done")
        s_gp = sem("gate_up_ready")
        s_sg = sem("sigmoid_done")
        s_t1 = sem("silu_done")
        s_pr = sem("product_done")
        s_gh = sem("product_high_done")
        s_gl = sem("product_low_done")
        s_dn = sem("down_ready")

        memd = mem.rearrange("b (t p) d -> p (b t) d", p=P)
        mwd = w_mem_kv.rearrange("l (c p) n -> p (l c) n", p=P)
        wod = w_out.rearrange("l (c p) n -> p (l c) n", p=P)
        gud = [w.rearrange("l (c p) n -> p (l c) n", p=P) for w in (w_gate, w_up)]
        dnd = w_down.rearrange("l (f p) n -> p (l f) n", p=P)
        outd = out.rearrange("b (t p) d -> p (b t) d", p=P)
        flat = "p c n -> p (c n)"

        XU0 = 4 + 2 * KC + 1
        T1 = TUSE * PAIRS
        W1 = W0 + 6 * PAIRS
        CU = XP * NT
        LAST_ORDER = (6, 7, 8, 9, 2, 3, 0, 1, 4, 5)
        EARLY = 6
        SPLITS = [i for k in range(EARLY) for i in (("w", k, 0), ("o", k, 0))]
        SPLITS += [("o", k, 1) for k in range(EARLY)] + [("w", k, 0) for k in range(EARLY, OC)]
        LATER = [("o", k, half) for half in range(2) for k in (8, 9, 6, 7)]
        SECOND = [("w", k, 1) for k in range(OC)]
        HIGH = {i: n + 1 for n, i in enumerate(SPLITS + LATER + SECOND)}
        LOW, made = {}, [0, 0]
        for i in SPLITS + LATER + SECOND:
            e = 0 if i in SPLITS and (i[0] == "w" or i[2] == 1) else 1
            made[e] += 1
            LOW[i] = (e, made[e])
        SPLIT_RATE = (4, 4, 4, 2, 2, 2, 2, 2, 0, 0, 0, 0)
        DVE_RATE = (1, 2, 2, 1, 0, 0, 0, 0, 0, 0, 0, 0)
        FILL_AT = 5
        X_PIECES = {0: 1, 1: 2, 2: 3, 3: 4, 4: 5, 5: 6, 6: 7, 8: 8, 9: 9, 11: 10, 12: 11}
        X_CONV = {1: 2, 3: 3, 5: 4, 7: 5, 10: 6, 13: 7}
        X_EVAC = {3: 0, 7: 1, 13: 2}
        CQ = HD ** -0.5

        def act_root(act, k, src, dst):
            if k:
                act.wait_ge(s_ssq, k)
            act.activation(dst, src, ACT.Square, accum_out=ssq[:, k:k + 1]).then_inc(s_ssq, 1)
            act.wait_ge(s_ssq, k + 1)
            act.activation(rms[:, k:k + 1], ssq[:, k:k + 1], ACT.Sqrt, bias=eps_col[:, :], scale=1.0 / D
                           ).then_inc(s_rms, 1)

        def dve_scale(dve, k, src, dst):
            dve.wait_ge(s_rms, k + 1)
            dve.reciprocal(rstd[:, k:k + 1], rms[:, k:k + 1]).then_inc(s_rstd, 1)
            dve.wait_ge(s_rstd, k + 1)
            dve.tensor_scalar(dst, src, rstd[:, k:k + 1], None, ALU.mult).then_inc(s_xn, 1)

        def pe_turn(pe, g, src, rows, c, scaled):
            if g >= 2:
                pe.wait_ge(s_xl, g - 1)
            pe.wait_ge(s_xn, scaled)
            for t in range(4):
                rows_t = xn[t][:, c * P:(c + 1) * P] if src is None else src[:, rows + t, c * P:(c + 1) * P]
                mm = pe.transpose(t_ps[:, g % 2, t * P:(t + 1) * P], rows_t, ident[:, :])
                if g == XU0 and t == 0:
                    mm.then_inc(s_dn, 1)
            mm.then_inc(s_xt, 1)

        def act_turned(act, g, dst, gain):
            act.wait_ge(s_xt, g + 1)
            act.activation(dst, t_ps[:, g % 2], ACT.Copy, scale=gain).then_inc(s_xh, 1)

        def dve_turned(dve, g, dst, high, gain):
            dve.wait_ge(s_xh, g + 1)
            dve.scalar_tensor_tensor(dst, t_ps[:, g % 2], gain, high.bitcast(F32), ALU.mult, ALU.subtract
                                     ).then_inc(s_xl, 1)

        def act_mem_w(act, k):
            act.wait_ge(s_w[k % 2], 16 * (k // 2 + 1))
            if k >= 2:
                act.wait_ge(s_pj, k - 1)
            act.activation(w_h[:, k % 2], w_raw[:, k % 2], ACT.Copy).then_inc(s_wh, 1)

        def dve_mem_w(dve, k):
            dve.wait_ge(s_wh, k + 1)
            dve.tensor_tensor(w_l[:, k % 2], w_raw[:, k % 2], w_h[:, k % 2].bitcast(F32), ALU.subtract
                              ).then_inc(s_wl, 1)

        def operand(i):
            what, k, half = i
            if what == "w":
                return wo_raw[:, (OC * half + k) % 4], wo_h[:, k], wo_l[:, k]
            c = slice(half * BANK, (half + 1) * BANK)
            if k in (PAIRS - 2, PAIRS - 1):
                src = om_t[:, (k - PAIRS + 2) * S + half * BANK:(k - PAIRS + 2) * S + (half + 1) * BANK]
            else:
                at_ = (k if k < PAIRS else k - 2) * S + half * BANK
                src = o_t[:, at_:at_ + BANK]
            return src, o_h[k][:, c], o_l[k][:, c]

        def act_split(act, i):
            what, k, half = i
            src, high, _ = operand(i)
            if i == SPLITS[0]:
                act.wait_ge(s_pj, W1)
            if i == LATER[0]:
                act.wait_ge(s_o, 8 * PAIRS + 1)
                act.wait_ge(s_pv, AR + NU * PAIRS)
            if what == "w":
                N = OC * half + k
                act.wait_ge(s_wo[N % 4], 16 * (N // 4 + 1))
                if half:
                    act.wait_ge(s_op, NT if k < EARLY else 2 * NT)
            act.activation(high, src, ACT.Copy).then_inc(s_sh, 1)

        def split_low(eng, i):
            src, high, low = operand(i)
            e, _ = LOW[i]
            eng.wait_ge(s_sh, HIGH[i])
            eng.tensor_tensor(low, src, high.bitcast(F32), ALU.subtract).then_inc(s_sl[e], 1)

        def wait_split(eng, i):
            e, n = LOW[i]
            eng.wait_ge(s_sl[e], n)

        def act_cross_q(act, b):
            act.wait_ge(s_pj, MW + 2 * b + 2)
            for half in range(2):
                c = slice(half * BANK, (half + 1) * BANK)
                act.activation((q_h, k_h)[b][1][:, c], j_ps[:, half], ACT.Copy).then_inc(s_qh, 1)
            for half in range(2):
                c = slice(half * BANK, (half + 1) * BANK)
                act.wait_ge(s_ql, 2 * b + half + 1)
                act.activation(xq_sq[:, b, c], j_ps[:, half], ACT.Square).then_inc(s_sq, 1)

        def dve_cross_q(dve, b):
            for half in range(2):
                c = slice(half * BANK, (half + 1) * BANK)
                dve.wait_ge(s_qh, 2 * b + half + 1)
                dve.tensor_tensor((q_l, k_l)[b][1][:, c], j_ps[:, half], (q_h, k_h)[b][1][:, c].bitcast(F32),
                                  ALU.subtract).then_inc(s_ql, 1)

        def pe_cross_scores(pe, c):
            x_, t = c // NT, c % NT
            qh, ql = (q_h[1], q_l[1]) if x_ == 0 else (k_h[1], k_l[1])
            for i, (q, kk) in enumerate(((qh, mk_h), (qh, mk_l), (ql, mk_h))):
                for h in range(2):
                    n = 2 * c + h
                    if i == 0 and n >= ZR:
                        pe.wait_ge(s_ce, n - ZR + 1)
                    r = slice(HD * h, HD * h + HD)
                    mm = pe.matmul(z_ps[:, n % ZR, 0:M], q[r, t * P:(t + 1) * P], kk[r, x_],
                                   start=(i == 0), stop=(i == 2))
                    if i == 2:
                        mm.then_inc(s_cs, 1)

        def dve_cross_max(dve, c):
            for h in range(2):
                n = 2 * c + h
                dve.wait_ge(s_cs, n + 1)
                dve.tensor_reduce(x_stat[:, 0, n:n + 1], z_ps[:, n % ZR, 0:M], AX.X, ALU.max).then_inc(s_cm, 1)
            dve.wait_ge(s_cm, 2 * c + 2)
            p = slice(2 * c, 2 * c + 2)
            dve.tensor_tensor(x_stat[:, 1, p], x_stat[:, 0, p], q_stat[:, 3, p], ALU.mult).then_inc(s_cb, 1)

        def act_cross_exp(act, c):
            act.wait_ge(s_cb, c + 1)
            if c >= GR:
                act.wait_ge(s_ct, c - GR + 1)
            for h in range(2):
                n = 2 * c + h
                act.activation(succ[:, c % GR, h * M:(h + 1) * M], z_ps[:, n % ZR, 0:M], ACT.Exp,
                               bias=x_stat[:, 1, n:n + 1], scale=q_stat[:, 2, n:n + 1],
                               accum_out=x_stat[:, 2, n:n + 1]).then_inc(s_ce, 1)

        def dve_cross_weights(dve, c):
            p = slice(2 * c, 2 * c + 2)
            dve.wait_ge(s_ce, 2 * c + 2)
            dve.reciprocal(x_stat[:, 3, p], x_stat[:, 2, p]).then_inc(s_cr, 1)
            dve.wait_ge(s_cr, c + 1)
            for h in range(2):
                w = succ[:, c % GR, h * M:(h + 1) * M]
                dve.tensor_scalar(w, w, x_stat[:, 3, 2 * c + h:2 * c + h + 1], None, ALU.mult).then_inc(s_cp, 1)

        def pe_cross_turn(pe, c):
            pe.wait_ge(s_cp, 2 * c + 2)
            if c >= 2:
                pe.wait_ge(s_ctl, c - 1)
            for b in range(4):
                mm = pe.transpose(t_ps[:, c % 2, b * P:(b + 1) * P], succ[:, c % GR, b * P:(b + 1) * P], ident[:, :])
            mm.then_inc(s_ct, 1)

        def act_cross_high(act, c):
            y, col = c // 2, c % 2
            act.wait_ge(s_ct, c + 1)
            if col == 0 and y >= AR:
                act.wait_ge(s_cv, y - AR + 1)
            act.activation(a_h[:, y % AR, :, col * P:(col + 1) * P], t_ps[:, c % 2].rearrange("p (j q) -> p j q", q=P),
                           ACT.Copy).then_inc(s_cth, 1)

        def dve_cross_low(dve, c):
            y, q = c // 2, slice((c % 2) * P, (c % 2 + 1) * P)
            dve.wait_ge(s_cth, c + 1)
            dve.tensor_tensor(a_l[:, y % AR, :, q], t_ps[:, c % 2].rearrange("p (j q) -> p j q", q=P),
                              a_h[:, y % AR, :, q].bitcast(F32), ALU.subtract).then_inc(s_ctl, 1)

        def pe_cross_values(pe, y):
            x_ = 2 * y // NT
            pe.wait_ge(s_ctl, 2 * y + 2)
            if y:
                pe.wait_ge(s_co, 2 * y)
            for h in range(2):
                for m in range(MT):
                    for i, a in enumerate((a_h, a_l)):
                        mm = pe.matmul(o_ps[:, h * 2 * P:(h + 1) * 2 * P],
                                       mv[:, m, x_, 2 * h:2 * h + 2, :].rearrange("p a d -> p (a d)"),
                                       a[:, y % AR, MT * h + m], start=(h == 0 and m == 0 and i == 0), stop=False,
                                       skip_group_check=True)
            mm.then_inc(s_cv, 1)

        def act_cross_low_rows(act, y):
            act.wait_ge(s_cv, y + 1)
            if y:
                act.wait_ge(s_co, 2 * y)
            act.activation(pv_low[0:HD, :], o_ps[HD:P, 0:2 * P], ACT.Copy).then_inc(s_cl, 1)
            act.activation(pv_low[HD:P, :], o_ps[0:HD, 2 * P:4 * P], ACT.Copy).then_inc(s_cl, 1)

        def dve_cross_heads(dve, y):
            at_ = (PAIRS - 2 + 2 * y // NT) * S + (y % (NT // 2)) * 2 * P
            dve.wait_ge(s_cl, 2 * y + 2)
            for h in range(2):
                r = slice(HD * h, HD * h + HD)
                dve.tensor_tensor(o_t[r, at_:at_ + 2 * P], o_ps[r, h * 2 * P:(h + 1) * 2 * P], pv_low[r, :], ALU.add
                                  ).then_inc(s_co, 1)

        def pe_project(pe, i, turns=()):
            t, n = i % NT, i // (2 * NT)
            last = i == 3 * NT - 1
            order = (range(EARLY), range(EARLY, OC), LAST_ORDER if last else range(OC))[i // NT]
            if i >= 2:
                pe.wait_ge(s_x2, i - 1)
            for at_, k in enumerate(order):
                if t == 0:
                    wait_split(pe, ("w", k, n))
                if n == 0 and t % 4 == 0:
                    wait_split(pe, ("o", k, t // 4))
                for j, (o, w) in enumerate(((o_h, wo_h), (o_h, wo_l), (o_l, wo_h))):
                    mm = pe.matmul(j_ps[:, i % 2], o[k][:, t * P:(t + 1) * P], w[:, k],
                                   start=(at_ == 0 and j == 0), stop=(at_ == len(order) - 1 and j == 2))
                if last and at_ == 5:
                    mm.then_inc(s_op, 1)
                if at_ in (2, 5, 8):
                    for c in turns[at_ // 3:at_ // 3 + 1]:
                        pe_turn(pe, XU0 + c, None, 0, c, MT + NT + 4)
            mm.then_inc(s_op, 1)

        PROJECTED = 3 * NT + 1
        X0 = 3 * NT

        def dve_add(dve, i):
            t, n = i % NT, i // (2 * NT)
            dve.wait_ge(s_op, i + 1 + (i == 3 * NT - 1))
            if i // NT != 1:
                dve.wait_ge(s_x2l[n][t], 16)
            else:
                dve.wait_ge(s_x2, t + 1)
            dst = part[:, t] if i < NT else x2[:, t, n * BANK:(n + 1) * BANK]
            src = dst if n else part[:, t]
            dve.tensor_tensor(dst, j_ps[:, i % 2], src, ALU.add).then_inc(s_x2, 1)

        def sp_ffn(sp, r, kind, c, j):
            if not (isinstance(r, int) and r < 2):
                sp.wait_ge(s_fl, r - 1)
            slot = j % 2
            if kind == "gate":
                fb, mat, kh = j // 4, j // 2 % 2, j % 2
                src = gud[mat][:, 4 * kh:4 * kh + 4, bass.ds((c * FB + fb) * P, P)]
                dst = f_raw[:, slot].rearrange("p (c n) -> p c n", c=4)
            else:
                fb, n = j // 2, j % 2
                src = dnd[:, bass.ds(c * FB + fb, 1), n * BANK:(n + 1) * BANK]
                dst = f_raw[:, slot:slot + 1]
            sp.dma_start(dst, src).then_inc(s_fw[slot], 16)

        def ffn_w(kind, par, j, high):
            if kind == "gate":
                fb, mat, kh = j // 4, j // 2 % 2, j % 2
                return (gw_h if high else gw_l)[:, fb, mat, 4 * kh:4 * kh + 4].rearrange(flat)
            return (dw_h if high else dw_l)[par][:, j // 2, (j % 2) * BANK:(j % 2 + 1) * BANK]

        def row_of(kind, c, j):
            if kind == "gate":
                return j if isinstance(c, int) and c == 0 else 12 * c - 4 + j
            return 16 + 12 * c + j - (8 if isinstance(c, int) and c == FC - 1 else 0)

        def act_ffn_w(act, kind, c, j, par=0):
            r = row_of(kind, c, j)
            rr = r - j % 2
            act.wait_ge(s_fw[j % 2], rr * 8 + 16)
            if kind == "gate":
                if isinstance(c, int) and c == 0:
                    act.wait_ge(s_op, PROJECTED - (j < 4))
                else:
                    act.wait_ge(s_gp, 8 * c - 4 + j // 2 + 1)
            act.activation(ffn_w(kind, par, j, True), f_raw[:, j % 2], ACT.Copy).then_inc(s_fh, 1)

        def dve_ffn_w(dve, kind, c, j, par=0):
            r = row_of(kind, c, j)
            dve.wait_ge(s_fh, r + 1)
            dve.tensor_tensor(ffn_w(kind, par, j, False), f_raw[:, j % 2], ffn_w(kind, par, j, True).bitcast(F32),
                              ALU.subtract).then_inc(s_fl, 1)

        def pe_gate_up(pe, c, half, fb, turns=False):
            first = isinstance(c, int) and c == 0
            q = 4 * c + 2 * half + fb
            if not (first and half == 0):
                pe.wait_ge(s_pr, q - 1)
            if first:
                pe.wait_ge(s_xl, XU0 + KC * (half + 1))
                pe.wait_ge(s_ssq, NS)
            for mat in range(2):
                for kh in range(2):
                    if half == 0:
                        pe.wait_ge(s_fl, row_of("gate", c, 4 * fb + 2 * mat + kh) + 1)
                    for k in range(4 * kh, 4 * kh + 4):
                        for i, (w, f) in enumerate(((gw_h, f_h), (gw_h, f_l), (gw_l, f_h))):
                            mm = pe.matmul(ps[:, 4 + 2 * fb + mat], w[:, fb, mat, k], f[half][:, k],
                                           start=(k == 0 and i == 0), stop=(k == KC - 1 and i == 2))
                        if turns and k % 2 and k < KC - 1:
                            pe_turn(pe, XU0 + KC + 3 * mat + k // 2, None, 0, 3 * mat + k // 2, NS)
                mm.then_inc(s_gp, 1)
            if turns:
                for c_ in range(6, KC):
                    pe_turn(pe, XU0 + KC + c_, None, 0, c_, NS)

        def act_sigmoid(act, c, half, fb):
            q = 4 * c + 2 * half + fb
            act.wait_ge(s_gp, 2 * q + 1)
            if not (isinstance(c, int) and c == 0 and half == 0):
                act.wait_ge(s_pr, q - 1)
            act.activation(sig[:, fb], ps[:, 4 + 2 * fb], ACT.Sigmoid).then_inc(s_sg, 1)

        def dve_product(dve, c, half, fb):
            q = 4 * c + 2 * half + fb
            dve.wait_ge(s_sg, q + 1)
            dve.tensor_tensor(sig[:, fb], ps[:, 4 + 2 * fb], sig[:, fb], ALU.mult).then_inc(s_t1, 1)
            dve.wait_ge(s_t1, q + 1)
            dve.wait_ge(s_gp, 2 * q + 2)
            if not (isinstance(c, int) and c == 0 and half == 0):
                dve.wait_ge(s_gl, q - 1)
            dve.tensor_tensor(prod[:, fb], ps[:, 5 + 2 * fb], sig[:, fb], ALU.mult).then_inc(s_pr, 1)

        def act_product_high(act, c, half, fb, par):
            q = 4 * c + 2 * half + fb
            act.wait_ge(s_pr, q + 1)
            if not (isinstance(c, int) and c == 0):
                act.wait_ge(s_dn, 2 * NT * (c - 1) + 1)
            act.activation(gu_h[par][:, fb, half * BANK:(half + 1) * BANK], prod[:, fb], ACT.Copy).then_inc(s_gh, 1)

        def dve_product_low(dve, c, half, fb, par):
            q = 4 * c + 2 * half + fb
            cols = slice(half * BANK, (half + 1) * BANK)
            dve.wait_ge(s_gh, q + 1)
            dve.tensor_tensor(gu_l[par][:, fb, cols], prod[:, fb], gu_h[par][:, fb, cols].bitcast(F32), ALU.subtract
                              ).then_inc(s_gl, 1)

        def pe_down(pe, c, par):
            pe.wait_ge(s_fl, row_of("down", c, 3) + 1)
            for t in range(NT):
                if t % 4 == 0:
                    pe.wait_ge(s_gl, 4 * c + 2 * (t // 4) + 2)
                for n in range(2):
                    d = 2 * t + n
                    pe.wait_ge(s_x2, X0 + 2 * NT * c + d - 3)
                    for fb in range(FB):
                        for i, (g, w) in enumerate(((gu_h, dw_h[par]), (gu_h, dw_l[par]), (gu_l, dw_h[par]))):
                            mm = pe.matmul(ps[:, (2, 3, 0, 1)[d % 4]], g[par][:, fb, t * P:(t + 1) * P],
                                           w[:, fb, n * BANK:(n + 1) * BANK],
                                           start=(fb == 0 and i == 0), stop=(fb == FB - 1 and i == 2))
                    mm.then_inc(s_dn, 1)

        def dve_down(dve, c, ahead, last_w):
            for t in range(NT):
                if ahead and 0 < t < 5:
                    dve_ffn_w(dve, "gate", c + 2, 3 + t)
                if last_w and t % 2 == 0:
                    dve_ffn_w(dve, "down", c + 1, t // 2, 1 - c % 2)
                for n in range(2):
                    d = 2 * t + n
                    dve.wait_ge(s_dn, 2 * NT * c + d + 2)
                    dve.wait_ge(s_x2, X0 - 2 * NT + 2 * NT * c + d + 1)
                    o = x2[:, t, n * BANK:(n + 1) * BANK]
                    dve.tensor_tensor(o, ps[:, (2, 3, 0, 1)[d % 4]], o, ALU.add).then_inc(s_x2, 1)

        def sp_step(sp, c, ahead=True):
            for j in range(4):
                sp_ffn(sp, row_of("down", c, j), "down", c, j)
            if ahead:
                for j in range(8):
                    sp_ffn(sp, row_of("gate", c + 2, j), "gate", c + 2, j)

        def act_ffn(act, c, par, nxt=True, ahead=True, last_w=False):
            if nxt:
                for j in range(4):
                    act_ffn_w(act, "down", c, j, par)
            if nxt:
                for half in range(2):
                    for fb in range(FB):
                        act_sigmoid(act, c + 1, half, fb)
                        act_product_high(act, c + 1, half, fb, 1 - par)
                        if half == 1 and ahead:
                            for j in range(4 * fb, 4 * fb + 4):
                                act_ffn_w(act, "gate", c + 2, j)
            if last_w:
                for j in range(4):
                    act_ffn_w(act, "down", c + 1, j, 1 - par)

        def dve_ffn(dve, c, par, nxt=True, ahead=True, last_w=False):
            if nxt:
                for j in range(4):
                    dve_ffn_w(dve, "down", c, j, par)
            if nxt:
                for half in range(2):
                    for fb in range(FB):
                        dve_product(dve, c + 1, half, fb)
                        dve_product_low(dve, c + 1, half, fb, 1 - par)
                        if half == 1 and fb == 0 and ahead:
                            for j in range(4):
                                dve_ffn_w(dve, "gate", c + 2, j)
            dve_down(dve, c, ahead, last_w)

        def pe_ffn(pe, c, par, nxt=True):
            if nxt:
                for half in range(2):
                    for fb in range(FB):
                        pe_gate_up(pe, c + 1, half, fb)
            pe_down(pe, c, par)

        TURN_AT = [(), (), (), (), (), (0, 1, 2), (3, 4, 5), (6, 7)]
        FLOOPS = (FC - 3) // 2
        block = ctx.enter_context(nc.Block())
        LOOPS = (PAIRS - 2) // 2

        @block.sync
        def _(sp):
            for t in range(MT):
                sp.dma_start(m_in[:, t], memd[:, t]).then_inc(s_m[t], 16)
            with nc.allow_non_contiguous_dma("gains, one per partition"):
                for i, g in enumerate((attn_norm, mem_norm, ffn_norm)):
                    sp.dma_start(gains[:, i], g.rearrange("l (c p) -> p (l c)", p=P)).then_inc(s_g, 16)
                for i, g in enumerate((xq_norm, xk_norm)):
                    for h in range(2):
                        sp.dma_start(g_cross[HD * h:HD * h + HD, i:i + 1], g.rearrange("l d -> d l")
                                     ).then_inc(s_g, 16)
            for t in range(4):
                sp.dma_start(x_in[:, t], xd[:, t]).then_inc(s_x[t], 16)
            for k in range(MW):
                if k >= 2:
                    sp.wait_ge(s_wl, k - 1)
                sp.dma_start(w_raw[:, k % 2].rearrange(flat), mwd[:, k]).then_inc(s_w[k % 2], 16)
                if k % 2:
                    t = 4 + k // 2
                    sp.dma_start(x_in[:, t], xd[:, t]).then_inc(s_x[t], 16)
            for k in range(2 * XP):
                load_half(sp, MW + k, 3 * D + (k // 2) * P, k)
            for k in range(6):
                load_w(sp, 0, k)
            with sp.Fori(0, LOOPS) as m:
                for par in range(2):
                    for k in range(6):
                        load_w(sp, 2 * m + par + 1, k)
            for k in range(6):
                load_w(sp, PAIRS - 1, k)
            sp.wait_ge(s_wl, W1)
            sp.wait_ge(s_pj, W1)
            for N in range(2 * OC):
                if N == OC:
                    wait_split(sp, ("o", EARLY - 1, 1))
                    wait_split(sp, ("o", EARLY - 1, 0))
                    for t in range(NT):
                        sp.dma_start(part[:, t], xd[:, t, 0:BANK]).then_inc(s_x2l[0][t], 16)
                    sp.wait_ge(s_o, 8 * PAIRS + 1)
                    for t in range(NT):
                        sp.dma_start(x2[:, t, BANK:D], xd[:, t, BANK:D]).then_inc(s_x2l[1][t], 16)
                if N >= 4:
                    wait_split(sp, ("w", (N - 4) % OC, (N - 4) // OC))
                k, n = N % OC, N // OC
                sp.dma_start(wo_raw[:, N % 4], wod[:, k, n * BANK:(n + 1) * BANK]).then_inc(s_wo[N % 4], 16)
            for j in range(2):
                sp_ffn(sp, j, "gate", 0, j)
            for j in range(2, 8):
                sp_ffn(sp, j, "gate", 0, j)
            for j in range(8):
                sp_ffn(sp, 8 + j, "gate", 1, j)
            with sp.Fori(0, FLOOPS) as m:
                for par in range(2):
                    sp_step(sp, 2 * m + par)
            sp_step(sp, FC - 3)
            sp_step(sp, FC - 2, ahead=False)
            sp_step(sp, FC - 1, ahead=False)
            for t in range(NT):
                sp.wait_ge(s_x2, X0 + 2 * NT * (FC - 1) + 2 * t + 2)
                sp.dma_start(outd[:, t], x2[:, t]).then_inc(s_out, 16)
            sp.wait_ge(s_out, 16 * NT)

        @block.gpsimd
        def _(pool):
            pool.memset(ident[:, :], 0.0).then_inc(s_id, 1)
            pool.memset(eps_col[:, :], EPS).then_inc(s_id, 1)
            pool.memset(fail[:, :, :], 1.0).then_inc(s_id, 1)
            pool.memset(ident_b[:, :], 0.0).then_inc(s_id, 1)
            pool.memset(future[:, :], FUTURE).then_inc(s_id, 1)
            pool.memset(half_ones[:, :], 0.0).then_inc(s_id, 1)
            pool.wait_ge(s_id, 6)
            for h in range(2):
                pool.memset(half_ones[HD * h:HD * h + HD, h:h + 1], 1.0).then_inc(s_id, 1)
                pool.wait_ge(s_id, 7 + h)
            for i in (ident, ident_b):
                pool.affine_select(out=i[:, :], in_=i[:, :], compare_op=ALU.not_equal, fill=1.0, base=0,
                                   pattern=[[-1, P]], channel_multiplier=1).then_inc(s_id, 1)
            pool.affine_select(out=future[:, :], in_=future[:, :], compare_op=ALU.is_ge, fill=0.0, base=0,
                               pattern=[[1, P]], channel_multiplier=-1).then_inc(s_id, 1)
            for i in SPLITS:
                if LOW[i][0] == 0:
                    split_low(pool, i)

        MADE = 11

        @block.scalar
        def _(act):
            act.wait_ge(s_id, MADE)
            for t in range(MT):
                act.wait_ge(s_m[t], 16)
                act_root(act, t, m_in[:, t], junk[:, :])
            for t in range(4):
                act.wait_ge(s_x[t], 16)
                act_root(act, MT + t, x_in[:, t], junk[:, :])
            act.wait_ge(s_g, 16 * 7)
            for g in range(4):
                act.wait_ge(s_xt, g + 1)
                for i in range(2):
                    last = act.activation(m_hh[:, 2 * g + i], t_ps[:, g % 2, i * M:(i + 1) * M], ACT.Copy,
                                          scale=gains[:, 1, 2 * g + i:2 * g + i + 1])
                last.then_inc(s_xh, 1)
            for k in range(2):
                act_mem_w(act, k)
            for c in range(KC):
                act_turned(act, 4 + c, hh[:, c, 0:BANK], gains[:, 0, c:c + 1])
            for k in range(2, MW):
                act_mem_w(act, k)
            for t in range(4, NT):
                act.wait_ge(s_x[t], 16)
                act_root(act, MT + t, x_in[:, t], junk[:, :])
            act.wait_ge(s_pj, MW)
            for m in range(MT):
                act.activation(mk_raw[:, m], j_ps[:, m, 0:XW], ACT.Copy).then_inc(s_mka, 1)
                act.activation(mv[:, m, :, 0:4:3, :], j_ps[:, m, XW:2 * XW].rearrange("p (x h d) -> p x h d", x=XP, h=2),
                               ACT.Copy).then_inc(s_mka, 1)
            act.wait_ge(s_mk, 2)
            act.activation(k_stat[:, 1], k_stat[:, 0], ACT.Sqrt, bias=eps_col[:, :], scale=1.0 / HD).then_inc(s_mka, 1)
            for c in range(KC):
                act_turned(act, 4 + KC + c, hh[:, c, BANK:2 * BANK], gains[:, 0, c:c + 1])
            act.wait_ge(s_gq, 1)
            act_turned(act, XU0 - 1, mk_h[:, :, :].rearrange("p x m -> p (x m)"), g_qk[:, :])
            for k in range(2 * XP):
                act_w_high(act, MW + k, MW // 2 + k // 2, k)
                if k == 3:
                    act_cross_q(act, 0)
            act_w(act, 0, 0)
            act_cross_q(act, 1)
            act_w(act, 0, 1)
            act.wait_ge(s_qs, 1)
            act.activation(q_stat[:, 0], o_ps[:, 0:2 * CU], ACT.Sqrt, bias=eps_col[:, :], scale=1.0 / HD
                           ).then_inc(s_qr, 1)
            act_cross_exp(act, 0)
            act_cross_exp(act, 1)
            for c in range(CU):
                if c in X_EVAC:
                    act_evac(act, 0, X_EVAC[c], 0)
                act_cross_high(act, c)
                if c + 2 < CU:
                    act_cross_exp(act, c + 2)
                if c % 2 == 0 and c:
                    act_cross_low_rows(act, c // 2 - 1)
                if c in X_CONV:
                    act_w(act, X_CONV[c] // 6, X_CONV[c] % 6)
            act_cross_low_rows(act, CU // 2 - 1)
            act_fail_succ(act, 0, 0, 0, first=True)
            act_fail_succ(act, 0, 0, 1, first=True)
            act_v(act, 0, 0)
            act_fail_succ(act, 0, 1, 0, first=True)
            act_fail_succ(act, 0, 1, 1, first=True)
            with act.Fori(0, LOOPS) as m:
                for par in range(2):
                    act_step(act, 2 * m + par, par)
            act_step(act, PAIRS - 2, 0)
            act_step(act, PAIRS - 1, 1, last=True)
            for i in LATER + SECOND:
                act_split(act, i)
            for t in range(NT):
                for c in TURN_AT[t]:
                    if c == 0:
                        wait_split(act, LATER[-1])
                    act_turned(act, XU0 + c, f_h[0][:, c], gains[:, 2, c:c + 1])
                if t == NT - 1:
                    for j in range(4):
                        act_ffn_w(act, "gate", 0, j)
                act.wait_ge(s_x2, 2 * NT + t + 1)
                act_root(act, MT + NT + t, x2[:, t], ps[:, 4:6].rearrange("p b n -> p (b n)"))
            for j in range(4, 8):
                act_ffn_w(act, "gate", 0, j)
            for half in range(2):
                for fb in range(FB):
                    act_sigmoid(act, 0, half, fb)
                    act_product_high(act, 0, half, fb, 0)
                    if half == 0 and fb == 0:
                        for c in range(KC):
                            act_turned(act, XU0 + KC + c, f_h[1][:, c], gains[:, 2, c:c + 1])
                    if half == 1:
                        for j in range(4 * fb, 4 * fb + 4):
                            act_ffn_w(act, "gate", 1, j)
            with act.Fori(0, FLOOPS) as m:
                for par in range(2):
                    act_ffn(act, 2 * m + par, par)
            act_ffn(act, FC - 3, 0)
            act_ffn(act, FC - 2, 1, ahead=False, last_w=True)

        @block.vector
        def _(dve):
            for t in range(MT):
                dve_scale(dve, t, m_in[:, t], m_in[:, t])
            for t in range(4):
                dve_scale(dve, MT + t, x_in[:, t], x_in[:, t])
            dve.wait_ge(s_g, 16 * 7)
            dve.tensor_tensor(g_qk[:, :], g_cross[:, 0:1], g_cross[:, 1:2], ALU.mult).then_inc(s_gq, 1)
            for g in range(4):
                dve.wait_ge(s_xh, g + 1)
                for i in range(2):
                    c = 2 * g + i
                    last = dve.scalar_tensor_tensor(m_hl[:, c], t_ps[:, g % 2, i * M:(i + 1) * M],
                                                    gains[:, 1, c:c + 1], m_hh[:, c].bitcast(F32),
                                                    ALU.mult, ALU.subtract)
                    if c == 0:
                        last.then_inc(s_o, 1)
                last.then_inc(s_xl, 1)
            for k in range(2):
                dve_mem_w(dve, k)
            for c in range(KC):
                dve_turned(dve, 4 + c, hl[:, c, 0:BANK], hh[:, c, 0:BANK], gains[:, 0, c:c + 1])
            for k in range(2, MW):
                dve_mem_w(dve, k)
            for t in range(4, NT):
                dve_scale(dve, MT + t, x_in[:, t], x_in[:, t])
            dve.wait_ge(s_mka, 2 * MT)
            for m in range(MT):
                dve.tensor_tensor(mv[:, m, :, 1:3, :], j_ps[:, m, XW:2 * XW].rearrange("p (x h d) -> p x h d", x=XP, h=2),
                                  mv[:, m, :, 0:4:3, :].bitcast(F32), ALU.subtract).then_inc(s_mv, 1)
            allk = mk_raw[:, :, :].rearrange("p m n -> p (m n)")
            allsq = mk_sq[:, :, :].rearrange("p m n -> p (m n)")
            dve.tensor_tensor(allsq, allk, allk, ALU.mult).then_inc(s_mk, 1)
            dve.wait_ge(s_mk, 1)
            dve.tensor_reduce(k_stat[:, 0], allsq.rearrange("p (g d) -> p g d", d=HD), AX.X, ALU.add).then_inc(s_mk, 1)
            dve.wait_ge(s_mka, 2 * MT + 1)
            dve.reciprocal(k_stat[:, 2], k_stat[:, 1]).then_inc(s_mk, 1)
            dve.wait_ge(s_mk, 3)
            for g in range(MT * 2 * XP):
                kk = allk[:, g * HD:(g + 1) * HD]
                dve.tensor_scalar(kk, kk, k_stat[:, 2, g:g + 1], None, ALU.mult).then_inc(s_mk, 1)
            for c in range(KC):
                dve_turned(dve, 4 + KC + c, hl[:, c, BANK:2 * BANK], hh[:, c, BANK:2 * BANK], gains[:, 0, c:c + 1])
            dve_turned(dve, XU0 - 1, mk_l[:, :, :].rearrange("p x m -> p (x m)"),
                       mk_h[:, :, :].rearrange("p x m -> p (x m)"), g_qk[:, :])
            for k in range(2 * XP):
                dve_w_low(dve, MW + k, k)
                if k == 3:
                    dve_cross_q(dve, 0)
            dve_w(dve, 0, 0)
            dve_cross_q(dve, 1)
            dve_w(dve, 0, 1)
            dve.wait_ge(s_qr, 1)
            dve.reciprocal(q_stat[:, 1], q_stat[:, 0]).then_inc(s_qi, 1)
            dve.wait_ge(s_qi, 1)
            dve.tensor_scalar(q_stat[:, 2], q_stat[:, 1], CQ, None, ALU.mult).then_inc(s_qi, 1)
            dve.tensor_scalar(q_stat[:, 3], q_stat[:, 1], -CQ, None, ALU.mult).then_inc(s_qi, 1)
            dve.wait_ge(s_qi, 3)
            dve_cross_max(dve, 0)
            dve_cross_max(dve, 1)
            dve_cross_weights(dve, 0)
            for c in range(CU):
                if c in X_EVAC and X_EVAC[c] < 2:
                    dve_evac(dve, 0, X_EVAC[c], 0)
                if c + 1 < CU:
                    dve_cross_weights(dve, c + 1)
                dve_cross_low(dve, c)
                if c + 2 < CU:
                    dve_cross_max(dve, c + 2)
                if c % 2 == 0 and c:
                    dve_cross_heads(dve, c // 2 - 1)
                if c in X_CONV:
                    dve_w(dve, X_CONV[c] // 6, X_CONV[c] % 6)
            dve_cross_heads(dve, CU // 2 - 1)
            dve_scan(dve, 0, 0, 0)
            dve_scan(dve, 0, 0, 1)
            dve_weights(dve, 0, 0, 0)
            dve_weights(dve, 0, 0, 1)
            dve_v(dve, 0, 0)
            with dve.Fori(0, LOOPS) as m:
                for par in range(2):
                    dve_step(dve, 2 * m + par, par)
            dve_step(dve, PAIRS - 2, 0)
            dve_step(dve, PAIRS - 1, 1, last=True)
            for i in LATER[:4]:
                split_low(dve, i)
            for i in range(NU - 1 - FILL_AT, NT):
                dve_add(dve, i)
            for i in LATER[4:]:
                split_low(dve, i)
            for t in range(NT):
                dve_add(dve, NT + t)
                if t < EARLY:
                    split_low(dve, SECOND[t])
            for i in SECOND[EARLY:]:
                split_low(dve, i)
            for t in range(NT):
                for c in TURN_AT[t]:
                    dve_turned(dve, XU0 + c, f_l[0][:, c], f_h[0][:, c], gains[:, 2, c:c + 1])
                if t == NT - 1:
                    for j in range(2):
                        dve_ffn_w(dve, "gate", 0, j)
                dve_add(dve, 2 * NT + t)
                if t < 4:
                    dve_scale(dve, MT + NT + t, x2[:, t], xn[t][:, :])
            for j in range(2, 4):
                dve_ffn_w(dve, "gate", 0, j)
            dve.wait_ge(s_xt, XU0 + KC)
            for t in range(4, NT):
                dve_scale(dve, MT + NT + t, x2[:, t], xn[t - 4][:, :])
            for j in range(4, 8):
                dve_ffn_w(dve, "gate", 0, j)
            for half in range(2):
                for fb in range(FB):
                    dve_product(dve, 0, half, fb)
                    dve_product_low(dve, 0, half, fb, 0)
                    if half == 0 and fb == 0:
                        for c in range(KC):
                            dve_turned(dve, XU0 + KC + c, f_l[1][:, c], f_h[1][:, c], gains[:, 2, c:c + 1])
                    if half == 1:
                        for j in range(4 * fb, 4 * fb + 4):
                            dve_ffn_w(dve, "gate", 1, j)
            with dve.Fori(0, FLOOPS) as m:
                for par in range(2):
                    dve_ffn(dve, 2 * m + par, par)
            dve_ffn(dve, FC - 3, 0)
            dve_ffn(dve, FC - 2, 1, ahead=False, last_w=True)
            dve_ffn(dve, FC - 1, 0, nxt=False, ahead=False)

        @block.tensor
        def _(pe):
            pe.wait_ge(s_id, MADE)
            for g in range(4):
                if g >= 2:
                    pe.wait_ge(s_xl, g - 1)
                for i in range(2):
                    for t in range(MT):
                        pe.wait_ge(s_xn, t + 1)
                        mm = pe.transpose(t_ps[:, g % 2, (MT * i + t) * P:(MT * i + t + 1) * P],
                                          m_in[:, t, (2 * g + i) * P:(2 * g + i + 1) * P], ident[:, :])
                        if g == 0 and i == 0 and t == 0:
                            mm.then_inc(s_pv, AR)
                mm.then_inc(s_xt, 1)
            for c in range(KC):
                pe_turn(pe, 4 + c, x_in, 0, c, MT + 4)
            pe.wait_ge(s_xl, 4)
            for k in range(MW):
                pe.wait_ge(s_wl, k + 1)
                for i, (a, w) in enumerate(((m_hh, w_h), (m_hh, w_l), (m_hl, w_h))):
                    for m in range(MT):
                        mm = pe.matmul(j_ps[:, m], a[:, k, m * P:(m + 1) * P], w[:, k % 2].rearrange(flat),
                                       start=(k == 0 and i == 0), stop=(k == KC - 1 and i == 2))
                mm.then_inc(s_pj, 1)
            for c in range(KC):
                pe_turn(pe, 4 + KC + c, x_in, 4, c, MT + NT)
            pe.wait_ge(s_mk, 3 + MT * 2 * XP)
            pe.wait_ge(s_xl, XU0 - 2)
            for x_ in range(XP):
                for m in range(MT):
                    mm = pe.transpose(t_ps[:, (XU0 - 1) % 2, (MT * x_ + m) * P:(MT * x_ + m + 1) * P],
                                      mk_raw[:, m, x_ * P:(x_ + 1) * P], ident[:, :])
            mm.then_inc(s_xt, 1)
            pe.wait_ge(s_mv, MT)
            pe.wait_ge(s_mka, 2 * MT)
            pe.wait_ge(s_xl, XU0)
            for b in range(XP):
                if b:
                    pe.wait_ge(s_sq, 2)
                for piece in range(4):
                    pe_project_in(pe, MW + 2 * b, piece)
            pe.wait_ge(s_sq, 2 * XP)
            for c in range(CU):
                x_, t = c // NT, c % NT
                mm = pe.matmul(o_ps[:, 2 * c:2 * c + 2], xq_sq[:, x_, t * P:(t + 1) * P], half_ones[:, :],
                               start=True, stop=True)
            mm.then_inc(s_qs, 1)
            pe_cross_scores(pe, 0)
            pe_piece(pe, 0, 0, first=True)
            pe_cross_scores(pe, 1)
            pe.wait_ge(s_qr, 1)
            for c in range(CU):
                pe_cross_turn(pe, c)
                if c + 2 < CU:
                    pe_cross_scores(pe, c + 2)
                if c in X_PIECES:
                    pe_piece(pe, 0, X_PIECES[c], first=True)
                if c % 2:
                    pe_cross_values(pe, c // 2)
            pe_scores(pe, 0, 0, 0, first=True)
            pe.wait_ge(s_ctl, CU)
            for half in range(2):
                pe.wait_ge(s_eh, 4 + half + 1)
                for j in range(4):
                    col = (4 * half + j) * P
                    mm = pe.transpose(t_ps[:, half, j * P:(j + 1) * P], v_t[1][:, col:col + P], ident[:, :])
                mm.then_inc(s_t, 1)
            pe_scores(pe, 0, 1, 0, first=True)
            pe.wait_ge(s_co, CU)
            with pe.Fori(0, LOOPS) as m:
                for par in range(2):
                    pe_step(pe, 2 * m + par, par)
            pe_step(pe, PAIRS - 2, 0)
            pe_step(pe, PAIRS - 1, 1, last=True)
            for i in range(NU - FILL_AT, 2 * NT):
                pe_project(pe, i)
            pe.wait_ge(s_tl, T1)
            for t in range(NT):
                pe_project(pe, 2 * NT + t, TURN_AT[t])
            pe_gate_up(pe, 0, 0, 0)
            pe_gate_up(pe, 0, 0, 1, turns=True)
            pe_gate_up(pe, 0, 1, 0)
            pe_gate_up(pe, 0, 1, 1)
            with pe.Fori(0, FLOOPS) as m:
                for par in range(2):
                    pe_ffn(pe, 2 * m + par, par)
            pe_ffn(pe, FC - 3, 0)
            pe_ffn(pe, FC - 2, 1)
            pe_ffn(pe, FC - 1, 0, nxt=False)


INPUTS = ["x", "mem", "attn_norm", "mem_norm", "w_mem_kv", "xq_norm", "xk_norm", "w_out", "ffn_norm",
          "w_gate", "w_up", "w_down", "sb_w_in"]


def kernel(**inputs):
    import numpy as np
    import concourse.bacc as bacc
    from concourse.bass_utils import run_bass_kernel_spmd

    nc = bacc.Bacc("TRN2", target_bir_lowering=False, num_devices=1)
    arrays, args = {}, []
    for name in INPUTS:
        a = np.ascontiguousarray(inputs[name])
        arrays[f"in_{name}"] = a
        args.append(nc.dram_tensor(f"in_{name}", a.shape, mybir.dt.from_np(a.dtype), kind="ExternalInput").ap())
    args.append(nc.dram_tensor("out", inputs["x"].shape, F32, kind="ExternalOutput").ap())
    trunk(nc, *args)
    return run_bass_kernel_spmd(nc, [arrays], core_ids=[0]).results[0]["out"]
```

```python
from contextlib import ExitStack

import concourse.bass as bass
from concourse import mybir

ALU = mybir.AluOpType
ACT = mybir.ActivationFunctionType
AX = mybir.AxisListType
F32 = mybir.dt.float32
F32R = mybir.dt.float32r
BF16 = mybir.dt.bfloat16

P = 128
BANK = 512
HD = 64
EPS = 1e-6
QSCALE = HD ** -0.5


def trunk(nc, x, mem, attn_norm, mem_norm, w_mem_kv, xq_norm, xk_norm, w_out, ffn_norm, w_gate, w_up, w_down,
          sb_w_in, out):
    _, S, D = x.shape
    NT = S // P
    KC = D // P
    NH = S // BANK
    PAIRS = D // (2 * HD)
    M = mem.shape[1]
    MT = M // P
    XW = w_mem_kv.shape[2] // 2
    XP = XW // (2 * HD)
    OC = PAIRS + XP
    FF = w_gate.shape[2]
    FB = 2
    FC = FF // (FB * P)
    assert (NT, KC, NH, PAIRS, MT, XP) == (8, 8, 2, 8, 2, 2) and FC * FB * P == FF and FC % 2 == 1

    UNITS = []
    for g in range(NT // 2):
        for c in range((2 * g + 1) * P // BANK, -1, -1):
            for i in (2 * g, 2 * g + 1):
                n = (i + 1) * P
                UNITS.append((i, c * BANK, min(n - c * BANK, BANK), n - c * BANK <= BANK))
    NU = len(UNITS)
    USES = 2 * NU
    TUSE = USES + 2
    GROUP_END = [u for u in range(1, NU, 2) if UNITS[u][1] == 0]
    MW = KC
    W0 = MW + 2 * XP
    CONV_AT = (2, 4, 6, 8, 9, 11)
    PIECES = ((0,), (1,), (2,), (3,), (4,), (5,), (6,), (7,), (8, 9), (10,), (11,), ())
    DOUBLE_AT = 9
    EVAC_AT = {4: 0, 8: 1, 11: 2}
    ZR, FR, GR, AR = 3, 4, 4, 2
    assert USES % ZR == 0 and USES % FR == 0 and USES % GR == 0 and NU % AR == 0 and TUSE % 2 == 0

    with ExitStack() as ctx:
        cursor = [-(-nc.sbuf_base // 32) * 32]

        def at(name, shape, dt, off):
            return nc.alloc_sbuf_tensor_at(name, shape, dt, offset=off)

        def size(shape):
            n = 4
            for s in shape[1:]:
                n *= s
            return -(-n // 32) * 32

        def take(name, shape, dt=F32, columns=None):
            t = at(name, [shape[0], columns] if columns else shape, dt, cursor[0])
            cursor[0] += size(shape)
            return t

        def sem(name):
            return ctx.enter_context(nc.semaphore(name))

        ident = take("ident", [P, P])
        own = take("own", [P, BANK // 2 + 1], BF16, BANK + 2)
        eps_col = take("eps_col", [P, 1])
        gains = take("gains", [P, 3, KC])
        g_cross = take("g_cross", [P, 2])
        g_qk = take("g_qk", [P, 1])
        half_ones = take("half_ones", [P, 2])
        NS = MT + 2 * NT
        ssq = take("ssq", [P, NS])
        rms = take("rms", [P, NS])
        rstd = take("rstd", [P, NS])
        mk_at = cursor[0]
        mk_h = take("mk_h", [P, XP, M], F32R)
        mk_l = take("mk_l", [P, XP, M], F32R)
        mv = take("mv", [P, MT, XP, 4, HD], F32R)
        h_at = cursor[0]
        hh = take("hh", [P, KC, S], F32R)
        hl = take("hl", [P, KC, S], F32R)
        o_at = cursor[0]
        o_t = take("o_t", [P, PAIRS * S])
        qk_at = cursor[0]
        q_h, q_l, k_h, k_l = [], [], [], []
        for b in range(2):
            for name, to in (("q_h", q_h), ("q_l", q_l), ("k_h", k_h), ("k_l", k_l)):
                to.append(take(f"{name}{b}", [P, S], F32R))
        q_a, q_b, k_a, k_b = q_h, q_l, k_h, []
        v_s = [None, None]
        v_s[1] = take("v_s1", [P, NT, 4, HD], F32R)
        v0_at = cursor[0]
        v_s[0] = take("v_s0", [P, NT, 4, HD], F32R)
        raw_at = cursor[0]
        w_raw = take("w_raw", [P, 2, 4, P])
        w_h = take("w_h", [P, 2, 4, P], F32R)
        wl_at = cursor[0]
        w_l = take("w_l", [P, 2, 4, P], F32R)
        fail_at = cursor[0]
        fail = take("fail", [P, FR, BANK + 4])
        x_at = cursor[0]
        succ = take("succ", [P, GR, BANK])
        a_h = take("a_h", [P, AR, 4, 2 * P], F32R)
        a_l = take("a_l", [P, AR, 4, 2 * P], F32R)
        k_b += [take(f"k_b{b}", [P, S], F32R) for b in range(2)]
        pv_low = take("pv_low", [P, 2 * P])
        assert cursor[0] <= nc.sbuf_usable_end
        KB = 1024
        ROW = 4 * S

        v_t = [at(f"v_t{b}", [P, S], F32, qk_at + (4 * b + 1) * ROW) for b in range(2)]
        x_in = at("x_in", [P, NT, D], F32, x_at)
        m_in = at("m_in", [P, MT, D], F32, qk_at)
        m_hh = at("m_hh", [P, KC, M], F32R, qk_at + 2 * ROW)
        m_hl = at("m_hl", [P, KC, M], F32R, qk_at + 4 * ROW)
        mw_raw = at("mw_raw", [P, KC, BANK], F32, o_at)
        mw_h = at("mw_h", [P, KC, BANK], F32R, o_at + 4 * ROW)
        mw_l = at("mw_l", [P, 4, BANK], F32R, v0_at - 2 * ROW)
        k_stat = at("k_stat", [P, 3, MT * 2 * XP], F32, v0_at - 2 * ROW)
        q_stat = at("q_stat", [P, 4, NT * 2 * XP], F32, v0_at - 2 * ROW + 512)
        x_stat = at("x_stat", [P, 4, NT * 2 * XP], F32, v0_at - 2 * ROW + 1024)
        mk_raw = at("mk_raw", [P, MT, XW], F32, o_at)
        mk_sq = at("mk_sq", [P, MT, XW], F32, o_at + ROW)
        junk = at("junk", [P, D], F32, v0_at)
        xq_sq = at("xq_sq", [P, XP, S], F32, v0_at)
        om_t = at("om_t", [P, 2 * S], F32, mk_at)
        wo_h = at("wo_h", [P, OC, BANK], F32R, h_at)
        wo_l = at("wo_l", [P, OC, BANK], F32R, h_at + OC * BANK * 4)
        wo_raw = at("wo_raw", [P, 4, BANK], F32, raw_at)
        rest = h_at + 2 * OC * BANK * 4
        hi_at = ([rest + k * ROW for k in range(6)] + [qk_at + (4 + 2 * k) * ROW for k in range(3)]
                 + [x_at + 32 * KB - 2 * ROW])
        lo_at = ([qk_at + k * ROW for k in range(4)] + [v0_at, v0_at + ROW]
                 + [qk_at + (5 + 2 * k) * ROW for k in range(3)] + [x_at + 32 * KB - ROW])
        o_h = [at(f"o_h{k}", [P, S], F32R, hi_at[k]) for k in range(OC)]
        o_l = [at(f"o_l{k}", [P, S], F32R, lo_at[k]) for k in range(OC)]
        x2 = at("x2", [P, NT, D], F32, fail_at)
        part = at("part", [P, NT, BANK], F32, o_at)
        xn = [at(f"xn{t}", [P, D], F32, (mk_at, mk_at + ROW, raw_at, raw_at + ROW)[t]) for t in range(4)]
        f_h = [at("f_h0", [P, KC, BANK], F32R, o_at), at("f_h1", [P, KC, BANK], F32R, h_at)]
        f_l = [at("f_l0", [P, KC, BANK], F32R, o_at + 16 * KB), at("f_l1", [P, KC, BANK], F32R, h_at + 16 * KB)]
        f_raw = at("f_raw", [P, 2, BANK], F32, wl_at)
        f_raw2 = at("f_raw2", [P, 2, BANK], F32, qk_at + 4 * ROW)
        gw_h = at("gw_h", [P, FB, 2, KC, P], F32R, h_at + 32 * KB)
        gw_l = at("gw_l", [P, FB, 2, KC, P], F32R, h_at + 48 * KB)
        dw_h = [at("dw_h0", [P, FB, D], F32R, qk_at), at("dw_h1", [P, FB, D], F32R, v0_at)]
        dw_l = [at("dw_l0", [P, FB, D], F32R, qk_at + 2 * ROW), at("dw_l1", [P, FB, D], F32R, v0_at + 2 * ROW)]
        gu_h = [at("gu_h0", [P, FB, S], F32R, qk_at + 4 * ROW), at("gu_h1", [P, FB, S], F32R, qk_at + 8 * ROW)]
        gu_l = [at("gu_l0", [P, FB, S], F32R, qk_at + 6 * ROW), at("gu_l1", [P, FB, S], F32R, mk_at)]
        sig = at("sig", [P, 2, BANK], F32, x_at + 32 * KB - 2 * ROW)
        prod = at("prod", [P, 2, BANK], F32, x_at + 32 * KB - ROW)

        ps = ctx.enter_context(nc.psum_tensor("ps", [P, 8, BANK], F32))
        t_ps, j_ps, z_ps, o_ps = ps[:, 0:2], ps[:, 2:4], ps[:, 4:7], ps[:, 7]

        s_x = [sem(f"x{t}_loaded") for t in range(NT)]
        s_g = sem("gains_loaded")
        s_id = sem("constants_made")
        s_ssq = sem("squares_summed")
        s_rms = sem("root_taken")
        s_rstd = sem("root_inverted")
        s_xn = sem("x_scaled")
        s_xt = sem("x_transposed")
        s_xh = sem("x_high_done")
        s_xl = sem("x_low_done")
        s_w = [sem("w_even_loaded"), sem("w_odd_loaded")]
        s_wh = sem("w_high_done")
        s_wl = sem("w_low_done")
        s_pj = sem("w_used")
        s_eh = sem("qkv_high_done")
        s_el = sem("qk_low_done")
        s_kd = sem("k_high_doubled")
        s_z = sem("scores_ready")
        s_fg = sem("fail_succ_ready")
        s_scan = sem("stick_scanned")
        s_a = sem("weights_ready")
        s_t = sem("weights_transposed")
        s_th = sem("transposed_high_done")
        s_tl = sem("transposed_low_done")
        s_pv = sem("values_summed")
        s_pl = sem("low_part_copied")
        s_o = sem("heads_written")
        s_out = sem("out_stored")

        xd = x.rearrange("b (t p) d -> p (b t) d", p=P)
        wd = sb_w_in.rearrange("l (c p) n -> p (l c) n", p=P)

        def load_half(sp, n, column, k):
            if not (isinstance(n, int) and n < MW + 2):
                sp.wait_ge(s_wl, n - 1)
            sp.dma_start(w_raw[:, k % 2], wd[:, 4 * (k % 2):4 * (k % 2) + 4, bass.ds(column, P)]
                         ).then_inc(s_w[k % 2], 16)

        def load_w(sp, s, k):
            load_half(sp, W0 + 6 * s + k, (k // 2) * D + s * P, k)

        def pe_first_half(pe, half):
            pe.wait_ge(s_xl, 4 + KC * (half + 1))
            for kc in range(KC):
                if kc % 4 == 0:
                    pe.wait_ge(s_wl, MW + kc // 4 + 1)
                for i, (w, h) in enumerate(((w_h, hh), (w_h, hl), (w_l, hh))):
                    mm = pe.matmul(j_ps[:, half], w[:, kc // 4, kc % 4], h[:, kc, half * BANK:(half + 1) * BANK],
                                   start=(kc == 0 and i == 0), stop=(kc == KC - 1 and i == 2))
                if half and kc % 4 == 3:
                    mm.then_inc(s_pj, 1)

        def pe_project_in(pe, n, piece, out=j_ps, only=None, left=None):
            hf, q = (piece % 4) // 2, piece % 2
            if q == 0 and only != 1:
                pe.wait_ge(s_wl, n + hf + 1)
            for c in (2 * q, 2 * q + 1) if only is None else (2 * q + only,):
                kc = 4 * hf + c
                parts = [(i, half) for i in range(3) for half in range(2)]
                if kc == 0:
                    parts.sort(key=lambda p: p[1])
                for i, half in parts:
                    if kc == 0 and i == 0 and left:
                        left(half)
                    w, h = ((w_h, hh), (w_h, hl), (w_l, hh))[i]
                    mm = pe.matmul(out[:, half], w[:, hf, c], h[:, kc, half * BANK:(half + 1) * BANK],
                                   start=(kc == 0 and i == 0), stop=(kc == KC - 1 and i == 2))
            if q == 1 and only != 0:
                mm.then_inc(s_pj, 1)

        def pe_piece(pe, s, piece, first=False, only=None):
            b = piece // 4

            def left(half):
                if first and b == 0:
                    pe.wait_ge(s_sq, 1 + half)
                else:
                    pe.wait_ge(s_eh, 6 * s + 2 * b - 1 + half)
                    if b:
                        pe.wait_ge(s_el, 4 * s + 2 * b - 1 + half)
            pe_project_in(pe, W0 + 6 * s + 2 * b, piece, only=only, left=left)

        def pe_v(pe, s, par, tbase):
            for half in range(2):
                pe.wait_ge(s_eh, 6 * s + 4 + half + 1)
                pe.wait_ge(s_tl, tbase + half - 1)
                for j in range(4):
                    col = (4 * half + j) * P
                    mm = pe.transpose(t_ps[:, half, j * P:(j + 1) * P], v_t[1 - par][:, col:col + P], ident[:, :])
                mm.then_inc(s_t, 1)

        def pe_scores(pe, s, u, par, first=False):
            i, k0, w, diag = UNITS[u]
            if u == 0:
                pe.wait_ge(s_el, 4 * s + 4)
                pe.wait_ge(s_kd, s + 1)
            for h in range(2):
                n = 2 * u + h
                if first and n < ZR:
                    pe.wait_ge(s_ce, 2 * CU)
                else:
                    pe.wait_ge(s_fg, 2 * (USES * s + n - ZR) + 2)
            for t in range(2):
                for h in range(2):
                    n = 2 * u + h
                    r = slice(HD * h, HD * h + HD) if t else slice(0, P)
                    kk = k_l if t else (k_a, k_b)[h]
                    mm = pe.matmul(z_ps[:, n % ZR, 0:w], (q_a, q_b)[h][par][r, i * P:(i + 1) * P],
                                   kk[par][r, k0:k0 + w], start=(t == 0), stop=(t == 1))
                    if t:
                        mm.then_inc(s_z, 1)

        def pe_transposes(pe, s, u, h):
            n = 2 * u + h
            _, _, w, _ = UNITS[u]
            pe.wait_ge(s_a, USES * s + n + 1)
            pe.wait_ge(s_tl, 2 + TUSE * s + n - 1)
            for j in range(w // P):
                mm = pe.transpose(t_ps[:, n % 2, j * P:(j + 1) * P], succ[:, n % GR, j * P:(j + 1) * P], ident[:, :])
            mm.then_inc(s_t, 1)

        def pe_values(pe, s, u, par):
            i, k0, w, _ = UNITS[u]
            w_first = UNITS[u - 1][2]
            opens = UNITS[u][3]
            up = u // 2
            for h in range(2):
                slot = (2 * up + h) % AR
                pe.wait_ge(s_tl, 2 + TUSE * s + 2 * u + h + 1)
                if opens and h == 0:
                    g = (i - 1) // 2
                    pe.wait_ge(s_o, 8 * s + 2 * g + 1)
                if up == 0 and h == 0:
                    pe.wait_ge(s_tl, 2 + TUSE * s)
                for j in range(w // P):
                    q0 = 0 if j * P < w_first else P
                    for t, a in enumerate((a_h, a_l)):
                        mm = pe.matmul(o_ps[:, h * 2 * P + q0:(h + 1) * 2 * P],
                                       v_s[par][:, k0 // P + j, 2 * h:2 * h + 2, :].rearrange("p a d -> p (a d)"),
                                       a[:, slot, j, q0:2 * P],
                                       start=(opens and h == 0 and j == 0 and t == 0), stop=False,
                                       skip_group_check=True)
                mm.then_inc(s_pv, 1)

        def pe_step(pe, s, par, last=False):
            for u in range(NU):
                pe_transposes(pe, s, u, 0)
                pe_transposes(pe, s, u, 1)
                if u + 2 < NU:
                    pe_scores(pe, s, u + 2, par)
                elif not last:
                    pe_scores(pe, s + 1, u + 2 - NU, 1 - par)
                if last:
                    if u >= FILL_AT:
                        pe_project(pe, u - FILL_AT)
                else:
                    for piece in PIECES[u]:
                        pe_piece(pe, s + 1, piece)
                    if u == NU - 1:
                        pe_v(pe, s + 1, 1 - par, 2 + TUSE * s + USES)
                if u % 2:
                    pe_values(pe, s, u, par)

        def act_w(act, s, k):
            act_w_high(act, W0 + 6 * s + k, XP + 3 * s + k // 2, k)

        def act_w_high(act, n, loads, k):
            act.wait_ge(s_w[k % 2], 16 * (loads + 1))
            if not (isinstance(loads, int) and loads == 0):
                act.wait_ge(s_pj, n - 1)
            act.activation(w_h[:, k % 2], w_raw[:, k % 2], ACT.Copy).then_inc(s_wh, 1)

        def act_evac(act, s, b, par):
            act.wait_ge(s_pj, W0 + 6 * s + 2 * b + 2)
            for half in range(2):
                c = slice(half * BANK, (half + 1) * BANK)
                if b == 2:
                    done = act.activation(v_t[1 - par][:, c], j_ps[:, half], ACT.Copy)
                else:
                    for h in range(2):
                        r = slice(HD * h, HD * h + HD)
                        dst = ((q_a, q_b), (k_a, k_b))[b][h][par]
                        done = act.activation(dst[r, c], j_ps[r, half], ACT.Copy)
                done.then_inc(s_eh, 1)

        def act_v(act, par, tcount):
            for half in range(2):
                act.wait_ge(s_t, tcount + half + 1)
                src = t_ps[:, half].rearrange("p (j h d) -> p j h d", j=4, h=2)
                act.activation(v_s[par][:, 4 * half:4 * half + 4, 0:4:3, :], src, ACT.Copy).then_inc(s_th, 1)

        def act_fail_succ(act, s, u, h, first=False):
            n = 2 * u + h
            w = UNITS[u][2]
            act.wait_ge(s_z, USES * s + n + 1)
            if not (first and n < FR):
                act.wait_ge(s_a, USES * s + n - FR + 1)
            act.activation(fail[:, n % FR, 0:w], z_ps[:, n % ZR, 0:w], ACT.Sigmoid, scale=-QSCALE).then_inc(s_fg, 1)
            if not (first and n < GR):
                act.wait_ge(s_t, 2 + TUSE * s + n - GR + 1 - (0 if u >= 2 else 2))
            act.activation(succ[:, n % GR, 0:w], z_ps[:, n % ZR, 0:w], ACT.Sigmoid, scale=QSCALE).then_inc(s_fg, 1)

        def act_high(act, s, u, h):
            n = 2 * u + h
            w = UNITS[u][2]
            up, col = u // 2, u % 2
            act.wait_ge(s_t, 2 + TUSE * s + n + 1)
            if col == 0:
                act.wait_ge(s_pv, NU * s + 2 * up + h + 1)
            act.activation(a_h[:, (2 * up + h) % AR, 0:w // P, col * P:(col + 1) * P],
                           t_ps[:, n % 2, 0:w].rearrange("p (j q) -> p j q", q=P), ACT.Copy).then_inc(s_th, 1)

        def act_low_rows(act, s, u):
            g = UNITS[u][0] // 2
            act.wait_ge(s_pv, AR + NU * s + u + 1)
            act.wait_ge(s_o, 8 * s + 2 * g + 1)
            act.activation(pv_low[0:HD, :], o_ps[HD:P, 0:2 * P], ACT.Copy).then_inc(s_pl, 1)
            act.activation(pv_low[HD:P, :], o_ps[0:HD, 2 * P:4 * P], ACT.Copy).then_inc(s_pl, 1)

        def act_step(act, s, par, last=False):
            side = iter(SPLITS) if last else None
            for u in range(NU):
                if u in EVAC_AT and not last:
                    act_evac(act, s + 1, EVAC_AT[u], 1 - par)
                act_high(act, s, u, 0)
                if u + 2 < NU:
                    act_fail_succ(act, s, u + 2, 0)
                elif not last:
                    act_fail_succ(act, s + 1, u + 2 - NU, 0)
                if last:
                    for _ in range(SPLIT_RATE[u] // 2):
                        act_split(act, next(side))
                act_high(act, s, u, 1)
                if u - 1 in GROUP_END:
                    act_low_rows(act, s, u - 1)
                if u + 2 < NU:
                    act_fail_succ(act, s, u + 2, 1)
                elif not last:
                    act_fail_succ(act, s + 1, u + 2 - NU, 1)
                if last:
                    for _ in range(SPLIT_RATE[u] - SPLIT_RATE[u] // 2):
                        act_split(act, next(side))
                if u in CONV_AT and not last:
                    k = CONV_AT.index(u)
                    if k < 4 or not (isinstance(s, int) and s == PAIRS - 2):
                        act_w(act, s + 1 + (k + 2) // 6, (k + 2) % 6)
                if u == NU - 1 and not last:
                    act_v(act, 1 - par, 2 + TUSE * s + USES)
            act_low_rows(act, s, NU - 1)

        def dve_w(dve, s, k):
            dve_w_low(dve, W0 + 6 * s + k, k)

        def dve_w_low(dve, n, k):
            dve.wait_ge(s_wh, n + 1)
            dve.tensor_tensor(w_l[:, k % 2], w_raw[:, k % 2], w_h[:, k % 2].bitcast(F32), ALU.subtract
                              ).then_inc(s_wl, 1)

        def dve_evac(dve, s, b, par):
            for half in range(2):
                c = slice(half * BANK, (half + 1) * BANK)
                dve.wait_ge(s_eh, 6 * s + 2 * b + half + 1)
                for h in range(2):
                    r, other = slice(HD * h, HD * h + HD), slice(HD - HD * h, P - HD * h)
                    high = ((q_a, q_b), (k_a, k_b))[b][h][par]
                    low = k_l[par][r, c] if b else high[other, c]
                    done = dve.tensor_tensor(low, j_ps[r, half], high[r, c].bitcast(F32), ALU.subtract)
                done.then_inc(s_el, 1)

        def dve_double(dve, s, par):
            for h in range(2):
                r, other = slice(HD * h, HD * h + HD), slice(HD - HD * h, P - HD * h)
                done = dve.tensor_copy((k_a, k_b)[h][par][other, :], (k_a, k_b)[h][par][r, :].bitcast(F32))
            done.then_inc(s_kd, 1)

        def dve_v(dve, par, tcount):
            for half in range(2):
                dve.wait_ge(s_th, tcount + half + 1)
                j = slice(4 * half, 4 * half + 4)
                dve.tensor_tensor(v_s[par][:, j, 1:3, :],
                                  t_ps[:, half].rearrange("p (j h d) -> p j h d", j=4, h=2),
                                  v_s[par][:, j, 0:4:3, :].bitcast(F32), ALU.subtract).then_inc(s_tl, 1)

        def dve_scan(dve, s, u, h):
            n = 2 * u + h
            _, k0, w, diag = UNITS[u]
            f = fail[:, n % FR]
            dve.wait_ge(s_fg, 2 * (USES * s + n) + 2)
            if diag:
                back = f[:, 0:w + 1][:, ::-1]
                dve.tensor_tensor_scan(back, back, own[:, BANK - w:BANK + 1][:, ::-1], 0.0, ALU.mult, ALU.max
                                       ).then_inc(s_scan, 1)
            else:
                dve.wait_ge(s_a, USES * s + n - FR + 1)
                back = f[:, 0:w][:, ::-1]
                dve.tensor_tensor_scan(back, back, back, f[:, BANK:BANK + 1], ALU.mult, ALU.bypass
                                       ).then_inc(s_scan, 1)

        def dve_weights(dve, s, u, h):
            n = 2 * u + h
            _, k0, w, _ = UNITS[u]
            f, g = fail[:, n % FR], succ[:, n % GR, 0:w]
            dve.wait_ge(s_scan, USES * s + n + 1)
            done = dve.tensor_tensor(g, f[:, 1:w + 1], g, ALU.mult)
            if k0:
                if w == BANK:
                    done.then_inc(s_last, 1)
                    dve.wait_ge(s_last, 2 * s + h + 1)
                done = dve.tensor_copy(f[:, BANK:BANK + 1], f[:, 0:1])
            done.then_inc(s_a, 1)

        def dve_low(dve, s, u, h):
            n = 2 * u + h
            w = UNITS[u][2]
            up, col = u // 2, u % 2
            dve.wait_ge(s_th, 2 + TUSE * s + n + 1)
            slot = (2 * up + h) % AR
            c = slice(col * P, (col + 1) * P)
            dve.tensor_tensor(a_l[:, slot, 0:w // P, c], t_ps[:, n % 2, 0:w].rearrange("p (j q) -> p j q", q=P),
                              a_h[:, slot, 0:w // P, c].bitcast(F32), ALU.subtract).then_inc(s_tl, 1)

        def dve_heads(dve, s, u):
            g = UNITS[u][0] // 2
            dve.wait_ge(s_pl, 8 * s + 2 * g + 2)
            for h in range(2):
                r = slice(HD * h, HD * h + HD)
                if isinstance(s, int) and s >= PAIRS - 2:
                    dst = om_t[r, (s - PAIRS + 2) * S + g * 2 * P:(s - PAIRS + 2) * S + (g + 1) * 2 * P]
                else:
                    dst = o_t[r, bass.ds(s * S + g * 2 * P, 2 * P)]
                dve.tensor_tensor(dst, o_ps[r, h * 2 * P:(h + 1) * 2 * P],
                                  pv_low[r, :], ALU.add).then_inc(s_o, 1)

        def dve_step(dve, s, par, last=False):
            side = iter([i for i in SPLITS if LOW[i][0] == 1])
            for u in range(NU):
                nxt = (s, u + 1) if u + 1 < NU else (s + 1, 0) if not last else None
                if u in EVAC_AT and EVAC_AT[u] < 2 and not last:
                    dve_evac(dve, s + 1, EVAC_AT[u], 1 - par)
                for h in range(2):
                    if nxt:
                        dve_scan(dve, *nxt, h)
                    dve_low(dve, s, u, h)
                    if nxt:
                        dve_weights(dve, *nxt, h)
                if u - 1 in GROUP_END:
                    dve_heads(dve, s, u - 1)
                if u == DOUBLE_AT and not last:
                    dve_double(dve, s + 1, 1 - par)
                if last:
                    for _ in range(DVE_RATE[u]):
                        split_low(dve, next(side))
                    if u > FILL_AT:
                        dve_add(dve, u - 1 - FILL_AT)
                if u in CONV_AT and not last:
                    k = CONV_AT.index(u)
                    if k < 4 or not (isinstance(s, int) and s == PAIRS - 2):
                        dve_w(dve, s + 1 + (k + 2) // 6, (k + 2) % 6)
                if u == NU - 1 and not last:
                    dve_v(dve, 1 - par, 2 + TUSE * s + USES)
            dve_heads(dve, s, NU - 1)

        s_last = sem("last_tile_weights_done")
        s_m = [sem(f"mem{t}_loaded") for t in range(MT)]
        s_mw = [sem(f"mem_w{k}_loaded") for k in range(KC // 2)]
        s_mk = sem("mem_keys_done")
        s_mka = sem("mem_keys_copied")
        s_mv = sem("mem_values_low_done")
        s_gq = sem("cross_gains_multiplied")
        s_sq = sem("cross_q_squared")
        s_qs = sem("cross_q_squares_summed")
        s_qr = sem("cross_q_roots")
        s_qi = sem("cross_q_scales")
        s_cs = sem("cross_scores_ready")
        s_cm = sem("cross_max_taken")
        s_cb = sem("cross_bias_ready")
        s_ce = sem("cross_exp_done")
        s_cr = sem("cross_sum_inverted")
        s_cp = sem("cross_weights_ready")
        s_cv = sem("cross_values_summed")
        s_cl = sem("cross_low_copied")
        s_co = sem("cross_heads_written")
        s_wo = [sem(f"w_out_slot{k}_loaded") for k in range(4)]
        s_qh = sem("cross_q_high_done")
        s_ql = sem("cross_q_low_done")
        s_ct = sem("cross_weights_transposed")
        s_cth = sem("cross_transposed_high_done")
        s_ctl = sem("cross_transposed_low_done")
        s_sh = sem("split_high_done")
        s_sl = [sem("split_low_done_by_gpsimd"), sem("split_low_done_by_vector")]
        s_op = sem("projection_ready")
        s_x2l = [[sem(f"residual{t}_{side}_loaded") for t in range(NT)] for side in ("left", "right")]
        s_x2 = sem("residual_added")
        s_fw = [sem("ffn_w_even_loaded"), sem("ffn_w_odd_loaded")]
        s_fx = [sem("ffn_w_extra_even_loaded"), sem("ffn_w_extra_odd_loaded")]
        s_fh = sem("ffn_w_high_done")
        s_fl = sem("ffn_w_low_done")
        s_gp = sem("gate_up_ready")
        s_sg = sem("sigmoid_done")
        s_t1 = sem("silu_done")
        s_pr = sem("product_done")
        s_gh = sem("product_high_done")
        s_gl = sem("product_low_done")
        s_dn = sem("down_ready")

        memd = mem.rearrange("b (t p) d -> p (b t) d", p=P)
        mwd = w_mem_kv.rearrange("l (c p) n -> p (l c) n", p=P)
        wod = w_out.rearrange("l (c p) n -> p (l c) n", p=P)
        gud = [w.rearrange("l (c p) n -> p (l c) n", p=P) for w in (w_gate, w_up)]
        dnd = w_down.rearrange("l (f p) n -> p (l f) n", p=P)
        outd = out.rearrange("b (t p) d -> p (b t) d", p=P)
        flat = "p c n -> p (c n)"

        XU0 = 4 + 2 * KC + 1
        T1 = TUSE * PAIRS
        W1 = W0 + 6 * PAIRS
        CU = XP * NT
        LAST_ORDER = (6, 7, 8, 9, 2, 3, 0, 1, 4, 5)
        EARLY = 6
        SPLITS = [i for k in range(EARLY) for i in (("w", k, 0), ("o", k, 0))]
        SPLITS += [("o", k, 1) for k in range(EARLY)] + [("w", k, 0) for k in range(EARLY, OC)]
        LATER = [("o", k, half) for half in range(2) for k in (8, 9, 6, 7)]
        SECOND = [("w", k, 1) for k in range(OC)]
        HIGH = {i: n + 1 for n, i in enumerate(SPLITS + LATER + SECOND)}
        LOW, made = {}, [0, 0]
        for i in SPLITS + LATER + SECOND:
            e = 0 if i in SPLITS and (i[0] == "w" or i[2] == 1) else 1
            made[e] += 1
            LOW[i] = (e, made[e])
        SPLIT_RATE = (4, 4, 4, 2, 2, 2, 2, 2, 0, 0, 0, 0)
        DVE_RATE = (1, 2, 2, 1, 0, 0, 0, 0, 0, 0, 0, 0)
        FILL_AT = 5
        X_COUNT = (1, 1, 1, 1, 1, 1, 1, 1, 0, 1, 1, 1, 1, 2, 2, 0)
        X_CONV = {1: 3, 4: 4, 8: 5, 13: 6, 15: 7}
        X_EVAC = {0: 0, 8: 1, 15: 2}
        CQ = HD ** -0.5
        WARM = 4

        def act_root(act, k, src, dst):
            if k:
                act.wait_ge(s_ssq, k)
            act.activation(dst, src, ACT.Square, accum_out=ssq[:, k:k + 1]).then_inc(s_ssq, 1)
            act.wait_ge(s_ssq, k + 1)
            act.activation(rms[:, k:k + 1], ssq[:, k:k + 1], ACT.Sqrt, bias=eps_col[:, :], scale=1.0 / D
                           ).then_inc(s_rms, 1)

        def dve_scale(dve, k, src, dst):
            dve.wait_ge(s_rms, k + 1)
            dve.reciprocal(rstd[:, k:k + 1], rms[:, k:k + 1]).then_inc(s_rstd, 1)
            dve.wait_ge(s_rstd, k + 1)
            dve.tensor_scalar(dst, src, rstd[:, k:k + 1], None, ALU.mult).then_inc(s_xn, 1)

        def turn_ps(g):
            return ps[:, (0, 1, 4, 5)[g % 4]] if g < XU0 else t_ps[:, g % 2]

        def wait_turn_bank(pe, g):
            if g >= XU0:
                pe.wait_ge(s_xl, g - 1)
            elif g >= 4:
                pe.wait_ge(s_xl, g - 3)

        def pe_turn(pe, g, src, rows, c, scaled):
            wait_turn_bank(pe, g)
            pe.wait_ge(s_xn, scaled)
            for t in range(4):
                rows_t = xn[t][:, c * P:(c + 1) * P] if src is None else src[:, rows + t, c * P:(c + 1) * P]
                mm = pe.transpose(turn_ps(g)[:, t * P:(t + 1) * P], rows_t, ident[:, :])
                if g == XU0 and t == 0:
                    mm.then_inc(s_dn, 1)
            mm.then_inc(s_xt, 1)

        def act_turned(act, g, dst, gain):
            act.wait_ge(s_xt, g + 1)
            act.activation(dst, turn_ps(g), ACT.Copy, scale=gain).then_inc(s_xh, 1)

        def dve_turned(dve, g, dst, high, gain):
            dve.wait_ge(s_xh, g + 1)
            dve.scalar_tensor_tensor(dst, turn_ps(g), gain, high.bitcast(F32), ALU.mult, ALU.subtract
                                     ).then_inc(s_xl, 1)

        def act_mem_w(act, k):
            act.wait_ge(s_mw[k // 2], 16)
            act.activation(mw_h[:, k], mw_raw[:, k], ACT.Copy).then_inc(s_wh, 1)

        def dve_mem_w(dve, k):
            dve.wait_ge(s_wh, k + 1)
            if k >= 4:
                dve.wait_ge(s_pj, k - 3)
            dve.tensor_tensor(mw_l[:, k % 4], mw_raw[:, k], mw_h[:, k].bitcast(F32), ALU.subtract).then_inc(s_wl, 1)

        def pe_mem(pe, k):
            pe.wait_ge(s_wl, k + 1)
            for i, (a, w) in enumerate(((m_hh, mw_h[:, k]), (m_hh, mw_l[:, k % 4]), (m_hl, mw_h[:, k]))):
                for m in range(MT):
                    mm = pe.matmul(ps[:, 6 + m], a[:, k, m * P:(m + 1) * P], w,
                                   start=(k == 0 and i == 0), stop=(k == KC - 1 and i == 2))
            mm.then_inc(s_pj, 1)

        def operand(i):
            what, k, half = i
            if what == "w":
                return wo_raw[:, (OC * half + k) % 4], wo_h[:, k], wo_l[:, k]
            c = slice(half * BANK, (half + 1) * BANK)
            if k in (PAIRS - 2, PAIRS - 1):
                src = om_t[:, (k - PAIRS + 2) * S + half * BANK:(k - PAIRS + 2) * S + (half + 1) * BANK]
            else:
                at_ = (k if k < PAIRS else k - 2) * S + half * BANK
                src = o_t[:, at_:at_ + BANK]
            return src, o_h[k][:, c], o_l[k][:, c]

        def act_split(act, i):
            what, k, half = i
            src, high, _ = operand(i)
            if i == SPLITS[0]:
                act.wait_ge(s_pj, W1)
            if i == LATER[0]:
                act.wait_ge(s_o, 8 * PAIRS + 1)
                act.wait_ge(s_pv, AR + NU * PAIRS)
            if what == "w":
                N = OC * half + k
                act.wait_ge(s_wo[N % 4], 16 * (N // 4 + 1))
                if half:
                    act.wait_ge(s_op, NT if k < EARLY else 2 * NT)
            act.activation(high, src, ACT.Copy).then_inc(s_sh, 1)

        def split_low(eng, i):
            src, high, low = operand(i)
            e, _ = LOW[i]
            eng.wait_ge(s_sh, HIGH[i])
            eng.tensor_tensor(low, src, high.bitcast(F32), ALU.subtract).then_inc(s_sl[e], 1)

        def wait_split(eng, i):
            e, n = LOW[i]
            eng.wait_ge(s_sl[e], n)

        xq_ps = [j_ps, ps[:, 4:6]]

        def act_cross_q(act, b):
            act.wait_ge(s_pj, MW + 2 * b + 2)
            for half in range(2):
                c = slice(half * BANK, (half + 1) * BANK)
                act.activation((q_h, k_h)[b][1][:, c], xq_ps[b][:, half], ACT.Copy).then_inc(s_qh, 1)
            for half in range(2):
                c = slice(half * BANK, (half + 1) * BANK)
                act.wait_ge(s_ql, 2 * b + half + 1)
                act.activation(xq_sq[:, b, c], xq_ps[b][:, half], ACT.Square).then_inc(s_sq, 1)

        def dve_cross_q(dve, b):
            for half in range(2):
                c = slice(half * BANK, (half + 1) * BANK)
                dve.wait_ge(s_qh, 2 * b + half + 1)
                dve.tensor_tensor((q_l, k_l)[b][1][:, c], xq_ps[b][:, half], (q_h, k_h)[b][1][:, c].bitcast(F32),
                                  ALU.subtract).then_inc(s_ql, 1)

        def pe_cross_scores(pe, c):
            x_, t = c // NT, c % NT
            qh, ql = (q_h[1], q_l[1]) if x_ == 0 else (k_h[1], k_l[1])
            for i, (q, kk) in enumerate(((qh, mk_h), (qh, mk_l), (ql, mk_h))):
                for h in range(2):
                    n = 2 * c + h
                    if i == 0 and n >= ZR:
                        pe.wait_ge(s_ce, n - ZR + 1)
                    r = slice(HD * h, HD * h + HD)
                    mm = pe.matmul(z_ps[:, n % ZR, 0:M], q[r, t * P:(t + 1) * P], kk[r, x_],
                                   start=(i == 0), stop=(i == 2))
                    if i == 2:
                        mm.then_inc(s_cs, 1)

        def dve_cross_max(dve, c):
            for h in range(2):
                n = 2 * c + h
                dve.wait_ge(s_cs, n + 1)
                dve.tensor_reduce(x_stat[:, 0, n:n + 1], z_ps[:, n % ZR, 0:M], AX.X, ALU.max).then_inc(s_cm, 1)
            dve.wait_ge(s_cm, 2 * c + 2)
            p = slice(2 * c, 2 * c + 2)
            dve.tensor_tensor(x_stat[:, 1, p], x_stat[:, 0, p], q_stat[:, 3, p], ALU.mult).then_inc(s_cb, 1)

        def act_cross_exp(act, c):
            act.wait_ge(s_cb, c + 1)
            if c >= GR:
                act.wait_ge(s_ct, c - GR + 1)
            for h in range(2):
                n = 2 * c + h
                act.activation(succ[:, c % GR, h * M:(h + 1) * M], z_ps[:, n % ZR, 0:M], ACT.Exp,
                               bias=x_stat[:, 1, n:n + 1], scale=q_stat[:, 2, n:n + 1],
                               accum_out=x_stat[:, 2, n:n + 1]).then_inc(s_ce, 1)

        def dve_cross_weights(dve, c):
            p = slice(2 * c, 2 * c + 2)
            dve.wait_ge(s_ce, 2 * c + 2)
            dve.reciprocal(x_stat[:, 3, p], x_stat[:, 2, p]).then_inc(s_cr, 1)
            dve.wait_ge(s_cr, c + 1)
            for h in range(2):
                w = succ[:, c % GR, h * M:(h + 1) * M]
                dve.tensor_scalar(w, w, x_stat[:, 3, 2 * c + h:2 * c + h + 1], None, ALU.mult).then_inc(s_cp, 1)

        def pe_cross_turn(pe, c):
            pe.wait_ge(s_cp, 2 * c + 2)
            if c >= 2:
                pe.wait_ge(s_ctl, c - 1)
            for b in range(4):
                mm = pe.transpose(t_ps[:, c % 2, b * P:(b + 1) * P], succ[:, c % GR, b * P:(b + 1) * P], ident[:, :])
            mm.then_inc(s_ct, 1)

        def act_cross_high(act, c):
            y, col = c // 2, c % 2
            act.wait_ge(s_ct, c + 1)
            if col == 0 and y >= AR:
                act.wait_ge(s_cv, y - AR + 1)
            act.activation(a_h[:, y % AR, :, col * P:(col + 1) * P], t_ps[:, c % 2].rearrange("p (j q) -> p j q", q=P),
                           ACT.Copy).then_inc(s_cth, 1)

        def dve_cross_low(dve, c):
            y, q = c // 2, slice((c % 2) * P, (c % 2 + 1) * P)
            dve.wait_ge(s_cth, c + 1)
            dve.tensor_tensor(a_l[:, y % AR, :, q], t_ps[:, c % 2].rearrange("p (j q) -> p j q", q=P),
                              a_h[:, y % AR, :, q].bitcast(F32), ALU.subtract).then_inc(s_ctl, 1)

        def pe_cross_values(pe, y):
            x_ = 2 * y // NT
            pe.wait_ge(s_ctl, 2 * y + 2)
            if y:
                pe.wait_ge(s_co, 2 * y)
            for h in range(2):
                for m in range(MT):
                    for i, a in enumerate((a_h, a_l)):
                        mm = pe.matmul(o_ps[:, h * 2 * P:(h + 1) * 2 * P],
                                       mv[:, m, x_, 2 * h:2 * h + 2, :].rearrange("p a d -> p (a d)"),
                                       a[:, y % AR, MT * h + m], start=(h == 0 and m == 0 and i == 0), stop=False,
                                       skip_group_check=True)
            mm.then_inc(s_cv, 1)

        def act_cross_low_rows(act, y):
            act.wait_ge(s_cv, y + 1)
            if y:
                act.wait_ge(s_co, 2 * y)
            act.activation(pv_low[0:HD, :], o_ps[HD:P, 0:2 * P], ACT.Copy).then_inc(s_cl, 1)
            act.activation(pv_low[HD:P, :], o_ps[0:HD, 2 * P:4 * P], ACT.Copy).then_inc(s_cl, 1)

        def dve_cross_heads(dve, y):
            at_ = (PAIRS - 2 + 2 * y // NT) * S + (y % (NT // 2)) * 2 * P
            dve.wait_ge(s_cl, 2 * y + 2)
            for h in range(2):
                r = slice(HD * h, HD * h + HD)
                dve.tensor_tensor(o_t[r, at_:at_ + 2 * P], o_ps[r, h * 2 * P:(h + 1) * 2 * P], pv_low[r, :], ALU.add
                                  ).then_inc(s_co, 1)

        def pe_project(pe, i, turns=()):
            t, n = i % NT, i // (2 * NT)
            last = i == 3 * NT - 1
            order = (range(EARLY), range(EARLY, OC), LAST_ORDER if last else range(OC))[i // NT]
            if i >= 2:
                pe.wait_ge(s_x2, i - 1)
            for at_, k in enumerate(order):
                if t == 0:
                    wait_split(pe, ("w", k, n))
                if n == 0 and t % 4 == 0:
                    wait_split(pe, ("o", k, t // 4))
                for j, (o, w) in enumerate(((o_h, wo_h), (o_h, wo_l), (o_l, wo_h))):
                    mm = pe.matmul(j_ps[:, i % 2], o[k][:, t * P:(t + 1) * P], w[:, k],
                                   start=(at_ == 0 and j == 0), stop=(at_ == len(order) - 1 and j == 2))
                if last and at_ == 5:
                    mm.then_inc(s_op, 1)
                if at_ in (2, 5, 8):
                    for c in turns[at_ // 3:at_ // 3 + 1]:
                        pe_turn(pe, XU0 + c, None, 0, c, MT + NT + 4)
            mm.then_inc(s_op, 1)

        PROJECTED = 3 * NT + 1
        X0 = 3 * NT

        def dve_add(dve, i):
            t, n = i % NT, i // (2 * NT)
            dve.wait_ge(s_op, i + 1 + (i == 3 * NT - 1))
            if i // NT != 1:
                dve.wait_ge(s_x2l[n][t], 16)
            else:
                dve.wait_ge(s_x2, t + 1)
            dst = part[:, t] if i < NT else x2[:, t, n * BANK:(n + 1) * BANK]
            src = dst if n else part[:, t]
            dve.tensor_tensor(dst, j_ps[:, i % 2], src, ALU.add).then_inc(s_x2, 1)

        def sp_ffn(sp, r, kind, c, j):
            extra = extra_slot(r)
            if extra:
                sp.wait_ge(s_op, PROJECTED - 1)
            elif isinstance(r, int) and r in (4, 5):
                sp.wait_ge(s_fl, r - 3)
            elif not (isinstance(r, int) and r < 2):
                sp.wait_ge(s_fl, r - 1)
            slot = j % 2
            raw = f_raw2 if extra else f_raw
            if kind == "gate":
                fb, mat, kh = j // 4, j // 2 % 2, j % 2
                src = gud[mat][:, 4 * kh:4 * kh + 4, bass.ds((c * FB + fb) * P, P)]
                dst = raw[:, slot].rearrange("p (c n) -> p c n", c=4)
            else:
                fb, n = j // 2, j % 2
                src = dnd[:, bass.ds(c * FB + fb, 1), n * BANK:(n + 1) * BANK]
                dst = f_raw[:, slot:slot + 1]
            sp.dma_start(dst, src).then_inc((s_fx if extra else s_fw)[slot], 16)

        def ffn_w(kind, par, j, high):
            if kind == "gate":
                fb, mat, kh = j // 4, j // 2 % 2, j % 2
                return (gw_h if high else gw_l)[:, fb, mat, 4 * kh:4 * kh + 4].rearrange(flat)
            return (dw_h if high else dw_l)[par][:, j // 2, (j % 2) * BANK:(j % 2 + 1) * BANK]

        def row_of(kind, c, j):
            if kind == "gate":
                return j if isinstance(c, int) and c == 0 else 12 * c - 4 + j
            return 16 + 12 * c + j - (8 if isinstance(c, int) and c == FC - 1 else 0)

        def extra_slot(r):
            return isinstance(r, int) and r in (2, 3)

        def act_ffn_w(act, kind, c, j, par=0):
            r = row_of(kind, c, j)
            rr = r - j % 2
            if extra_slot(r):
                act.wait_ge(s_fx[j % 2], 16)
            else:
                act.wait_ge(s_fw[j % 2], 16 if isinstance(r, int) and r < 2 else rr * 8)
            if kind == "gate":
                if isinstance(c, int) and c == 0:
                    act.wait_ge(s_op, PROJECTED - (j < 4))
                else:
                    act.wait_ge(s_gp, 8 * c - 4 + j // 2 + 1)
            raw = f_raw2 if extra_slot(r) else f_raw
            act.activation(ffn_w(kind, par, j, True), raw[:, j % 2], ACT.Copy).then_inc(s_fh, 1)

        def dve_ffn_w(dve, kind, c, j, par=0):
            r = row_of(kind, c, j)
            dve.wait_ge(s_fh, r + 1)
            raw = f_raw2 if extra_slot(r) else f_raw
            dve.tensor_tensor(ffn_w(kind, par, j, False), raw[:, j % 2], ffn_w(kind, par, j, True).bitcast(F32),
                              ALU.subtract).then_inc(s_fl, 1)

        def pe_gate_up(pe, c, half, fb, turns=False):
            first = isinstance(c, int) and c == 0
            q = 4 * c + 2 * half + fb
            if not (first and half == 0):
                pe.wait_ge(s_pr, q - 1)
            if first:
                pe.wait_ge(s_xl, XU0 + KC * (half + 1))
                pe.wait_ge(s_ssq, NS)
            for mat in range(2):
                for kh in range(2):
                    if half == 0:
                        pe.wait_ge(s_fl, row_of("gate", c, 4 * fb + 2 * mat + kh) + 1)
                    for k in range(4 * kh, 4 * kh + 4):
                        for i, (w, f) in enumerate(((gw_h, f_h), (gw_h, f_l), (gw_l, f_h))):
                            mm = pe.matmul(ps[:, 4 + 2 * fb + mat], w[:, fb, mat, k], f[half][:, k],
                                           start=(k == 0 and i == 0), stop=(k == KC - 1 and i == 2))
                        if turns and k % 2 and k < KC - 1:
                            pe_turn(pe, XU0 + KC + 3 * mat + k // 2, None, 0, 3 * mat + k // 2, NS)
                mm.then_inc(s_gp, 1)
            if turns:
                for c_ in range(6, KC):
                    pe_turn(pe, XU0 + KC + c_, None, 0, c_, NS)

        def act_sigmoid(act, c, half, fb):
            q = 4 * c + 2 * half + fb
            act.wait_ge(s_gp, 2 * q + 1)
            if not (isinstance(c, int) and c == 0 and half == 0):
                act.wait_ge(s_pr, q - 1)
            act.activation(sig[:, fb], ps[:, 4 + 2 * fb], ACT.Sigmoid).then_inc(s_sg, 1)

        def dve_product(dve, c, half, fb):
            q = 4 * c + 2 * half + fb
            dve.wait_ge(s_sg, q + 1)
            dve.tensor_tensor(sig[:, fb], ps[:, 4 + 2 * fb], sig[:, fb], ALU.mult).then_inc(s_t1, 1)
            dve.wait_ge(s_t1, q + 1)
            dve.wait_ge(s_gp, 2 * q + 2)
            if not (isinstance(c, int) and c == 0 and half == 0):
                dve.wait_ge(s_gl, q - 1)
            dve.tensor_tensor(prod[:, fb], ps[:, 5 + 2 * fb], sig[:, fb], ALU.mult).then_inc(s_pr, 1)

        def act_product_high(act, c, half, fb, par):
            q = 4 * c + 2 * half + fb
            act.wait_ge(s_pr, q + 1)
            if not (isinstance(c, int) and c == 0):
                act.wait_ge(s_dn, 2 * NT * (c - 1) + 1)
            act.activation(gu_h[par][:, fb, half * BANK:(half + 1) * BANK], prod[:, fb], ACT.Copy).then_inc(s_gh, 1)

        def dve_product_low(dve, c, half, fb, par):
            q = 4 * c + 2 * half + fb
            cols = slice(half * BANK, (half + 1) * BANK)
            dve.wait_ge(s_gh, q + 1)
            dve.tensor_tensor(gu_l[par][:, fb, cols], prod[:, fb], gu_h[par][:, fb, cols].bitcast(F32), ALU.subtract
                              ).then_inc(s_gl, 1)

        def pe_down(pe, c, par):
            pe.wait_ge(s_fl, row_of("down", c, 3) + 1)
            for t in range(NT):
                if t % 4 == 0:
                    pe.wait_ge(s_gl, 4 * c + 2 * (t // 4) + 2)
                for n in range(2):
                    d = 2 * t + n
                    pe.wait_ge(s_x2, X0 + 2 * NT * c + d - 3)
                    for fb in range(FB):
                        for i, (g, w) in enumerate(((gu_h, dw_h[par]), (gu_h, dw_l[par]), (gu_l, dw_h[par]))):
                            mm = pe.matmul(ps[:, (2, 3, 0, 1)[d % 4]], g[par][:, fb, t * P:(t + 1) * P],
                                           w[:, fb, n * BANK:(n + 1) * BANK],
                                           start=(fb == 0 and i == 0), stop=(fb == FB - 1 and i == 2))
                    mm.then_inc(s_dn, 1)

        def dve_down(dve, c, ahead, last_w):
            for t in range(NT):
                if ahead and 0 < t < 5:
                    dve_ffn_w(dve, "gate", c + 2, 3 + t)
                if last_w and t % 2 == 0:
                    dve_ffn_w(dve, "down", c + 1, t // 2, 1 - c % 2)
                for n in range(2):
                    d = 2 * t + n
                    dve.wait_ge(s_dn, 2 * NT * c + d + 2)
                    dve.wait_ge(s_x2, X0 - 2 * NT + 2 * NT * c + d + 1)
                    o = x2[:, t, n * BANK:(n + 1) * BANK]
                    dve.tensor_tensor(o, ps[:, (2, 3, 0, 1)[d % 4]], o, ALU.add).then_inc(s_x2, 1)

        def sp_step(sp, c, ahead=True):
            for j in range(4):
                sp_ffn(sp, row_of("down", c, j), "down", c, j)
            if ahead:
                for j in range(8):
                    sp_ffn(sp, row_of("gate", c + 2, j), "gate", c + 2, j)

        def act_ffn(act, c, par, nxt=True, ahead=True, last_w=False):
            if nxt:
                for j in range(4):
                    act_ffn_w(act, "down", c, j, par)
            if nxt:
                for half in range(2):
                    for fb in range(FB):
                        act_sigmoid(act, c + 1, half, fb)
                        act_product_high(act, c + 1, half, fb, 1 - par)
                        if half == 1 and ahead:
                            for j in range(4 * fb, 4 * fb + 4):
                                act_ffn_w(act, "gate", c + 2, j)
            if last_w:
                for j in range(4):
                    act_ffn_w(act, "down", c + 1, j, 1 - par)

        def dve_ffn(dve, c, par, nxt=True, ahead=True, last_w=False):
            if nxt:
                for j in range(4):
                    dve_ffn_w(dve, "down", c, j, par)
            if nxt:
                for half in range(2):
                    for fb in range(FB):
                        dve_product(dve, c + 1, half, fb)
                        dve_product_low(dve, c + 1, half, fb, 1 - par)
                        if half == 1 and fb == 0 and ahead:
                            for j in range(4):
                                dve_ffn_w(dve, "gate", c + 2, j)
            dve_down(dve, c, ahead, last_w)

        def pe_ffn(pe, c, par, nxt=True):
            if nxt:
                for half in range(2):
                    for fb in range(FB):
                        pe_gate_up(pe, c + 1, half, fb)
            pe_down(pe, c, par)

        TURN_AT = [(), (), (), (), (), (0, 1, 2), (3, 4, 5), (6, 7)]
        FLOOPS = (FC - 3) // 2
        block = ctx.enter_context(nc.Block())
        LOOPS = (PAIRS - 2) // 2

        @block.sync
        def _(sp):
            for t in range(MT):
                sp.dma_start(m_in[:, t], memd[:, t]).then_inc(s_m[t], 16)
            with nc.allow_non_contiguous_dma("gains, one per partition"):
                for i, g in enumerate((attn_norm, mem_norm, ffn_norm)):
                    sp.dma_start(gains[:, i], g.rearrange("l (c p) -> p (l c)", p=P)).then_inc(s_g, 16)
                for i, g in enumerate((xq_norm, xk_norm)):
                    for h in range(2):
                        sp.dma_start(g_cross[HD * h:HD * h + HD, i:i + 1], g.rearrange("l d -> d l")
                                     ).then_inc(s_g, 16)
            for t in range(4):
                sp.dma_start(x_in[:, t], xd[:, t]).then_inc(s_x[t], 16)
            for k in range(KC // 2):
                sp.dma_start(mw_raw[:, 2 * k:2 * k + 2], mwd[:, 2 * k:2 * k + 2]).then_inc(s_mw[k], 16)
            for t in range(4, NT):
                sp.dma_start(x_in[:, t], xd[:, t]).then_inc(s_x[t], 16)
            for k in range(2 * XP):
                load_half(sp, MW + k, 3 * D + (k // 2) * P, k)
            for k in range(6):
                load_w(sp, 0, k)
            with sp.Fori(0, LOOPS) as m:
                for par in range(2):
                    for k in range(6):
                        load_w(sp, 2 * m + par + 1, k)
            for k in range(6):
                load_w(sp, PAIRS - 1, k)
            sp.wait_ge(s_wl, W1)
            sp.wait_ge(s_pj, W1)
            for N in range(2 * OC):
                if N == OC:
                    wait_split(sp, ("o", EARLY - 1, 1))
                    wait_split(sp, ("o", EARLY - 1, 0))
                    for t in range(NT):
                        sp.dma_start(part[:, t], xd[:, t, 0:BANK]).then_inc(s_x2l[0][t], 16)
                    sp.wait_ge(s_o, 8 * PAIRS + 1)
                    for t in range(NT):
                        sp.dma_start(x2[:, t, BANK:D], xd[:, t, BANK:D]).then_inc(s_x2l[1][t], 16)
                if N >= 4:
                    wait_split(sp, ("w", (N - 4) % OC, (N - 4) // OC))
                k, n = N % OC, N // OC
                sp.dma_start(wo_raw[:, N % 4], wod[:, k, n * BANK:(n + 1) * BANK]).then_inc(s_wo[N % 4], 16)
            for j in range(2):
                sp_ffn(sp, j, "gate", 0, j)
            for j in range(2, 8):
                sp_ffn(sp, j, "gate", 0, j)
            for j in range(8):
                sp_ffn(sp, 8 + j, "gate", 1, j)
            with sp.Fori(0, FLOOPS) as m:
                for par in range(2):
                    sp_step(sp, 2 * m + par)
            sp_step(sp, FC - 3)
            sp_step(sp, FC - 2, ahead=False)
            sp_step(sp, FC - 1, ahead=False)
            for t in range(NT):
                sp.wait_ge(s_x2, X0 + 2 * NT * (FC - 1) + 2 * t + 2)
                sp.dma_start(outd[:, t], x2[:, t]).then_inc(s_out, 16)
            sp.wait_ge(s_out, 16 * NT)

        @block.gpsimd
        def _(pool):
            pool.memset(ident[:, :], 0.0).then_inc(s_id, 1)
            pool.memset(eps_col[:, :], EPS).then_inc(s_id, 1)
            pool.memset(fail[:, :, :], 1.0).then_inc(s_id, 1)
            pool.memset(own[:, :], 0.0).then_inc(s_id, 1)
            pool.memset(half_ones[:, :], 0.0).then_inc(s_id, 1)
            pool.wait_ge(s_id, 5)
            for h in range(2):
                pool.memset(half_ones[HD * h:HD * h + HD, h:h + 1], 1.0).then_inc(s_id, 1)
                pool.wait_ge(s_id, 6 + h)
            for square in (ident[:, :], own[:, BANK - P:BANK]):
                pool.affine_select(out=square, in_=square, compare_op=ALU.not_equal, fill=1.0, base=0,
                                   pattern=[[-1, P]], channel_multiplier=1).then_inc(s_id, 1)
            for i in SPLITS:
                if LOW[i][0] == 0:
                    split_low(pool, i)

        MADE = 9

        @block.scalar
        def _(act):
            act.wait_ge(s_id, MADE)
            for t in range(MT):
                act.wait_ge(s_m[t], 16)
                act_root(act, t, m_in[:, t], junk[:, :])
            act.wait_ge(s_g, 16 * 7)
            for g in range(4):
                act.wait_ge(s_xt, g + 1)
                for i in range(2):
                    last = act.activation(m_hh[:, 2 * g + i], turn_ps(g)[:, i * M:(i + 1) * M], ACT.Copy,
                                          scale=gains[:, 1, 2 * g + i:2 * g + i + 1])
                last.then_inc(s_xh, 1)
            for k in range(4):
                act_mem_w(act, k)
            for t in range(4):
                act.wait_ge(s_x[t], 16)
                act_root(act, MT + t, x_in[:, t], junk[:, :])
            for c in range(KC):
                act_turned(act, 4 + c, hh[:, c, 0:BANK], gains[:, 0, c:c + 1])
            for k in range(4, MW):
                act_mem_w(act, k)
            for k in range(2):
                act_w_high(act, MW + k, 0, k)
            for t in range(4, NT):
                act.wait_ge(s_x[t], 16)
                act_root(act, MT + t, x_in[:, t], junk[:, :])
            for c in range(KC):
                act_turned(act, 4 + KC + c, hh[:, c, BANK:2 * BANK], gains[:, 0, c:c + 1])
            act.wait_ge(s_pj, MW)
            for m in range(MT):
                act.activation(mk_raw[:, m], ps[:, 6 + m, 0:XW], ACT.Copy).then_inc(s_mka, 1)
                values = ps[:, 6 + m, XW:2 * XW].rearrange("p (x h d) -> p x h d", x=XP, h=2)
                act.activation(mv[:, m, :, 0:4:3, :], values, ACT.Copy).then_inc(s_mka, 1)
            act.wait_ge(s_mk, 2)
            act.activation(k_stat[:, 1], k_stat[:, 0], ACT.Sqrt, bias=eps_col[:, :], scale=1.0 / HD).then_inc(s_mka, 1)
            for k in range(2, 4):
                act_w_high(act, MW + k, 1, k)
            act_cross_q(act, 0)
            act.wait_ge(s_gq, 1)
            act_turned(act, XU0 - 1, mk_h[:, :, :].rearrange("p x m -> p (x m)"), g_qk[:, :])
            act_w(act, 0, 0)
            act_w(act, 0, 1)
            act_cross_q(act, 1)
            act.wait_ge(s_qs, 1)
            act.activation(q_stat[:, 0], o_ps[:, 0:2 * CU], ACT.Sqrt, bias=eps_col[:, :], scale=1.0 / HD
                           ).then_inc(s_qr, 1)
            act_w(act, 0, 2)
            act_cross_exp(act, 0)
            act_cross_exp(act, 1)
            for c in range(CU):
                if c in X_EVAC:
                    act_evac(act, 0, X_EVAC[c], 0)
                act_cross_high(act, c)
                if c + 2 < CU:
                    act_cross_exp(act, c + 2)
                if c % 2 == 0 and c:
                    act_cross_low_rows(act, c // 2 - 1)
                if c in X_CONV:
                    act_w(act, X_CONV[c] // 6, X_CONV[c] % 6)
            act_cross_low_rows(act, CU // 2 - 1)
            act_fail_succ(act, 0, 0, 0, first=True)
            act_fail_succ(act, 0, 0, 1, first=True)
            act_v(act, 0, 0)
            act_fail_succ(act, 0, 1, 0, first=True)
            act_fail_succ(act, 0, 1, 1, first=True)
            with act.Fori(0, LOOPS) as m:
                for par in range(2):
                    act_step(act, 2 * m + par, par)
            act_step(act, PAIRS - 2, 0)
            act_step(act, PAIRS - 1, 1, last=True)
            for i in LATER + SECOND:
                act_split(act, i)
            for t in range(NT):
                for c in TURN_AT[t]:
                    if c == 0:
                        wait_split(act, LATER[-1])
                    act_turned(act, XU0 + c, f_h[0][:, c], gains[:, 2, c:c + 1])
                if t == NT - 1:
                    for j in range(4):
                        act_ffn_w(act, "gate", 0, j)
                act.wait_ge(s_x2, 2 * NT + t + 1)
                act_root(act, MT + NT + t, x2[:, t], ps[:, 4:6].rearrange("p b n -> p (b n)"))
            for j in range(4, 8):
                act_ffn_w(act, "gate", 0, j)
            for half in range(2):
                for fb in range(FB):
                    act_sigmoid(act, 0, half, fb)
                    act_product_high(act, 0, half, fb, 0)
                    if half == 0 and fb == 0:
                        for c in range(KC):
                            act_turned(act, XU0 + KC + c, f_h[1][:, c], gains[:, 2, c:c + 1])
                    if half == 1:
                        for j in range(4 * fb, 4 * fb + 4):
                            act_ffn_w(act, "gate", 1, j)
            with act.Fori(0, FLOOPS) as m:
                for par in range(2):
                    act_ffn(act, 2 * m + par, par)
            act_ffn(act, FC - 3, 0)
            act_ffn(act, FC - 2, 1, ahead=False, last_w=True)

        @block.vector
        def _(dve):
            for t in range(MT):
                dve_scale(dve, t, m_in[:, t], m_in[:, t])
            dve.wait_ge(s_g, 16 * 7)
            dve.tensor_tensor(g_qk[:, :], g_cross[:, 0:1], g_cross[:, 1:2], ALU.mult).then_inc(s_gq, 1)
            for g in range(4):
                dve.wait_ge(s_xh, g + 1)
                for i in range(2):
                    c = 2 * g + i
                    last = dve.scalar_tensor_tensor(m_hl[:, c], turn_ps(g)[:, i * M:(i + 1) * M],
                                                    gains[:, 1, c:c + 1], m_hh[:, c].bitcast(F32),
                                                    ALU.mult, ALU.subtract)
                    if c == 0:
                        last.then_inc(s_o, 1)
                last.then_inc(s_xl, 1)
            for k in range(4):
                dve_mem_w(dve, k)
            for t in range(4):
                dve_scale(dve, MT + t, x_in[:, t], x_in[:, t])
            for c in range(KC):
                dve_turned(dve, 4 + c, hl[:, c, 0:BANK], hh[:, c, 0:BANK], gains[:, 0, c:c + 1])
            for k in range(4, MW):
                dve_mem_w(dve, k)
            for k in range(2):
                dve_w_low(dve, MW + k, k)
            for t in range(4, NT):
                dve_scale(dve, MT + t, x_in[:, t], x_in[:, t])
            for c in range(KC):
                dve_turned(dve, 4 + KC + c, hl[:, c, BANK:2 * BANK], hh[:, c, BANK:2 * BANK], gains[:, 0, c:c + 1])
            dve.wait_ge(s_mka, 2 * MT)
            for m in range(MT):
                values = ps[:, 6 + m, XW:2 * XW].rearrange("p (x h d) -> p x h d", x=XP, h=2)
                dve.tensor_tensor(mv[:, m, :, 1:3, :], values,
                                  mv[:, m, :, 0:4:3, :].bitcast(F32), ALU.subtract).then_inc(s_mv, 1)
            allk = mk_raw[:, :, :].rearrange("p m n -> p (m n)")
            allsq = mk_sq[:, :, :].rearrange("p m n -> p (m n)")
            dve.tensor_tensor(allsq, allk, allk, ALU.mult).then_inc(s_mk, 1)
            dve.wait_ge(s_mk, 1)
            dve.tensor_reduce(k_stat[:, 0], allsq.rearrange("p (g d) -> p g d", d=HD), AX.X, ALU.add).then_inc(s_mk, 1)
            dve.wait_ge(s_mka, 2 * MT + 1)
            dve.reciprocal(k_stat[:, 2], k_stat[:, 1]).then_inc(s_mk, 1)
            dve.wait_ge(s_mk, 3)
            for g in range(MT * 2 * XP):
                kk = allk[:, g * HD:(g + 1) * HD]
                dve.tensor_scalar(kk, kk, k_stat[:, 2, g:g + 1], None, ALU.mult).then_inc(s_mk, 1)
            for k in range(2, 4):
                dve_w_low(dve, MW + k, k)
            dve_cross_q(dve, 0)
            dve_turned(dve, XU0 - 1, mk_l[:, :, :].rearrange("p x m -> p (x m)"),
                       mk_h[:, :, :].rearrange("p x m -> p (x m)"), g_qk[:, :])
            dve_w(dve, 0, 0)
            dve_w(dve, 0, 1)
            dve_cross_q(dve, 1)
            dve.wait_ge(s_qr, 1)
            dve.reciprocal(q_stat[:, 1], q_stat[:, 0]).then_inc(s_qi, 1)
            dve.wait_ge(s_qi, 1)
            dve.tensor_scalar(q_stat[:, 2], q_stat[:, 1], CQ, None, ALU.mult).then_inc(s_qi, 1)
            dve.tensor_scalar(q_stat[:, 3], q_stat[:, 1], -CQ, None, ALU.mult).then_inc(s_qi, 1)
            dve.wait_ge(s_qi, 3)
            dve_w(dve, 0, 2)
            dve_cross_max(dve, 0)
            dve_cross_max(dve, 1)
            dve_cross_weights(dve, 0)
            for c in range(CU):
                if c in X_EVAC and X_EVAC[c] < 2:
                    dve_evac(dve, 0, X_EVAC[c], 0)
                if c == 9:
                    dve_double(dve, 0, 0)
                if c + 2 < CU:
                    dve_cross_max(dve, c + 2)
                if c + 1 < CU:
                    dve_cross_weights(dve, c + 1)
                dve_cross_low(dve, c)
                if c % 2 == 0 and c:
                    dve_cross_heads(dve, c // 2 - 1)
                if c in X_CONV:
                    dve_w(dve, X_CONV[c] // 6, X_CONV[c] % 6)
            dve_cross_heads(dve, CU // 2 - 1)
            dve_scan(dve, 0, 0, 0)
            dve_scan(dve, 0, 0, 1)
            dve_weights(dve, 0, 0, 0)
            dve_weights(dve, 0, 0, 1)
            dve_v(dve, 0, 0)
            with dve.Fori(0, LOOPS) as m:
                for par in range(2):
                    dve_step(dve, 2 * m + par, par)
            dve_step(dve, PAIRS - 2, 0)
            dve_step(dve, PAIRS - 1, 1, last=True)
            for i in LATER[:4]:
                split_low(dve, i)
            for i in range(NU - 1 - FILL_AT, NT):
                dve_add(dve, i)
            for i in LATER[4:]:
                split_low(dve, i)
            for t in range(NT):
                dve_add(dve, NT + t)
                if t < EARLY:
                    split_low(dve, SECOND[t])
            for i in SECOND[EARLY:]:
                split_low(dve, i)
            for t in range(NT):
                for c in TURN_AT[t]:
                    dve_turned(dve, XU0 + c, f_l[0][:, c], f_h[0][:, c], gains[:, 2, c:c + 1])
                if t == NT - 1:
                    for j in range(2):
                        dve_ffn_w(dve, "gate", 0, j)
                dve_add(dve, 2 * NT + t)
                if t < 4:
                    dve_scale(dve, MT + NT + t, x2[:, t], xn[t][:, :])
            for j in range(2, 4):
                dve_ffn_w(dve, "gate", 0, j)
            dve.wait_ge(s_xt, XU0 + KC)
            for t in range(4, NT):
                dve_scale(dve, MT + NT + t, x2[:, t], xn[t - 4][:, :])
            for j in range(4, 8):
                dve_ffn_w(dve, "gate", 0, j)
            for half in range(2):
                for fb in range(FB):
                    dve_product(dve, 0, half, fb)
                    dve_product_low(dve, 0, half, fb, 0)
                    if half == 0 and fb == 0:
                        for c in range(KC):
                            dve_turned(dve, XU0 + KC + c, f_l[1][:, c], f_h[1][:, c], gains[:, 2, c:c + 1])
                    if half == 1:
                        for j in range(4 * fb, 4 * fb + 4):
                            dve_ffn_w(dve, "gate", 1, j)
            with dve.Fori(0, FLOOPS) as m:
                for par in range(2):
                    dve_ffn(dve, 2 * m + par, par)
            dve_ffn(dve, FC - 3, 0)
            dve_ffn(dve, FC - 2, 1, ahead=False, last_w=True)
            dve_ffn(dve, FC - 1, 0, nxt=False, ahead=False)

        @block.tensor
        def _(pe):
            pe.wait_ge(s_id, MADE)
            for _ in range(WARM):
                pe.matmul(ps[:, 3], ident[:, :], fail[:, 0, 0:BANK], start=True, stop=True)
            for g in range(4):
                for i in range(2):
                    for t in range(MT):
                        pe.wait_ge(s_xn, t + 1)
                        mm = pe.transpose(turn_ps(g)[:, (MT * i + t) * P:(MT * i + t + 1) * P],
                                          m_in[:, t, (2 * g + i) * P:(2 * g + i + 1) * P], ident[:, :])
                        if g == 0 and i == 0 and t == 0:
                            mm.then_inc(s_pv, AR)
                mm.then_inc(s_xt, 1)
            pe.wait_ge(s_xl, 4)
            for k in range(4):
                pe_mem(pe, k)
            for c in range(KC):
                pe_turn(pe, 4 + c, x_in, 0, c, MT + 4)
            for k in range(4, MW):
                pe_mem(pe, k)
            pe_first_half(pe, 0)
            for c in range(KC):
                pe_turn(pe, 4 + KC + c, x_in, 4, c, MT + NT)
            pe_first_half(pe, 1)
            wait_turn_bank(pe, XU0 - 1)
            pe.wait_ge(s_mk, 3 + MT * 2 * XP)
            for x_ in range(XP):
                for m in range(MT):
                    mm = pe.transpose(turn_ps(XU0 - 1)[:, (MT * x_ + m) * P:(MT * x_ + m + 1) * P],
                                      mk_raw[:, m, x_ * P:(x_ + 1) * P], ident[:, :])
            mm.then_inc(s_xt, 1)
            for piece in range(4):
                pe_project_in(pe, MW + 2, piece, xq_ps[1])
            pe_piece(pe, 0, 0, first=True)
            pe.wait_ge(s_mv, MT)
            pe.wait_ge(s_mka, 2 * MT)
            pe.wait_ge(s_sq, 2 * XP)
            for c in range(CU):
                x_, t = c // NT, c % NT
                mm = pe.matmul(o_ps[:, 2 * c:2 * c + 2], xq_sq[:, x_, t * P:(t + 1) * P], half_ones[:, :],
                               start=True, stop=True)
            mm.then_inc(s_qs, 1)
            pe_piece(pe, 0, 1, first=True)
            pe.wait_ge(s_xl, XU0)
            pe_cross_scores(pe, 0)
            pe_piece(pe, 0, 2, first=True)
            pe_cross_scores(pe, 1)
            pe_piece(pe, 0, 3, first=True)
            pe.wait_ge(s_qr, 1)
            for c in range(CU):
                if c + 2 < CU:
                    pe_cross_scores(pe, c + 2)
                pe_cross_turn(pe, c)
                for k in range(2 * 4 + sum(X_COUNT[:c]), 2 * 4 + sum(X_COUNT[:c + 1])):
                    pe_piece(pe, 0, k // 2, first=True, only=k % 2)
                if c % 2:
                    pe_cross_values(pe, c // 2)
            pe_scores(pe, 0, 0, 0, first=True)
            pe.wait_ge(s_ctl, CU)
            for half in range(2):
                pe.wait_ge(s_eh, 4 + half + 1)
                for j in range(4):
                    col = (4 * half + j) * P
                    mm = pe.transpose(t_ps[:, half, j * P:(j + 1) * P], v_t[1][:, col:col + P], ident[:, :])
                mm.then_inc(s_t, 1)
            pe_scores(pe, 0, 1, 0, first=True)
            pe.wait_ge(s_co, CU)
            with pe.Fori(0, LOOPS) as m:
                for par in range(2):
                    pe_step(pe, 2 * m + par, par)
            pe_step(pe, PAIRS - 2, 0)
            pe_step(pe, PAIRS - 1, 1, last=True)
            for i in range(NU - FILL_AT, 2 * NT):
                pe_project(pe, i)
            pe.wait_ge(s_tl, T1)
            for t in range(NT):
                pe_project(pe, 2 * NT + t, TURN_AT[t])
            pe_gate_up(pe, 0, 0, 0)
            pe_gate_up(pe, 0, 0, 1, turns=True)
            pe_gate_up(pe, 0, 1, 0)
            pe_gate_up(pe, 0, 1, 1)
            with pe.Fori(0, FLOOPS) as m:
                for par in range(2):
                    pe_ffn(pe, 2 * m + par, par)
            pe_ffn(pe, FC - 3, 0)
            pe_ffn(pe, FC - 2, 1)
            pe_ffn(pe, FC - 1, 0, nxt=False)


INPUTS = ["x", "mem", "attn_norm", "mem_norm", "w_mem_kv", "xq_norm", "xk_norm", "w_out", "ffn_norm",
          "w_gate", "w_up", "w_down", "sb_w_in"]


def kernel(**inputs):
    import numpy as np
    import concourse.bacc as bacc
    from concourse.bass_utils import run_bass_kernel_spmd

    nc = bacc.Bacc("TRN2", target_bir_lowering=False, num_devices=1)
    arrays, args = {}, []
    for name in INPUTS:
        a = np.ascontiguousarray(inputs[name])
        arrays[f"in_{name}"] = a
        args.append(nc.dram_tensor(f"in_{name}", a.shape, mybir.dt.from_np(a.dtype), kind="ExternalInput").ap())
    args.append(nc.dram_tensor("out", inputs["x"].shape, F32, kind="ExternalOutput").ap())
    trunk(nc, *args)
    return run_bass_kernel_spmd(nc, [arrays], core_ids=[0]).results[0]["out"]
```
